# Optimizing a Trainium2 kernel written in Bass

```python
import jax, jax.numpy as jnp
from jax import lax
import numpy as np
import math

D_MODEL = 1024
BATCH = 1
SEQ = 256
DEPTH = 1

GRID_W = 64
CTX_LEN = 256
RET_HEADS = 8
RET_QK_DIM = 64
RET_V_DIM = 128
RET_QK_WIDTH = RET_HEADS * RET_QK_DIM
RET_V_WIDTH = RET_HEADS * RET_V_DIM
CHUNK = 128
ROPE_BASE = 10000.0
FOURIER_GROUPS = 4
FOURIER_GROUP_DIM = 128
FOURIER_WIDTH = FOURIER_GROUPS * FOURIER_GROUP_DIM
Q_OFF = 0
K_OFF = Q_OFF + RET_QK_WIDTH
V_OFF = K_OFF + RET_QK_WIDTH
G_OFF = V_OFF + RET_V_WIDTH
F_OFF = G_OFF + RET_V_WIDTH
IN_COLS = F_OFF + FOURIER_WIDTH
N_BRANCHES = 2
FFN_DIM = 2816
CONV_W = 3
N_MOD = 6
EPS = 1e-6


def rms_norm(x, w):
    x32 = x.astype(jnp.float32)
    y = x32 * lax.rsqrt(jnp.mean(x32 * x32, axis=-1, keepdims=True) + EPS)
    return (y * w.astype(jnp.float32)).astype(x.dtype)

def modulate(h, shift, scale):
    return h * (1 + scale) + shift

def split_heads(t, n_heads):
    b, l, w = t.shape
    return t.reshape(b, l, n_heads, w // n_heads).transpose(0, 2, 1, 3)

def rope_2d(t, row, col):
    n_freq = RET_QK_DIM // 4
    inv = ROPE_BASE ** (-jnp.arange(n_freq, dtype=jnp.float32) / n_freq)
    ang = jnp.concatenate([row[:, None] * inv, col[:, None] * inv], axis=-1)
    cos, sin = jnp.cos(ang), jnp.sin(ang)
    half = RET_QK_DIM // 2
    t1, t2 = t[..., :half], t[..., half:]
    return jnp.concatenate([t1 * cos - t2 * sin, t1 * sin + t2 * cos], axis=-1).astype(t.dtype)

def log_gamma(a):
    return -jnp.exp(a.astype(jnp.float32))

def chunk_retention(q, k, v, a, s0):
    b, h, l, dk = q.shape
    dv = v.shape[-1]
    n = l // CHUNK
    lg = log_gamma(a)
    qc = q.reshape(b, h, n, CHUNK, dk)
    kc = k.reshape(b, h, n, CHUNK, dk)
    vc = v.reshape(b, h, n, CHUNK, dv)
    pos = jnp.arange(CHUNK, dtype=jnp.float32)
    diff = pos[:, None] - pos[None, :]
    intra_decay = jnp.where(diff >= 0, jnp.exp(lg[:, None, None] * jnp.maximum(diff, 0.0)), 0.0)
    scores = jnp.einsum('bhncd,bhnsd->bhncs', qc, kc) * intra_decay[None, :, None]
    intra = jnp.einsum('bhncs,bhnse->bhnce', scores, vc)
    k_dec = kc * jnp.exp(lg[:, None] * (CHUNK - 1 - pos))[None, :, None, :, None]
    kv = jnp.einsum('bhnsd,bhnse->nbhde', k_dec, vc)
    chunk_decay = jnp.exp(lg * CHUNK)[None, :, None, None]

    def step(s, kv_n):
        return chunk_decay * s + kv_n, s

    s_final, s_prev = lax.scan(step, s0.astype(jnp.float32), kv)
    q_dec = qc * jnp.exp(lg[:, None] * (pos + 1))[None, :, None, :, None]
    inter = jnp.einsum('bhncd,nbhde->bhnce', q_dec, s_prev)
    return (intra + inter).reshape(b, h, l, dv), s_final

def retention_state(k, v, a):
    l = k.shape[2]
    lg = log_gamma(a)
    w = jnp.exp(lg[:, None] * (l - 1 - jnp.arange(l, dtype=jnp.float32)))
    return jnp.einsum('bhld,bhle,hl->bhde', k, v, w)

def bidir_retention(q, k, v, a_f, a_b, s_f0, s_b0):
    o_f, s_f = chunk_retention(q, k, v, a_f, s_f0)
    o_b, s_b = chunk_retention(jnp.flip(q, 2), jnp.flip(k, 2), jnp.flip(v, 2), a_b, s_b0)
    return o_f + jnp.flip(o_b, 2), s_f, s_b

def ret_readout(o, g, w_o):
    mu = jnp.mean(o, axis=-1, keepdims=True)
    var = jnp.mean(jnp.square(o - mu), axis=-1, keepdims=True)
    o = (o - mu) * lax.rsqrt(var + EPS)
    b, h, l, dv = o.shape
    o = o.transpose(0, 2, 1, 3).reshape(b, l, h * dv).astype(g.dtype)
    return (o * jax.nn.silu(g)) @ w_o

def fourier_mix(f, w_f):
    b, l, _ = f.shape
    fg = f.reshape(b, l, FOURIER_GROUPS, FOURIER_GROUP_DIM).astype(jnp.float32)
    z = jnp.fft.fft2(fg, axes=(1, 3), norm='ortho').real
    return z.reshape(b, l, FOURIER_WIDTH).astype(f.dtype) @ w_f

def merge_branches(h, ret_d, four_d, w_bg, b_bg, w_out):
    gates = jax.nn.sigmoid(h @ w_bg + b_bg)
    g_r, g_f = jnp.split(gates, N_BRANCHES, axis=-1)
    return (g_r * ret_d + g_f * four_d) @ w_out

def depthwise_conv3(u, w, b):
    up = jnp.pad(u, ((0, 0), (1, 1), (0, 0)))
    return up[:, :-2] * w[0] + up[:, 1:-1] * w[1] + up[:, 2:] * w[2] + b

def conv_ffn(h, w_up, conv_w, conv_b, w_down):
    u = depthwise_conv3(h @ w_up, conv_w, conv_b)
    a, val = jnp.split(u, 2, axis=-1)
    return (jax.nn.gelu(a) * val) @ w_down

def split_proj(p):
    return (p[..., Q_OFF:K_OFF], p[..., K_OFF:V_OFF], p[..., V_OFF:G_OFF],
            p[..., G_OFF:F_OFF], p[..., F_OFF:IN_COLS])

def first_inputs(seed: int = 0) -> dict:
    key = jax.random.key(seed)
    ks = jax.random.split(key, 24)

    def nrm(k, shape, scale):
        return jax.random.normal(k, shape, jnp.float32) * scale

    d = D_MODEL
    base_decay = jnp.log(-jnp.log1p(-(2.0 ** (-5.0 - jnp.arange(RET_HEADS, dtype=jnp.float32)))))
    return {
        "x": nrm(ks[0], (BATCH, SEQ, d), 1.0),
        "c": nrm(ks[1], (BATCH, d), 1.0),
        "ctx": nrm(ks[2], (BATCH, CTX_LEN, d), 1.0),
        "c_ctx": nrm(ks[3], (d,), 1.0),
        "w_mod": nrm(ks[4], (DEPTH, d, N_MOD * d), 0.5 * d ** -0.5),
        "b_mod": nrm(ks[5], (DEPTH, N_MOD * d), 0.01),
        "norm1_w": 1.0 + nrm(ks[6], (DEPTH, d), 0.05),
        "w_in": nrm(ks[7], (DEPTH, d, IN_COLS), d ** -0.5),
        "ret_decay_f": base_decay[None] + nrm(ks[8], (DEPTH, RET_HEADS), 0.1),
        "ret_decay_b": base_decay[None] + nrm(ks[9], (DEPTH, RET_HEADS), 0.1),
        "w_ret_out": nrm(ks[10], (DEPTH, RET_V_WIDTH, d), RET_V_WIDTH ** -0.5),
        "w_four_out": nrm(ks[11], (DEPTH, FOURIER_WIDTH, d), FOURIER_WIDTH ** -0.5),
        "w_branch_gate": nrm(ks[12], (DEPTH, d, N_BRANCHES * d), d ** -0.5),
        "b_branch_gate": nrm(ks[13], (DEPTH, N_BRANCHES * d), 0.01),
        "w_out": nrm(ks[14], (DEPTH, d, d), d ** -0.5),
        "norm2_w": 1.0 + nrm(ks[15], (DEPTH, d), 0.05),
        "w_up": nrm(ks[16], (DEPTH, d, 2 * FFN_DIM), d ** -0.5),
        "conv_w": nrm(ks[17], (DEPTH, CONV_W, 2 * FFN_DIM), CONV_W ** -0.5),
        "conv_b": nrm(ks[18], (DEPTH, 2 * FFN_DIM), 0.01),
        "w_down": nrm(ks[19], (DEPTH, FFN_DIM, d), FFN_DIM ** -0.5),
        "final_norm_w": 1.0 + nrm(ks[20], (d,), 0.05),
    }

def first_block(x, c, ctx, c_ctx, w_mod, b_mod, norm1_w, w_in, ret_decay_f, ret_decay_b,
              w_ret_out, w_four_out, w_branch_gate, b_branch_gate, w_out, norm2_w,
              w_up, conv_w, conv_b, w_down, final_norm_w):
    b, l, _ = x.shape
    rows = l // GRID_W
    row = jnp.repeat(jnp.arange(rows, dtype=jnp.float32), GRID_W)
    col = jnp.tile(jnp.arange(GRID_W, dtype=jnp.float32), rows)
    q_scale = RET_QK_DIM ** -0.5
    silu_c = jax.nn.silu(c)
    silu_cc = jax.nn.silu(c_ctx)
    xc = ctx
    for layer in range(DEPTH):
        last = layer == DEPTH - 1
        wi = w_in[layer]
        a_f, a_b = ret_decay_f[layer], ret_decay_b[layer]
        mod = silu_c @ w_mod[layer] + b_mod[layer]
        sh1, sc1, g1, sh2, sc2, g2 = [m[:, None, :] for m in jnp.split(mod, N_MOD, axis=-1)]
        mc = jnp.split(silu_cc @ w_mod[layer] + b_mod[layer], N_MOD)

        h = modulate(rms_norm(x, norm1_w[layer]), sh1, sc1)
        hc = modulate(rms_norm(xc, norm1_w[layer]), mc[0], mc[1])

        if last:
            kc = split_heads(hc @ wi[:, K_OFF:V_OFF], RET_HEADS)
            vc = split_heads(hc @ wi[:, V_OFF:G_OFF], RET_HEADS)
            s_f = retention_state(kc, vc, a_f)
            s_b = retention_state(jnp.flip(kc, 2), jnp.flip(vc, 2), a_b)
        else:
            qc, kc, vc, gc, fc = split_proj(hc @ wi)
            qc = split_heads(qc, RET_HEADS) * q_scale
            kc = split_heads(kc, RET_HEADS)
            vc = split_heads(vc, RET_HEADS)
            zeros = jnp.zeros((b, RET_HEADS, RET_QK_DIM, RET_V_DIM), jnp.float32)
            oc, s_f, s_b = bidir_retention(qc, kc, vc, a_f, a_b, zeros, zeros)
            yc = merge_branches(hc, ret_readout(oc, gc, w_ret_out[layer]),
                                fourier_mix(fc, w_four_out[layer]),
                                w_branch_gate[layer], b_branch_gate[layer], w_out[layer])
            xc = xc + mc[2] * yc
            hc2 = modulate(rms_norm(xc, norm2_w[layer]), mc[3], mc[4])
            xc = xc + mc[5] * conv_ffn(hc2, w_up[layer], conv_w[layer], conv_b[layer], w_down[layer])

        q, k, v, g, f = split_proj(h @ wi)
        q = rope_2d(split_heads(q, RET_HEADS), row, col) * q_scale
        k = rope_2d(split_heads(k, RET_HEADS), row, col)
        v = split_heads(v, RET_HEADS)
        o, _, _ = bidir_retention(q, k, v, a_f, a_b, s_f, s_b)
        y = merge_branches(h, ret_readout(o, g, w_ret_out[layer]),
                           fourier_mix(f, w_four_out[layer]),
                           w_branch_gate[layer], b_branch_gate[layer], w_out[layer])
        x = x + g1 * y
        h2 = modulate(rms_norm(x, norm2_w[layer]), sh2, sc2)
        x = x + g2 * conv_ffn(h2, w_up[layer], conv_w[layer], conv_b[layer], w_down[layer])
    return rms_norm(x, final_norm_w)


CHUNK_2 = 64
RMS_EPS = 1e-6
RW_HEADS = 8
RW_HEAD_DIM = 64
RW_WIDTH = RW_HEADS * RW_HEAD_DIM
RW_DECAY_LORA = 64
RW_AAA_LORA = 64
RW_GATE_LORA = 128
RW_GN_EPS = 64e-5
ML_HEADS = 4
ML_HEAD_DIM = 128
ML_WIDTH = ML_HEADS * ML_HEAD_DIM
ML_CONV = 4
ML_NORM_EPS = 1e-5
N_BRANCH = 2
PEER_HEADS = 8
PEER_KEYS = 128
PEER_EXPERTS = PEER_KEYS * PEER_KEYS
PEER_QDIM = 256
PEER_HALF = PEER_QDIM // 2
PEER_TOPK = 16
PEER_TOKEN_BLOCK = 128
RW_COLS = 3 * RW_WIDTH + RW_DECAY_LORA + RW_AAA_LORA + RW_GATE_LORA
ML_COLS = 4 * ML_WIDTH + 2 * ML_HEADS
GATE_COLS = N_BRANCH * D_MODEL
IN_COLS_2 = RW_COLS + ML_COLS + GATE_COLS


F32 = jnp.float32

def _rmsnorm(x, g):
    xf = x.astype(F32)
    y = xf * lax.rsqrt(jnp.mean(xf * xf, axis=-1, keepdims=True) + RMS_EPS)
    return (y * g.astype(F32)).astype(x.dtype)

def _causal_conv(x, w, b):
    c = x.shape[-1]
    y = lax.conv_general_dilated(x, w[:, None, :], window_strides=(1,), padding=[(w.shape[0] - 1, 0)],
                                 dimension_numbers=('NWC', 'WIO', 'NWC'), feature_group_count=c)
    return y + b

def _rwkv7(z, mu, w0, w_up, a0, a_up, g_up, k_k, k_a, r_k, gn_w, gn_b):
    bsz, t_len, _ = z.shape
    z = z.astype(F32)
    z_prev = jnp.pad(z, ((0, 0), (1, 0), (0, 0)))[:, :-1]
    zs = z + (z_prev - z) * mu.astype(F32)
    o1 = RW_WIDTH; o2 = 2 * RW_WIDTH; o3 = 3 * RW_WIDTH
    o4 = o3 + RW_DECAY_LORA; o5 = o4 + RW_AAA_LORA
    r, k, v = zs[..., :o1], zs[..., o1:o2], zs[..., o2:o3]
    zw, za, zg = zs[..., o3:o4], zs[..., o4:o5], zs[..., o5:]
    w_log = -jax.nn.softplus(-(w0.astype(F32) + jnp.tanh(zw) @ w_up.astype(F32))) - 0.5
    decay = jnp.exp(-jnp.exp(w_log))
    a = jax.nn.sigmoid(a0.astype(F32) + za @ a_up.astype(F32))
    g = jax.nn.sigmoid(zg) @ g_up.astype(F32)
    hs = lambda t: t.reshape(bsz, t_len, RW_HEADS, RW_HEAD_DIM)
    r, k, v, decay, a = hs(r), hs(k), hs(v), hs(decay), hs(a)
    kk = k * k_k.astype(F32).reshape(RW_HEADS, RW_HEAD_DIM)
    kk = kk / jnp.maximum(jnp.sqrt(jnp.sum(kk * kk, axis=-1, keepdims=True)), 1e-12)
    k = k * (1.0 + (a - 1.0) * k_a.astype(F32).reshape(RW_HEADS, RW_HEAD_DIM))

    def step(S, inp):
        r_t, w_t, k_t, v_t, kk_t, b_t = inp
        sa = jnp.einsum('bhvk,bhk->bhv', S, -kk_t)
        S = S * w_t[:, :, None, :] + sa[..., None] * b_t[:, :, None, :] + v_t[..., None] * k_t[:, :, None, :]
        return S, jnp.einsum('bhvk,bhk->bhv', S, r_t)

    tm = lambda t: jnp.moveaxis(t, 1, 0)
    s0 = jnp.zeros((bsz, RW_HEADS, RW_HEAD_DIM, RW_HEAD_DIM), F32)
    _, y = lax.scan(step, s0, (tm(r), tm(decay), tm(k), tm(v), tm(kk), tm(kk * a)))
    y = jnp.moveaxis(y, 0, 1)
    mean = jnp.mean(y, axis=-1, keepdims=True)
    var = jnp.mean(jnp.square(y - mean), axis=-1, keepdims=True)
    y = (y - mean) * lax.rsqrt(var + RW_GN_EPS) * gn_w.astype(F32).reshape(RW_HEADS, RW_HEAD_DIM) \
        + gn_b.astype(F32).reshape(RW_HEADS, RW_HEAD_DIM)
    y = y + jnp.sum(r * k * r_k.astype(F32), axis=-1, keepdims=True) * v
    return y.reshape(bsz, t_len, RW_WIDTH) * g

def _mlstm(z, cq_w, cq_b, ck_w, ck_b, b_i, b_f, norm_w):
    bsz, t_len, _ = z.shape
    z = z.astype(F32)
    w1 = ML_WIDTH; w2 = 2 * ML_WIDTH; w3 = 3 * ML_WIDTH; w4 = 4 * ML_WIDTH
    q_pre, k_pre, v, o_pre = z[..., :w1], z[..., w1:w2], z[..., w2:w3], z[..., w3:w4]
    i_pre, f_pre = z[..., w4:w4 + ML_HEADS], z[..., w4 + ML_HEADS:]
    q = jax.nn.silu(_causal_conv(q_pre, cq_w.astype(F32), cq_b.astype(F32)))
    k = jax.nn.silu(_causal_conv(k_pre, ck_w.astype(F32), ck_b.astype(F32)))
    n_chunks = t_len // CHUNK_2
    chunked = lambda t: t.reshape(bsz, n_chunks, CHUNK_2, ML_HEADS, ML_HEAD_DIM).transpose(0, 3, 1, 2, 4)
    gate_c = lambda t: t.reshape(bsz, n_chunks, CHUNK_2, ML_HEADS).transpose(0, 3, 1, 2)
    q = chunked(q)
    k = chunked(k) * (ML_HEAD_DIM ** -0.5)
    v = chunked(v)
    ig = gate_c(i_pre + b_i.astype(F32))
    lf = jax.nn.log_sigmoid(gate_c(f_pre + b_f.astype(F32)))
    bcum = jnp.cumsum(lf, axis=-1)
    causal = jnp.tril(jnp.ones((CHUNK_2, CHUNK_2), dtype=bool))
    d_log = jnp.where(causal, bcum[..., :, None] - bcum[..., None, :] + ig[..., None, :], -jnp.inf)
    g_end = bcum[..., -1]
    a_s = g_end[..., None] - bcum + ig
    m_loc = jnp.max(a_s, axis=-1)
    wts = jnp.exp(a_s - m_loc[..., None])
    c_loc = jnp.einsum('bhcl,bhclv,bhclk->bhcvk', wts, v, k)
    n_loc = jnp.einsum('bhcl,bhclk->bhck', wts, k)

    def step(carry, inp):
        c_st, n_st, m_st = carry
        c_l, n_l, m_l, g_c = inp
        m_new = jnp.maximum(g_c + m_st, m_l)
        s_old = jnp.exp(g_c + m_st - m_new)
        s_new = jnp.exp(m_l - m_new)
        c_next = s_old[..., None, None] * c_st + s_new[..., None, None] * c_l
        n_next = s_old[..., None] * n_st + s_new[..., None] * n_l
        return (c_next, n_next, m_new), (c_st, n_st, m_st)

    init = (jnp.zeros((bsz, ML_HEADS, ML_HEAD_DIM, ML_HEAD_DIM), F32),
            jnp.zeros((bsz, ML_HEADS, ML_HEAD_DIM), F32),
            jnp.zeros((bsz, ML_HEADS), F32))
    mv = lambda t: jnp.moveaxis(t, 2, 0)
    _, (c_in, n_in, m_in) = lax.scan(step, init, (mv(c_loc), mv(n_loc), mv(m_loc), mv(g_end)))
    c_in = jnp.moveaxis(c_in, 0, 2)
    n_in = jnp.moveaxis(n_in, 0, 2)
    m_in = jnp.moveaxis(m_in, 0, 2)
    inter_log = bcum + m_in[..., None]
    m_t = jnp.maximum(jnp.max(d_log, axis=-1), inter_log)
    scores = jnp.einsum('bhcld,bhcsd->bhcls', q, k) * jnp.exp(d_log - m_t[..., None])
    inter_w = jnp.exp(inter_log - m_t)
    num = jnp.einsum('bhcls,bhcsd->bhcld', scores, v) + inter_w[..., None] * jnp.einsum('bhcvk,bhclk->bhclv', c_in, q)
    den = jnp.sum(scores, axis=-1) + inter_w * jnp.einsum('bhck,bhclk->bhcl', n_in, q)
    h = num / jnp.maximum(jnp.abs(den), jnp.exp(-m_t))[..., None]
    h = h.transpose(0, 2, 3, 1, 4).reshape(bsz, t_len, ML_HEADS, ML_HEAD_DIM)
    mean = jnp.mean(h, axis=-1, keepdims=True)
    var = jnp.mean(jnp.square(h - mean), axis=-1, keepdims=True)
    h = (h - mean) * lax.rsqrt(var + ML_NORM_EPS)
    h = h.reshape(bsz, t_len, ML_WIDTH) * norm_w.astype(F32)
    return h * jax.nn.sigmoid(o_pre)

def _peer(h, w_q, sub_keys, u_emb, v_emb):
    bsz, t_len, d = h.shape
    tok = h.reshape(-1, d)
    n_tok = tok.shape[0]
    q = (tok @ w_q).astype(F32).reshape(n_tok, PEER_HEADS, 2, PEER_HALF)
    s = jnp.einsum('nhpc,hpkc->nhpk', q, sub_keys.astype(F32))
    s_top, i_top = lax.top_k(s, PEER_TOPK)
    cand = (s_top[:, :, 0, :, None] + s_top[:, :, 1, None, :]).reshape(n_tok, PEER_HEADS, PEER_TOPK * PEER_TOPK)
    cand_idx = (i_top[:, :, 0, :, None] * PEER_KEYS + i_top[:, :, 1, None, :]).reshape(n_tok, PEER_HEADS, PEER_TOPK * PEER_TOPK)
    best, pos = lax.top_k(cand, PEER_TOPK)
    expert = jnp.take_along_axis(cand_idx, pos, axis=-1)
    gate = jax.nn.softmax(best, axis=-1)
    n_blk = n_tok // PEER_TOKEN_BLOCK
    sel = PEER_HEADS * PEER_TOPK

    def retrieve(args):
        tb, eb, gb = args
        act = jax.nn.gelu(jnp.einsum('tkd,td->tk', u_emb[eb], tb), approximate=False) * gb
        return jnp.einsum('tk,tkd->td', act, v_emb[eb])

    out = lax.map(retrieve, (tok.reshape(n_blk, PEER_TOKEN_BLOCK, d),
                             expert.reshape(n_blk, PEER_TOKEN_BLOCK, sel),
                             gate.astype(tok.dtype).reshape(n_blk, PEER_TOKEN_BLOCK, sel)))
    return out.reshape(bsz, t_len, d)

def second_inputs(seed: int = 0) -> dict:
    key = jax.random.key(seed)
    ks = jax.random.split(key, 40)
    nrm = lambda k, shape, scale: jax.random.normal(k, shape, F32) * scale
    L = DEPTH
    return {
        "x": nrm(ks[0], (BATCH, SEQ, D_MODEL), 1.0),
        "norm1_g": 1.0 + nrm(ks[1], (L, D_MODEL), 0.02),
        "w_in": nrm(ks[2], (L, D_MODEL, IN_COLS_2), D_MODEL ** -0.5),
        "rw_mu": jax.random.uniform(ks[3], (L, RW_COLS), F32, 0.0, 1.0),
        "rw_w0": jnp.broadcast_to(jnp.linspace(-6.0, -1.0, RW_WIDTH, dtype=F32), (L, RW_WIDTH)) + nrm(ks[4], (L, RW_WIDTH), 0.1),
        "rw_w_up": nrm(ks[5], (L, RW_DECAY_LORA, RW_WIDTH), 0.1),
        "rw_a0": nrm(ks[6], (L, RW_WIDTH), 0.1),
        "rw_a_up": nrm(ks[7], (L, RW_AAA_LORA, RW_WIDTH), 0.1),
        "rw_g_up": nrm(ks[8], (L, RW_GATE_LORA, RW_WIDTH), RW_GATE_LORA ** -0.5),
        "rw_k_k": 0.85 + nrm(ks[9], (L, RW_WIDTH), 0.02),
        "rw_k_a": 1.0 + nrm(ks[10], (L, RW_WIDTH), 0.02),
        "rw_r_k": nrm(ks[11], (L, RW_HEADS, RW_HEAD_DIM), 0.1),
        "rw_gn_w": 1.0 + nrm(ks[12], (L, RW_WIDTH), 0.02),
        "rw_gn_b": nrm(ks[13], (L, RW_WIDTH), 0.02),
        "ml_conv_q_w": nrm(ks[14], (L, ML_CONV, ML_WIDTH), 0.5),
        "ml_conv_q_b": nrm(ks[15], (L, ML_WIDTH), 0.02),
        "ml_conv_k_w": nrm(ks[16], (L, ML_CONV, ML_WIDTH), 0.5),
        "ml_conv_k_b": nrm(ks[17], (L, ML_WIDTH), 0.02),
        "ml_b_i": nrm(ks[18], (L, ML_HEADS), 0.1),
        "ml_b_f": jnp.broadcast_to(jnp.linspace(3.0, 6.0, ML_HEADS, dtype=F32), (L, ML_HEADS)) + nrm(ks[19], (L, ML_HEADS), 0.1),
        "ml_norm_w": 1.0 + nrm(ks[20], (L, ML_WIDTH), 0.02),
        "gate_b": nrm(ks[21], (L, GATE_COLS), 0.02),
        "p_rw": nrm(ks[22], (L, RW_WIDTH, D_MODEL), RW_WIDTH ** -0.5),
        "p_ml": nrm(ks[23], (L, ML_WIDTH, D_MODEL), ML_WIDTH ** -0.5),
        "w_out": nrm(ks[24], (L, D_MODEL, D_MODEL), D_MODEL ** -0.5),
        "norm2_g": 1.0 + nrm(ks[25], (L, D_MODEL), 0.02),
        "peer_w_q": nrm(ks[26], (L, D_MODEL, PEER_HEADS * PEER_QDIM), D_MODEL ** -0.5),
        "peer_sub_keys": nrm(ks[27], (L, PEER_HEADS, 2, PEER_KEYS, PEER_HALF), PEER_HALF ** -0.5),
        "peer_u": nrm(ks[28], (L, PEER_EXPERTS, D_MODEL), D_MODEL ** -0.5),
        "peer_v": nrm(ks[29], (L, PEER_EXPERTS, D_MODEL), 0.25),
        "final_g": 1.0 + nrm(ks[30], (D_MODEL,), 0.02),
    }

def second_block(x, norm1_g, w_in, rw_mu, rw_w0, rw_w_up, rw_a0, rw_a_up, rw_g_up, rw_k_k, rw_k_a, rw_r_k,
              rw_gn_w, rw_gn_b, ml_conv_q_w, ml_conv_q_b, ml_conv_k_w, ml_conv_k_b, ml_b_i, ml_b_f, ml_norm_w,
              gate_b, p_rw, p_ml, w_out, norm2_g, peer_w_q, peer_sub_keys, peer_u, peer_v, final_g):
    bsz, t_len, d = x.shape
    for l in range(DEPTH):
        h = _rmsnorm(x, norm1_g[l])
        z = h @ w_in[l]
        z_rw = z[..., :RW_COLS]
        z_ml = z[..., RW_COLS:RW_COLS + ML_COLS]
        z_gate = z[..., RW_COLS + ML_COLS:]
        y_rw = _rwkv7(z_rw, rw_mu[l], rw_w0[l], rw_w_up[l], rw_a0[l], rw_a_up[l], rw_g_up[l],
                      rw_k_k[l], rw_k_a[l], rw_r_k[l], rw_gn_w[l], rw_gn_b[l]).astype(x.dtype)
        y_ml = _mlstm(z_ml, ml_conv_q_w[l], ml_conv_q_b[l], ml_conv_k_w[l], ml_conv_k_b[l],
                      ml_b_i[l], ml_b_f[l], ml_norm_w[l]).astype(x.dtype)
        gate = jax.nn.sigmoid((z_gate + gate_b[l]).astype(F32)).astype(x.dtype).reshape(bsz, t_len, N_BRANCH, d)
        merged = gate[:, :, 0, :] * (y_rw @ p_rw[l]) + gate[:, :, 1, :] * (y_ml @ p_ml[l])
        x = x + merged @ w_out[l]
        x = x + _peer(_rmsnorm(x, norm2_g[l]), peer_w_q[l], peer_sub_keys[l], peer_u[l], peer_v[l])
    return _rmsnorm(x, final_g)


def setup_inputs(seed=0):
    out = dict(first_inputs(seed))
    for name, value in second_inputs(seed + 1).items():
        if name != "x":
            out[name + "_2"] = value
    return out


def reference(
    x, c, ctx, c_ctx, w_mod, b_mod, norm1_w, w_in, ret_decay_f, ret_decay_b, w_ret_out,
    w_four_out, w_branch_gate, b_branch_gate, w_out, norm2_w, w_up, conv_w, conv_b, w_down,
    final_norm_w, norm1_g_2, w_in_2, rw_mu_2, rw_w0_2, rw_w_up_2, rw_a0_2, rw_a_up_2, rw_g_up_2,
    rw_k_k_2, rw_k_a_2, rw_r_k_2, rw_gn_w_2, rw_gn_b_2, ml_conv_q_w_2, ml_conv_q_b_2,
    ml_conv_k_w_2, ml_conv_k_b_2, ml_b_i_2, ml_b_f_2, ml_norm_w_2, gate_b_2, p_rw_2, p_ml_2,
    w_out_2, norm2_g_2, peer_w_q_2, peer_sub_keys_2, peer_u_2, peer_v_2, final_g_2,
):
    x = first_block(
        x, c, ctx, c_ctx, w_mod, b_mod, norm1_w, w_in, ret_decay_f, ret_decay_b, w_ret_out,
        w_four_out, w_branch_gate, b_branch_gate, w_out, norm2_w, w_up, conv_w, conv_b, w_down,
        final_norm_w,
    )
    return second_block(
        x, norm1_g_2, w_in_2, rw_mu_2, rw_w0_2, rw_w_up_2, rw_a0_2, rw_a_up_2, rw_g_up_2,
        rw_k_k_2, rw_k_a_2, rw_r_k_2, rw_gn_w_2, rw_gn_b_2, ml_conv_q_w_2, ml_conv_q_b_2,
        ml_conv_k_w_2, ml_conv_k_b_2, ml_b_i_2, ml_b_f_2, ml_norm_w_2, gate_b_2, p_rw_2, p_ml_2,
        w_out_2, norm2_g_2, peer_w_q_2, peer_sub_keys_2, peer_u_2, peer_v_2, final_g_2,
    )


_drawn_inputs = setup_inputs


def setup_inputs(seed=0):
    import zlib

    import numpy as np

    out = dict(_drawn_inputs(seed))
    spreads = {}
    factors = {'b_mod': 2.731,
     'b_branch_gate': 36.556,
     'conv_b': 6.423,
     'norm1_g_2': 2.767,
     'rw_a0_2': 3.164,
     'rw_k_k_2': 64.0,
     'rw_k_a_2': 4.749,
     'rw_gn_w_2': 41.584,
     'rw_gn_b_2': 41.92,
     'ml_conv_q_b_2': 59.304,
     'ml_conv_k_b_2': 63.312,
     'ml_b_i_2': 64.0,
     'ml_norm_w_2': 39.84,
     'gate_b_2': 7.488,
     'norm2_g_2': 25.536,
     'final_g_2': 7.718}
    for name, (base, spread) in spreads.items():
        noise = np.random.default_rng([zlib.crc32(name.encode()), seed]).standard_normal(out[name].shape)
        drawn = base * np.exp(spread * noise) if base else spread * noise
        out[name] = __import__('jax').numpy.asarray(drawn.astype(out[name].dtype))
    for name, factor in factors.items():
        out[name] = (out[name] * factor).astype(out[name].dtype)
    return out
```

```python
from contextlib import ExitStack

import numpy as np
import concourse.bass as bass
from concourse import mybir

P = 128
D = 1024
KD = D // P
L = 256
RING = 3
LOOP = 6
F32 = mybir.dt.float32
F32R = mybir.dt.float32r
U32 = mybir.dt.uint32
ALU = mybir.AluOpType
ACT = mybir.ActivationFunctionType
AX = mybir.AxisListType.X
EXP_HALF = float(np.exp(-0.5))

PAGES = [("mod", 24), ("q", 2), ("k", 2), ("v", 4), ("g", 4), ("f", 2), ("bg", 8), ("ro", 4), ("fo", 2),
         ("wo", 4), ("up", 22), ("dn", 11), ("lora", 1), ("rkv", 6), ("mqk", 4), ("mv", 2), ("mo", 2),
         ("gt", 8), ("pr", 2), ("pm", 2), ("w2", 4), ("wq", 8), ("peer", 128)]
PAGE = {}
NPAGES = 0
for _name, _n in PAGES:
    PAGE[_name] = NPAGES
    NPAGES += _n

SPLIT0 = PAGE["q"]

TURNS = [("q", 2), ("k", 4), ("v", 8), ("g", 4), ("f", 2), ("bg", 8), ("ro", 4), ("fo", 4), ("wo", 4), ("up", 22),
         ("dn", 4), ("lora", 1), ("rkv", 6), ("mqk", 4), ("mv", 2), ("mo", 2), ("if", 1), ("gt", 8), ("pr", 4),
         ("pm", 4), ("w2", 4), ("wq", 8), ("peer", 128)]
TURN = {}
_t = 0
for _name, _n in TURNS:
    TURN[_name] = _t
    _t += _n

COLS = [("b_mod", 48), ("norm1_w", 8), ("b_bg", 16), ("norm2_w", 8), ("conv", 176), ("final_norm_w", 8),
        ("norm1_g_2", 8), ("mu", 14), ("w0", 4), ("a0", 4), ("k_k", 4), ("k_a", 4), ("r_k", 4), ("gn_w", 4),
        ("gn_b", 4), ("cqk", 40), ("ml_norm", 4), ("gate_b", 16), ("norm2_g", 8), ("dec_pair", 8), ("dec_row", 16),
        ("if_b", 2), ("eps6", 1), ("eps_gn", 1), ("eps_ml", 1)]
COL = {}
NCOLS = 0
for _name, _n in COLS:
    COL[_name] = (NCOLS, _n)
    NCOLS += _n

CONST1 = [("cosq", 256), ("sinq", 256), ("cosk", 256), ("sink", 256), ("dist_f", 512), ("dist_b", 512),
          ("mask12", 512), ("dft_d", 256), ("dft_l", 1024), ("perm", 128), ("pos_ctx", 32), ("pos_q", 512)]
CONST2 = [("mask4", 512), ("m1", 128), ("m1t", 128), ("levels", 640), ("scan", 256), ("causal", 512), ("sel", 512),
          ("wa_up", 512), ("g_up", 512), ("w_if", 64)]


def widths(table):
    at, out = 0, {}
    for name, n in table:
        out[name] = (at, n)
        at += n
    return out, at


C1, N1 = widths(CONST1)
C2, N2 = widths(CONST2)
PCONST = [("ident", 128), ("ones", 128), ("bones", 128), ("iota", 128)]
CP, NP_ = widths(PCONST)

SEMS = """acc_free0 acc_free1 x_in mod_used lo_ready fin_out out_dma const1_in decay_exp decay_m x_new mqk_pad const2_in
 gram_sb p1_mm mt_ready piece_used acc_ready hn_mm hn_sq hn_sqmm xs_sq xs_mm pconst_in sq1 stat1 c_silu h_ready
 perm_mm kw_ready state_mm probs scores o_sb out_mm qk_ready state_sb qdec fourier1 four_sb fourier2 z_sb
 ret_ready mg_ready h_new ffn_ready rows_done uc_mm bc_mm mqk_silu uc_sb m_probs ms_mm em_row m_h nd_mm ym_ready
 lora_tanh lora_mm kk_sq lora_act kk_mm bon_in bon_mm alpha_ready tok_sb tok_mm gram_mm x_init l_mm x_sb p1_sb
 x_mm xa_mm lv_sb u0_mm xa_sb s_sb sa_mm sa_sb ds_mm u0_sb y_mm y_sb y_ready xs_root x_in_psum subk_in key_sb
 key_mm selt_ready selt_mm oh_ready g_sb g_mm selt_sb a_ready experts_done hi_ready hn_cs hn_root c_in cols_in
 lg_ready root1 hraw h_hi wctx_arg wctx w_q part_hi decay_arg conv_mid conv_u gelu_done mqk_conv lf_abs lf_exp
 lf_ln mqk_taps m_arg m_exp zs_ready kk_root scan_done w_exp g_arg g_exp fg_in fin_sq fin_root dch part_in
 up_chain xfin kk_in a_chain""".split()


def build(nc, t, out):
    with ExitStack() as ctx:
        S = {n: ctx.enter_context(nc.semaphore(n)) for n in dict.fromkeys(SEMS)}
        loaded = [ctx.enter_context(nc.semaphore(f"page_loaded{i}")) for i in range(RING)]
        acc_free = [S["acc_free0"], S["acc_free1"]]

        B0 = 16512

        def place(name, off, shape, dt=F32):
            return nc.alloc_sbuf_tensor_at(name, [P, *shape], dt, offset=B0 + 4 * off)

        arena = place("arena", 0, [32768])
        xres = place("xres", 32768, [KD, L])
        late = place("late", 32768, [2048])
        late_r = place("late_r", 32768, [2048], F32R)
        h_r = place("h_r", 34816, [2, KD, L], F32R)
        hx = place("hx", 34816, [4096])
        ring = place("ring", 38912, [RING, 2, 8, P])
        piece = place("piece", 45056, [2, 3, 8, P], F32R)
        small = place("small", 51200, [512])
        cols = place("cols", 51712, [NCOLS])
        pc = place("pconst_sb", 52128, [NP_])
        ps = ctx.enter_context(nc.psum_tensor("ps", [P, 8, 512], F32))

        def at(off, n, base=arena, **kw):
            v = base[:, off:off + n]
            return v.rearrange(kw.pop("r"), **kw) if kw else v

        def col(name, i=0, n=1):
            return cols[:, COL[name][0] + i:COL[name][0] + i + n]

        ident = pc[:, 0:128]
        ones = pc[:, 128:256]
        bones = pc[:, 256:384]
        iota = pc[:, 384:512]

        def c1(name, r=None, **kw):
            v = at(4096 + C1[name][0], C1[name][1])
            return v.rearrange(r, **kw) if r else v

        def c2(name, r=None, **kw):
            v = at(28672 + C2[name][0], C2[name][1])
            return v.rearrange(r, **kw) if r else v

        def w3(off, a, b=L):
            return arena[:, off:off + a * b].rearrange("p (a b) -> p a b", a=a)

        def pair(name, hi, lo, a):
            return place(name + "_hi", hi, [a, L], F32R), place(name + "_lo", lo, [a, L], F32R)

        h = h_r[:, 0], h_r[:, 1]
        h_tmp = w3(12800, 8)
        hctx_r = pair("hctx", 2048, 25088, 8)
        o_r = pair("o", 29184, 18944, 8)
        z_r = pair("z", 17920, 20992, 4)
        mg_r = pair("mg", 22016, 25088, 8)
        ffn_r = pair("ffn", 0, 10752, 22)
        y_r = pair("y", 10752, 12800, 4)
        ym_r = pair("ym", 8192, 9216, 4)
        mg2_r = pair("mg2", 4096, 6144, 8)

        xctx = w3(0, 8)
        sq1 = at(8704, 4096).rearrange("p (k n) -> p k n", k=8)
        gates = w3(8704, 16)
        sg = w3(12800, 8)
        v_tok = w3(14848, 2, 1024)
        qraw = w3(16896, 8)
        qk = w3(18944, 8)
        kc_tok = w3(20992, 2, 512)
        vc_tok = w3(22016, 2, 1024)
        fT = w3(24064, 4)
        oT = w3(25088, 8)
        decay = w3(27136, 2, 512)
        probs = w3(28160, 2, 512)
        qdec = w3(29184, 8)
        st_f = at(31232, 512)
        st_b = at(31744, 512)
        rs1 = at(32256, 512)
        kw_f = w3(0, 2, 512)
        kw_b = w3(1024, 2, 512)
        four_a = w3(2048, 8)
        zT = w3(16896, 4)
        mg = w3(14848, 8)
        sq_o = w3(29184, 8)
        sq = w3(8704, 8)
        uav = w3(27136, 4)
        ga = w3(28160, 2)
        ffn_t = at(16384, 256)
        zraw = w3(0, 14)
        zs = w3(3584, 14)
        zd = w3(7168, 14)
        mqk_raw = w3(10752, 8, 259)
        mqk = w3(12832, 8)
        mv_tok = w3(14880, 2, 512)
        so = w3(15904, 4)
        gates2 = w3(16928, 16)
        gT = w3(0, 4)
        bon = w3(1024, 4)
        lw = w3(2048, 4)
        kk = w3(7168, 4)
        cum = w3(8192, 4)
        wcum = w3(9216, 4)
        winv = w3(10752, 4)
        wprev = w3(11776, 4)
        bT = w3(12800, 4)
        aT = w3(13824, 4)
        atok = w3(14848, 2, 512)
        ar = at(21024, 2048).rearrange("p (j i a n) -> p j i a n", j=4, i=2, a=2)
        beta = w3(23072, 4)
        kappa = w3(24096, 4)
        btok = w3(25120, 2, 512)
        ktok = w3(26144, 2, 512)
        vtok = w3(27168, 2, 512)
        gram = at(2048, 8192).rearrange("p (n a s) -> p n a s", n=16, a=4)
        mt = at(10752, 2048).rearrange("p (n s) -> p n s", n=16)
        sa = w3(12800, 2, 512)
        yT = w3(13824, 4)
        states = at(23072, 1280).rearrange("p (n j v) -> p n j v", n=5, j=4)
        rw_tmp = w3(11776, 4)
        mg2 = w3(2048, 8)
        Xn = at(0, 2048, hx).rearrange("p (n s) -> p n s", n=16)
        XT = at(2048, 2048, hx).rearrange("p (n s) -> p n s", n=16)
        P1 = [at(off, 512).rearrange("p (n s) -> p n s", n=4) for off in (10240, 24352)]
        U0 = at(10752, 1024).rearrange("p (i n) -> p i n", i=2)
        ltmp = w3(23072, 4)
        xat = at(0, 1024, hx).rearrange("p (j i n) -> p j i n", j=4, i=2)
        lv = at(1024, 1024, hx).rearrange("p (i n) -> p i n", i=2)
        m_rows = at(21024, 2048).rearrange("p (r n) -> p r n", r=8)
        m_bc = w3(23072, 4, 512)
        m_e = w3(25120, 2, 512)
        m_p = w3(26144, 2, 512)
        m_dn = w3(27168, 4)
        qP = w3(4096, 16)
        s_sb = at(8192, 4096).rearrange("p (t g n) -> p t g n", t=2, g=16)
        topv = at(12288, 512).rearrange("p (t g n) -> p t g n", t=2, g=16)
        topi = at(12800, 512).rearrange("p (t g n) -> p t g n", t=2, g=16)
        topf = at(13312, 512).rearrange("p (t g n) -> p t g n", t=2, g=16)
        cand = at(13824, 4096).rearrange("p (t g n) -> p t g n", t=2, g=8)
        best = at(17920, 256).rearrange("p (t g n) -> p t g n", t=2, g=8)
        posi = at(18176, 256).rearrange("p (t g n) -> p t g n", t=2, g=8)
        hlo = at(18432, 1024)
        eqb = at(19456, 2048)
        selv = at(21504, 768).rearrange("p (t c n) -> p t c n", t=2, c=3)
        gsm = at(22272, 64)
        subk = at(28672, 2048).rearrange("p (g n) -> p g n", g=16)
        G = arena[:, 0:32768].rearrange("p (e n) -> p e n", e=128)
        selT = at(0, 768, late).rearrange("p (c n) -> p c n", c=3)
        onehot = at(768, 1024, late).rearrange("p (b c n e) -> p b c n e", b=2, c=2, n=2)
        gelu_t = at(0, 512, late).rearrange("p (b n) -> p b n", b=2)
        a_r = late_r[:, 768:1792].rearrange("p (c b n) -> p c b n", c=2, b=2)
        fin = at(0, 2048)

        mod = small[:, 0:96].rearrange("p (m c) -> p m c", c=2)
        csil = small[:, 96:112].rearrange("p (k c) -> p k c", c=2)
        gain = small[:, 112:128].rearrange("p (k c) -> p k c", c=2)
        lgpair = small[:, 128:136]
        lgrow = small[:, 136:152]
        wctx = small[:, 152:184].rearrange("p (t n) -> p t n", t=2)
        gain2 = small[:, 184:192]
        wend = small[:, 192:208].rearrange("p (j c) -> p j c", j=4)
        ucol = small[:, 208:216]
        ar2 = at(21024, 2048).rearrange("p (m a n) -> p m a n", m=8, a=2)
        lora_in = w3(24096, 2)
        m_sq = w3(23072, 4)
        fgrow = at(3072, 1024)
        fstat = small[:, 216:224]
        rs = small[:, 256:512]
        eps6, eps_gn, eps_ml = col("eps6"), col("eps_gn"), col("eps_ml")

        block = ctx.enter_context(nc.Block())

        @block.sync
        def _(sp):
            sp.dma_start(xres[:], t["xT"][:, 0]).then_inc(S["x_in"], 16)
            sp.dma_start(xctx, t["xT"][:, 1]).then_inc(S["x_in"], 16)

            def page(p, i=0):
                sp.dma_start(ring[:, p % RING], t["stream"][p + RING * i]).then_inc(loaded[p % RING], 16)

            for p in range(RING):
                page(p)
            with sp.Fori(0, SPLIT0 // RING) as i:
                for u in range(RING):
                    sp.wait_ge(S["mod_used"], RING * i + (u + 1))
                    page(RING + u, i)
            rounds = (NPAGES - SPLIT0) // RING - 1
            with sp.Fori(0, rounds) as i:
                for u in range(RING):
                    sp.wait_ge(S["lo_ready"], 2 * RING * i + (2 * u + 2))
                    page(SPLIT0 + RING + u, i)
            for p in range(SPLIT0 + RING + RING * rounds, NPAGES):
                sp.wait_ge(S["lo_ready"], 2 * (p - SPLIT0 - RING) + 2)
                page(p)

            for tt in range(2):
                sp.wait_ge(S["fin_out"], tt + 1)
                sp.dma_start(out[tt * P:(tt + 1) * P, :], fin[:, tt * 1024:(tt + 1) * 1024]).then_inc(S["out_dma"], 16)
            sp.wait_ge(S["out_dma"], 32)

        @block.gpsimd
        def _(pool):
            g = nc.gpsimd
            pool.wait_ge(S["const1_in"], 16)
            for hh in range(8):
                pool.wait_ge(S["decay_exp"], hh + 1)
                g.tensor_tensor(decay[:, hh % 2], decay[:, hh % 2], c1("mask12"), ALU.mult).then_inc(S["decay_m"], 1)
            pool.wait_ge(S["x_new"], 2)
            g.memset(mqk_raw[:, :, 0:3], 0.0).then_inc(S["mqk_pad"], 1)
            pool.wait_ge(S["const2_in"], 16)
            pool.wait_ge(S["gram_sb"], 16)
            for lev in range(5):
                m = c2("levels")[:, lev * P:(lev + 1) * P].unsqueeze(1).to_broadcast([P, 4, P])
                for gr in range(4):
                    if lev:
                        pool.wait_ge(S["p1_mm"], 4 * (lev - 1) + gr + 1)
                    g.tensor_tensor(mt[:, 4 * gr:4 * gr + 4, :], gram[:, 4 * gr:4 * gr + 4, 0, :], m,
                                    ALU.mult).then_inc(S["mt_ready"], 1)

        @block.tensor
        def _(pe):
            def piece_of(p):
                return 2 * (p - SPLIT0)

            def three(o, a, b, start, stop, skip=False):
                m = mm(o, a[1], b[0], start=start, stop=False, skip_group_check=skip)
                mm(o, a[0], b[0], start=False, stop=False, skip_group_check=skip)
                mm(o, a[0], b[1], start=False, stop=stop, skip_group_check=skip)
                return m, mm_last[0]

            mm_last = [None]

            def mm(*args, **kw):
                mm_last[0] = nc.tensor.matmul(*args, **kw)
                return mm_last[0]

            def part(c, k):
                return piece[:, 0, c % 3, k, :], piece[:, 1, c % 3, k, :]

            def piece_in(c, i=0):
                pe.wait_ge(S["lo_ready"], c + 1 + 2 * LOOP * i)

            def turn(T, i=0):
                v = T // 2 + LOOP // 2 * i
                if not (isinstance(v, int) and v <= 0):
                    pe.wait_ge(acc_free[T % 2], v)

            def wide(p, T, rhs, ctx):
                turn(T)
                if ctx:
                    turn(T + 1)
                for s in range(2):
                    c = piece_of(p) + s
                    piece_in(c)
                    w = [piece[:, q, c % 3].rearrange("p k m -> p (k m)").rearrange("p (k m) -> p k m", k=4) for q in range(2)]
                    for b, lhs in enumerate((h, hctx_r)[:1 + ctx]):
                        for e in range(2):
                            half = slice(e * P, (e + 1) * P)
                            for kk in range(4):
                                k = 4 * s + kk
                                if b == 0 and rhs:
                                    a, m_ = [w[q][:, kk, half] for q in range(2)], [rhs[q][:, k, :] for q in range(2)]
                                else:
                                    a, m_ = [lhs[q][:, k, half] for q in range(2)], [w[q][:, kk, :] for q in range(2)]
                                first, last = three(ps[:, (T + b) % 2, e * L:(e + 1) * L], a, m_, k == 0 and e == 0, k == 7,
                                                    True)
                                if b == 0 and e == 0 and kk == 0:
                                    first.then_inc(S["piece_used"], 1)
                        if s == 1:
                            last.then_inc(S["acc_ready"], 1)

            def fm_piece(c, o, rhs, i=0):
                piece_in(c, i)
                for k in range(8):
                    first, last = three(o, part(c, k), (rhs[0][:, k, :], rhs[1][:, k, :]), k == 0, k == 7)
                    if k == 0:
                        first.then_inc(S["piece_used"], 1)
                return last

            def fm_page(p, T, rhs, i=0):
                turn(T, i)
                for s in range(2):
                    last = fm_piece(piece_of(p) + s, ps[:, T % 2, s * L:(s + 1) * L], rhs, i)
                last.then_inc(S["acc_ready"], 1)

            def fm_pages(name, n, rhs):
                rounds = n // LOOP if n >= 2 * LOOP else 0
                if rounds:
                    with pe.Fori(0, rounds) as i:
                        for u in range(LOOP):
                            fm_page(PAGE[name] + u, TURN[name] + u, rhs, i)
                for u in range(LOOP * rounds, n):
                    fm_page(PAGE[name] + u, TURN[name] + u, rhs)

            def packed(name, T, K, rhs, tiles=8):
                for n in range(tiles * K):
                    c, tile, k = piece_of(PAGE[name]) + n // 8, n // K, n % K
                    if n % 8 == 0:
                        piece_in(c)
                    if tile % 2 == 0 and k == 0:
                        turn(T + tile // 2)
                    first, last = three(ps[:, (T + tile // 2) % 2, (tile % 2) * L:(tile % 2 + 1) * L], part(c, n % 8),
                                        (rhs[0][:, k, :], rhs[1][:, k, :]), k == 0, k == K - 1)
                    if n % 8 == 0:
                        first.then_inc(S["piece_used"], 1)
                    if tile % 2 == 1 and k == K - 1:
                        last.then_inc(S["acc_ready"], 1)

            def head_norm(src, sqb, pairs, weights, base, banks):
                for q in range(pairs):
                    mm(ps[:, banks[q], :], weights, src[:, 2 * q:2 * q + 2, :], start=True,
                       stop=True).then_inc(S["hn_mm"], 1)
                for q in range(pairs):
                    pe.wait_ge(S["hn_sq"], base + q + 1)
                    mm(ps[:, banks[pairs + q], :], weights, sqb[:, 2 * q:2 * q + 2, :], start=True,
                       stop=True).then_inc(S["hn_sqmm"], 1)

            def x_norm(n):
                pe.wait_ge(S["xs_sq"], n + 1)
                for k in range(8):
                    m = mm(ps[:, 2, 0:L], ones, sq[:, k, :], start=k == 0, stop=k == 7)
                m.then_inc(S["xs_mm"], 1)

            pe.wait_ge(S["pconst_in"], 16)
            pe.wait_ge(S["sq1"], 2)
            for k in range(8):
                m = mm(ps[:, 3, :], ones, sq1[:, k, :], start=k == 0, stop=k == 7)
            m.then_inc(S["stat1"], 1)

            pe.wait_ge(S["c_silu"], 1)
            with pe.Fori(0, SPLIT0 // RING) as i:
                for u in range(RING):
                    pe.wait_ge(loaded[u], 16 * i + 16)
                    for s in range(2):
                        for k in range(8):
                            m = mm(ps[:, 2, bass.ds(4 * RING * i + 2 * (2 * u + s), 2)], ring[:, u, s, k, :], csil[:, k, :],
                                   start=k == 0, stop=k == 7)
                    m.then_inc(S["mod_used"], 1)

            pe.wait_ge(S["h_ready"], 8)
            fm_pages("q", 2, h)
            pe.wait_ge(S["h_ready"], 16)
            for u in range(2):
                wide(PAGE["k"] + u, TURN["k"] + 2 * u, h, True)
            for u in range(4):
                wide(PAGE["v"] + u, TURN["v"] + 2 * u, None, True)
            fm_pages("g", 4, h)
            fm_pages("f", 2, h)
            pe.wait_ge(S["const1_in"], 16)
            for q in range(4):
                mm(ps[:, 4 + q, :], c1("perm"), qraw[:, 2 * q:2 * q + 2, :], start=True,
                   stop=True).then_inc(S["perm_mm"], 1)
            pe.wait_ge(S["kw_ready"], 1)
            for d, kw in enumerate((kw_f, kw_b)):
                for hh in range(8):
                    r, j = (hh % 2) * 64, hh // 2
                    for tt in range(2):
                        m = mm(ps[r:r + 64, 2 + d, j * P:(j + 1) * P], kw[:, tt, hh * 64:(hh + 1) * 64],
                               vc_tok[:, tt, hh * P:(hh + 1) * P], start=tt == 0, stop=tt == 1)
                m.then_inc(S["state_mm"], 1)
            fm_pages("bg", 8, h)

            def scores(n):
                r, j = (n % 2) * 64, n // 2
                if n >= 2:
                    pe.wait_ge(S["probs"], n - 1)
                for st in range(2):
                    m = mm(ps[:, 4 + n % 2, st * L:(st + 1) * L], qk[r:r + 64, 4 + j, st * P:(st + 1) * P],
                           qk[r:r + 64, j, :], start=True, stop=True)
                m.then_inc(S["scores"], 1)

            def outputs(n):
                r, j = (n % 2) * 64, n // 2
                pe.wait_ge(S["probs"], n + 1)
                if n >= 2:
                    pe.wait_ge(S["o_sb"], n - 1)
                o = ps[:, 6 + n % 2, 0:L]
                for st in range(2):
                    mm(o, v_tok[:, st, n * P:(n + 1) * P], probs[:, n % 2, st * L:(st + 1) * L], start=st == 0,
                       stop=False)
                mm(o, st_f[r:r + 64, j * P:(j + 1) * P], qdec[r:r + 64, j, :], start=False, stop=False)
                mm(o, st_b[r:r + 64, j * P:(j + 1) * P], qdec[r:r + 64, 4 + j, :], start=False,
                   stop=True).then_inc(S["out_mm"], 1)

            pe.wait_ge(S["qk_ready"], 4)
            scores(0)
            pe.wait_ge(S["state_sb"], 2)
            pe.wait_ge(S["qdec"], 2)
            for n in range(8):
                if n < 7:
                    scores(n + 1)
                outputs(n)

            for n in range(8):
                b = (2, 3, 4, 5)[n // 2]
                if n % 2 == 0 and b == 5:
                    pe.wait_ge(S["probs"], 8)
                m = mm(ps[:, b, (n % 2) * L:(n % 2 + 1) * L], fT[:, n // 2, (n % 2) * P:(n % 2 + 1) * P], c1("dft_d"),
                       start=True, stop=True)
                if n % 2 == 1:
                    m.then_inc(S["fourier1"], 1)
            pe.wait_ge(S["o_sb"], 8)
            pe.wait_ge(S["four_sb"], 4)
            dft_l = c1("dft_l", "p (c t n) -> p c t n", c=2, t=2)
            for gi in range(4):
                n = 0
                for lt in range(2):
                    for c in range(2):
                        m = mm(ps[:, 6 + gi // 2, (gi % 2) * L:(gi % 2 + 1) * L],
                               four_a[:, 2 * gi + lt, c * P:(c + 1) * P], dft_l[:, c, lt, :], start=n == 0, stop=n == 3)
                        n += 1
                if gi % 2 == 1:
                    m.then_inc(S["fourier2"], 1)
            for q in range(4):
                mm(ps[:, 2 + q, :], ones, oT[:, 2 * q:2 * q + 2, :], start=True, stop=True).then_inc(S["hn_mm"], 1)
            pe.wait_ge(S["z_sb"], 2)
            for q in range(4):
                pe.wait_ge(S["hn_sq"], q + 1)
                mm(ps[:, (6, 7, 2, 3)[q], :], ones, sq_o[:, 2 * q:2 * q + 2, :], start=True,
                   stop=True).then_inc(S["hn_sqmm"], 1)
            pe.wait_ge(S["ret_ready"], 1)
            fm_pages("ro", 4, o_r)
            packed("fo", TURN["fo"], 4, z_r)
            pe.wait_ge(S["mg_ready"], 1)
            fm_pages("wo", 4, mg_r)
            x_norm(0)
            pe.wait_ge(S["h_new"], 8)
            fm_pages("up", 22, h)
            pe.wait_ge(S["ffn_ready"], 24)
            packed("dn", TURN["dn"], 22, ffn_r)
            x_norm(1)
            x_norm(2)
            pe.wait_ge(S["h_new"], 16)
            fm_pages("lora", 1, h)
            fm_pages("rkv", 6, h)
            fm_pages("mqk", 4, h)
            for u in range(2):
                wide(PAGE["mv"] + u, TURN["mv"] + u, None, False)
            fm_pages("mo", 2, h)
            pe.wait_ge(S["const2_in"], 16)
            T = TURN["if"]
            turn(T)
            w_if = c2("w_if", "p (k c) -> p k c", k=8)
            for c in range(2):
                for k in range(16):
                    m = mm(ps[0:4, T % 2, c * L:(c + 1) * L], w_if[:, k % 8, 4 * c:4 * c + 4], h[k // 8][:, k % 8, :].bitcast(F32),
                           start=k == 0, stop=k == 15)
            m.then_inc(S["acc_ready"], 1)
            fm_pages("gt", 8, h)

            pe.wait_ge(S["rows_done"], 2)
            for tt in range(2):
                m = nc.tensor.transpose(ps[:, 2, 4 * tt:4 * tt + 4], m_rows[0:4, 4, tt * P:(tt + 1) * P], ident[0:4, 0:4])
            m.then_inc(S["uc_mm"], 1)
            for n in range(4):
                mm(ps[:, 4 + n, :], c2("sel")[0:4, n * P:(n + 1) * P], m_rows[0:4, 5:7, :], start=True,
                   stop=True).then_inc(S["bc_mm"], 1)
            pe.wait_ge(S["mqk_silu"], 8)
            pe.wait_ge(S["uc_sb"], 1)

            def m_scores(n):
                if n >= 2:
                    pe.wait_ge(S["m_probs"], n - 1)
                for st in range(2):
                    m = mm(ps[:, 2 + n % 2, st * L:(st + 1) * L], mqk[:, 4 + n, st * P:(st + 1) * P], mqk[:, n, :],
                           start=True, stop=True)
                m.then_inc(S["ms_mm"], 1)

            m_scores(0)
            pe.wait_ge(S["em_row"], 4)
            for n in range(4):
                if n < 3:
                    m_scores(n + 1)
                pe.wait_ge(S["m_probs"], n + 1)
                if n >= 2:
                    pe.wait_ge(S["m_h"], n - 1)
                for st in range(2):
                    mm(ps[:, 4 + n % 2, 0:L], mv_tok[:, st, n * P:(n + 1) * P], m_p[:, n % 2, st * L:(st + 1) * L],
                       start=st == 0, stop=st == 1)
                for st in range(2):
                    m = mm(ps[:, 4 + n % 2, L:2 * L], ones, m_p[:, n % 2, st * L:(st + 1) * L], start=st == 0,
                           stop=st == 1)
                m.then_inc(S["nd_mm"], 1)
            pe.wait_ge(S["m_h"], 4)
            head_norm(m_dn, m_sq, 2, ones, 4, (6, 7, 2, 3))

            pe.wait_ge(S["ym_ready"], 1)
            pe.wait_ge(S["lora_tanh"], 2)
            wa_up, g_up = c2("wa_up"), c2("g_up")
            for q in range(6):
                for e in range(2):
                    m_ = (2 * q + e) % 4
                    o = ps[:, 2 + q, e * L:(e + 1) * L]
                    if q < 2:
                        m = mm(o, wa_up[0:64, m_ * P:(m_ + 1) * P], lora_in[0:64, 0, :], start=True, stop=True)
                    elif q < 4:
                        m = mm(o, wa_up[64:128, m_ * P:(m_ + 1) * P], zs[64:128, 12, :], start=True, stop=True)
                    else:
                        m = mm(o, g_up[:, m_ * P:(m_ + 1) * P], lora_in[:, 1, :], start=True, stop=True)
                m.then_inc(S["lora_mm"], 1)
            pe.wait_ge(S["kk_sq"], 1)
            pe.wait_ge(S["lora_act"], 4)
            for q in range(2):
                mm(ps[:, 2 + q, :], bones, ltmp[:, 2 * q:2 * q + 2, :], start=True, stop=True).then_inc(S["kk_mm"], 1)
            pe.wait_ge(S["bon_in"], 1)
            pe.wait_ge(S["lora_act"], 12)
            for q in range(2):
                mm(ps[:, 4 + q, :], bones, bon[:, 2 * q:2 * q + 2, :], start=True, stop=True).then_inc(S["bon_mm"], 1)
            pe.wait_ge(S["alpha_ready"], 1)
            for n in range(8):
                src, i = n // 2, n % 2
                if n >= 6:
                    pe.wait_ge(S["tok_sb"], n - 5)
                for j in range(4):
                    sl = slice(i * P, (i + 1) * P)
                    s_ = (ar[:, j, i, 0, :], beta[:, j, sl], kappa[:, j, sl], zs[:, 8 + j, sl])[src]
                    m = nc.tensor.transpose(ps[:, 2 + n % 6, j * P:(j + 1) * P], s_, ident)
                m.then_inc(S["tok_mm"], 1)
            pe.wait_ge(S["tok_sb"], 8)
            for n in range(16):
                i, hh = n // 8, n % 8
                r, j = (hh % 2) * 64, hh // 2
                sl = slice(i * P, (i + 1) * P)
                if n >= 4:
                    pe.wait_ge(S["gram_sb"], n - 3)
                o = ps[:, 2 + n % 4, :]
                mm(o[:, 0:256], beta[r:r + 64, j, sl], ar[r:r + 64, j, i, :, :], start=True, stop=True)
                mm(o[:, 256:512], kappa[r:r + 64, j, sl], ar[r:r + 64, j, i, :, :], start=True,
                   stop=True).then_inc(S["gram_mm"], 1)
                if n % 4 == 0 and n >= 4:
                    pe.wait_ge(S["x_init"], n // 4)
                c = n // 2 % 2
                m = mm(ps[:, 6 + n % 2, c * P:(c + 1) * P], ar[r:r + 64, j, i, 0, :], beta[r:r + 64, j, sl], start=True,
                       stop=True)
                if n % 4 == 3:
                    m.then_inc(S["l_mm"], 1)
            pe.wait_ge(S["x_init"], 4)

            def first_product(q):
                g4 = 4 * (q % 4)
                pe.wait_ge(S["mt_ready"], q + 1)
                if q >= 4:
                    pe.wait_ge(S["x_sb"], q - 3)
                if q >= 2:
                    pe.wait_ge(S["p1_sb"], q - 1)
                for e in range(4):
                    m = mm(ps[:, 2 + q % 2, e * P:(e + 1) * P], mt[:, g4 + e, :], Xn[:, g4 + e, :], start=True, stop=True)
                m.then_inc(S["p1_mm"], 1)

            first_product(0)
            for q in range(20):
                if q < 19:
                    first_product(q + 1)
                g4 = 4 * (q % 4)
                pe.wait_ge(S["p1_sb"], q + 1)
                if q >= 2:
                    pe.wait_ge(S["x_sb"], q - 1)
                for e in range(4):
                    if q < 16:
                        mm(ps[:, 4 + q % 2, e * P:(e + 1) * P], XT[:, g4 + e, :], P1[q % 2][:, e, :], start=True, stop=True)
                    m = mm(ps[:, 6 + q % 2, e * P:(e + 1) * P], P1[q % 2][:, e, :], XT[:, g4 + e, :], start=True, stop=True)
                m.then_inc(S["x_mm"], 1)
            pe.wait_ge(S["x_sb"], 20)
            for i in range(2):
                for hh in range(8):
                    r, j, n = (hh % 2) * 64, hh // 2, 8 * i + hh
                    m = mm(ps[r:r + 64, 2 + i, j * P:(j + 1) * P], atok[:, i, hh * 64:(hh + 1) * 64], XT[:, n, :],
                           start=True, stop=True)
                m.then_inc(S["xa_mm"], 1)
            for i in range(2):
                for hh in range(8):
                    m = mm(ps[:, 4 + i, hh * 64:(hh + 1) * 64], gram[:, 8 * i + hh, 2, :], vtok[:, i, hh * 64:(hh + 1) * 64],
                           start=True, stop=True)
                m.then_inc(S["xa_mm"], 1)
            for i in range(2):
                pe.wait_ge(S["lv_sb"], i + 1)
                for hh in range(8):
                    m = mm(ps[:, 6 + i, hh * 64:(hh + 1) * 64], XT[:, 8 * i + hh, :], lv[:, i, hh * 64:(hh + 1) * 64],
                           start=True, stop=True)
                m.then_inc(S["u0_mm"], 1)
            pe.wait_ge(S["xa_sb"], 2)
            pe.wait_ge(S["lv_sb"], 2)
            for n in range(4):
                i, r0 = n // 2, (n % 2) * 64
                pe.wait_ge(S["s_sb"], n + 1)
                for hh in range(8):
                    r, j = (hh % 2) * 64, hh // 2
                    c = 256 * (n % 2) + 64 * j
                    m = mm(ps[r0:r0 + 64, 2 + hh % 2, c:c + 64], xat[r:r + 64, j, i, r0:r0 + 64],
                           states[r:r + 64, n, j, :], start=True, stop=True)
                m.then_inc(S["sa_mm"], 1)
                pe.wait_ge(S["sa_sb"], n + 1)
                if n == 3:
                    break
                for hh in range(8):
                    r, j, c = (hh % 2) * 64, hh // 2, slice(hh * 64, (hh + 1) * 64)
                    o = ps[r:r + 64, 4 + n % 2, j * 64:(j + 1) * 64]
                    mm(o, btok[r0:r0 + 64, i, c], sa[r0:r0 + 64, i, c], start=True, stop=False)
                    m = mm(o, ktok[r0:r0 + 64, i, c], vtok[r0:r0 + 64, i, c], start=False, stop=True)
                m.then_inc(S["ds_mm"], 1)
            pe.wait_ge(S["u0_sb"], 2)
            for i in range(2):
                for hh in range(8):
                    r, j, c, n = (hh % 2) * 64, hh // 2, slice(hh * 64, (hh + 1) * 64), 8 * i + hh
                    o = ps[r:r + 64, 6 + i, j * P:(j + 1) * P]
                    mm(o, sa[:, i, c], gram[:, n, 1, :], start=True, stop=False)
                    mm(o, vtok[:, i, c], gram[:, n, 3, :], start=False, stop=False)
                    for e in range(2):
                        m = mm(o[:, e * 64:(e + 1) * 64], states[r:r + 64, 2 * i + e, j, :],
                               ar[r:r + 64, j, i, 1, e * 64:(e + 1) * 64], start=False, stop=e == 1)
                m.then_inc(S["y_mm"], 1)
            pe.wait_ge(S["y_sb"], 2)
            head_norm(yT, rw_tmp, 2, bones, 6, (2, 3, 4, 5))
            pe.wait_ge(S["y_ready"], 1)
            packed("pr", TURN["pr"], 4, y_r)
            pe.wait_ge(S["y_ready"], 2)
            packed("pm", TURN["pm"], 4, ym_r)
            pe.wait_ge(S["mg_ready"], 2)
            fm_pages("w2", 4, mg2_r)
            x_norm(3)
            pe.wait_ge(S["xs_root"], 4)
            for n in range(4):
                for k in range(4):
                    m = mm(ps[:, 2 + n, k * P:(k + 1) * P], xres[:, 4 * (n % 2) + k, (n // 2) * P:(n // 2 + 1) * P], ident,
                           start=k == 0, stop=False, skip_group_check=True)
            m.then_inc(S["x_in_psum"], 1)
            pe.wait_ge(S["h_new"], 24)

            pe.wait_ge(S["subk_in"], 16)

            def key_scores(n):
                T = TURN["wq"] + n
                pe.wait_ge(acc_free[T % 2], T // 2 + 1)
                if n >= 2:
                    pe.wait_ge(S["key_sb"], n - 1)
                for e in range(4):
                    m = mm(ps[:, 6 + n % 2, e * P:(e + 1) * P], qP[:, 2 * n + e % 2, (e // 2) * P:(e // 2 + 1) * P],
                           subk[:, 2 * n + e % 2, :], start=True, stop=True)
                m.then_inc(S["key_mm"], 1)

            for n in range(8):
                fm_page(PAGE["wq"] + n, TURN["wq"] + n, h)
                if n >= 1:
                    key_scores(n - 1)
            key_scores(7)
            pe.wait_ge(S["key_sb"], 8)
            for tt in range(2):
                pe.wait_ge(S["selt_ready"], tt + 1)
                for c in range(3):
                    m = nc.tensor.transpose(ps[:, 6 + tt, c * P:(c + 1) * P], selv[:, tt, c, :], ident)
                m.then_inc(S["selt_mm"], 1)

            def scatter(i):
                for b in range(4):
                    n = 4 * i + b
                    pe.wait_ge(S["oh_ready"], n + 1)
                    if b % 2 == 0 and not isinstance(i, int):
                        pe.wait_ge(S["g_sb"], 2 * i + (b // 2 - 1))
                    for e in range(2):
                        c = 2 * (b % 2) + e
                        m = mm(ps[:, 6 + b // 2, c * P:(c + 1) * P], onehot[:, b % 2, 0, e, :], onehot[:, b % 2, 1, e, :],
                               start=True, stop=True)
                    m.then_inc(S["g_mm"], 1)

            pe.wait_ge(S["selt_sb"], 2)
            scatter(0)
            with pe.Fori(1, L // 8) as i:
                scatter(i)

            C0, T0 = piece_of(PAGE["peer"]), TURN["peer"]

            def up(e, c, i=0):
                turn(T0 + e, i)
                fm_piece(c, ps[:, (T0 + e) % 2, 0:L], h, i).then_inc(S["acc_ready"], 1)

            def down(e, c, i=0):
                piece_in(c, i)
                pe.wait_ge(S["a_ready"], e + 1 + LOOP * i)
                for tt in range(2):
                    tok = slice(tt * P, (tt + 1) * P)
                    for half in range(2):
                        o = ps[:, 2 + 2 * tt + half, :]
                        a = a_r[:, 0, e % 2, tok], a_r[:, 1, e % 2, tok]
                        v = [piece[:, q, c % 3, 4 * half:4 * half + 4, :] for q in range(2)]
                        end = isinstance(i, int) and e == P - 1
                        f = mm(o, a[1], v[0], start=False, stop=False, skip_group_check=True)
                        if tt == 0 and half == 0:
                            f.then_inc(S["piece_used"], 1)
                        mm(o, a[0], v[0], start=False, stop=False, skip_group_check=True)
                        m = mm(o, a[0], v[1], start=False, stop=end, skip_group_check=True)
                if end:
                    m.then_inc(S["experts_done"], 1)

            pe.wait_ge(S["g_sb"], L // 4)
            up(0, C0)
            up(1, C0 + 1)
            with pe.Fori(0, 126 // LOOP) as i:
                for u in range(LOOP):
                    down(u, C0 + 2 + 2 * u, i)
                    up(2 + u, C0 + 3 + 2 * u, i)
            down(126, C0 + 254)
            down(127, C0 + 255)

        @block.scalar
        def _(act):
            A = nc.scalar.activation

            def split(p, i=0):
                for s in range(2):
                    c = 2 * (p - SPLIT0) + s
                    if s == 0:
                        act.wait_ge(loaded[p % RING], 16 * (p // RING + 1 + LOOP // RING * i))
                    if c >= 2 or not isinstance(i, int):
                        act.wait_ge(S["piece_used"], c - 1 + 2 * LOOP * i)
                    A(piece[:, 0, c % 3], ring[:, p % RING, s], ACT.Copy).then_inc(S["hi_ready"], 1)

            def stage(name, n, epilogue=None):
                rounds = n // LOOP if n >= 2 * LOOP else 0
                if rounds:
                    with act.Fori(0, rounds) as i:
                        for u in range(LOOP):
                            split(PAGE[name] + u + 1, i)
                            if epilogue:
                                epilogue(u, i)
                for u in range(LOOP * rounds, n):
                    if PAGE[name] + u + 1 < NPAGES:
                        split(PAGE[name] + u + 1)
                    if epilogue:
                        epilogue(u, 0)

            def evac(T, dst, func=ACT.Copy, src=slice(0, 512), i=0, per=0, **kw):
                act.wait_ge(S["acc_ready"], T + 1 + 2 * per * i)
                A(dst, ps[:, T % 2, src], func, **kw).then_inc(acc_free[T % 2], 1)

            def head_norm(src, sqb, pairs, base, banks, n, eps):
                for q in range(pairs):
                    act.wait_ge(S["hn_cs"], base + q + 1)
                    A(sqb[:, 2 * q:2 * q + 2, :], src[:, 2 * q:2 * q + 2, :], ACT.Square).then_inc(S["hn_sq"], 1)
                for q in range(pairs):
                    act.wait_ge(S["hn_sqmm"], base + q + 1)
                    A(sqb[:, 2 * q:2 * q + 2, :], ps[:, banks[q], :].rearrange("p (a n) -> p a n", a=2), ACT.Sqrt,
                      scale=1.0 / n, bias=eps).then_inc(S["hn_root"], 1)

            def x_norm(n):
                act.wait_ge(S["x_new"], n + 1)
                A(sq, xres[:], ACT.Square).then_inc(S["xs_sq"], 1)
                act.wait_ge(S["xs_mm"], n + 1)
                A(rs, ps[:, 2, 0:L], ACT.Sqrt, scale=1.0 / D, bias=eps6).then_inc(S["xs_root"], 1)

            act.dma_start(csil, t["cT"]).then_inc(S["c_in"], 16)
            act.dma_start(cols[:], t["cols"]).then_inc(S["cols_in"], 16)
            act.dma_start(pc[:], t["pconst"]).then_inc(S["pconst_in"], 16)
            act.wait_ge(S["c_in"], 16)
            A(csil, csil, ACT.Silu).then_inc(S["c_silu"], 1)
            act.wait_ge(S["x_in"], 32)
            A(sq1[:, :, 0:L], xres[:], ACT.Square).then_inc(S["sq1"], 1)
            A(sq1[:, :, L:], xctx, ACT.Square).then_inc(S["sq1"], 1)
            act.wait_ge(S["cols_in"], 16)
            A(lgpair, col("dec_pair", 0, 8), ACT.Exp)
            A(lgrow, col("dec_row", 0, 16), ACT.Exp).then_inc(S["lg_ready"], 1)
            act.wait_ge(S["stat1"], 1)
            A(rs1, ps[:, 3, :], ACT.Sqrt, scale=1.0 / D, bias=eps6).then_inc(S["root1"], 1)
            act.dma_start(at(4096, N1), t["const1"]).then_inc(S["const1_in"], 16)
            split(SPLIT0)
            for n in range(16):
                c, k = n // 8, n % 8
                act.wait_ge(S["hraw"], n + 1)
                A((h, hctx_r)[c][0][:, k, :], (h_tmp, xctx)[c][:, k, :], ACT.Identity,
                  bias=mod[:, k, c:c + 1]).then_inc(S["h_hi"], 1)
            stage("q", 2, lambda u, i: evac(TURN["q"] + u, qraw[:, 2 * u:2 * u + 2, :]))

            def k_page(u, i):
                evac(TURN["k"] + 2 * u, qraw[:, 4 + 2 * u:6 + 2 * u, :])
                evac(TURN["k"] + 2 * u + 1, kc_tok[:, :, u * L:(u + 1) * L])

            stage("k", 2, k_page)
            act.wait_ge(S["wctx_arg"], 1)
            A(small[:, 152:184], small[:, 152:184], ACT.Exp).then_inc(S["wctx"], 1)
            act.wait_ge(S["const1_in"], 16)
            for n in range(8):
                A(qdec[:, n, :], c1("pos_q")[:, (n // 4) * L:(n // 4 + 1) * L], ACT.Exp,
                  scale=lgpair[:, n:n + 1]).then_inc(S["w_q"], 1)

            def v_page(u, i):
                evac(TURN["v"] + 2 * u, v_tok[:, :, u * L:(u + 1) * L])
                evac(TURN["v"] + 2 * u + 1, vc_tok[:, :, u * L:(u + 1) * L])

            stage("v", 4, v_page)
            stage("g", 4, lambda u, i: evac(TURN["g"] + u, sg[:, 2 * u:2 * u + 2, :], ACT.Silu))
            stage("f", 2, lambda u, i: evac(TURN["f"] + u, fT[:, 2 * u:2 * u + 2, :]))
            for d, st in enumerate((st_f, st_b)):
                act.wait_ge(S["state_mm"], d + 1)
                A(st, ps[:, 2 + d, :], ACT.Copy).then_inc(S["state_sb"], 1)

            def sigmoids(name, dst, bias):
                def page(u, i):
                    T = TURN[name] + u
                    act.wait_ge(S["acc_ready"], T + 1)
                    for s in range(2):
                        m = 2 * u + s
                        a = A(dst[:, m, :], ps[:, T % 2, s * L:(s + 1) * L], ACT.Sigmoid, bias=col(bias, m))
                    a.then_inc(acc_free[T % 2], 1)
                stage(name, 8, page)

            def hi_part(pairs, src, dst, sem, base=0):
                for q in range(pairs):
                    act.wait_ge(S[sem], base + q + 1)
                    A(dst[:, 2 * q:2 * q + 2, :], src[:, 2 * q:2 * q + 2, :], ACT.Copy).then_inc(S["part_hi"], 1)

            sigmoids("bg", gates, "b_bg")

            def decay_exp(n):
                act.wait_ge(S["decay_arg"], n + 1)
                A(decay[:, n % 2, :], decay[:, n % 2, :], ACT.Exp).then_inc(S["decay_exp"], 1)

            decay_exp(0)
            decay_exp(1)
            for n in range(8):
                act.wait_ge(S["out_mm"], n + 1)
                A(oT[:, n, :], ps[:, 6 + n % 2, 0:L], ACT.Copy).then_inc(S["o_sb"], 1)
                if n < 6:
                    decay_exp(n + 2)
            for n in range(4):
                act.wait_ge(S["fourier1"], n + 1)
                A(four_a[:, 2 * n:2 * n + 2, :], ps[:, 2 + n, :].rearrange("p (a n) -> p a n", a=2),
                  ACT.Copy).then_inc(S["four_sb"], 1)
            head_norm(oT, sq_o, 4, 0, (6, 7, 2, 3), 128, eps6)
            hi_part(2, zT, z_r[0], "z_sb")
            hi_part(4, oT, o_r[0], "part_in")
            stage("ro", 4)
            stage("fo", 2)
            hi_part(4, mg, mg_r[0], "part_in", 4)
            stage("wo", 4)
            act.wait_ge(S["x_new"], 1)
            act.dma_start(at(28672, N2), t["const2"]).then_inc(S["const2_in"], 16)
            x_norm(0)
            for k in range(8):
                act.wait_ge(S["hraw"], 16 + k + 1)
                A(h[0][:, k, :], sq[:, k, :], ACT.Identity, bias=mod[:, 24 + k, 0:1]).then_inc(S["h_hi"], 1)

            def conv_page(u, i):
                T, b = TURN["up"] + u, u % 2
                n = LOOP * i + u
                act.wait_ge(S["acc_ready"], T + 1 + LOOP * i)
                act.wait_ge(S["ffn_ready"], n + 1)
                c0 = COL["conv"][0]
                for s in range(2):
                    a = A(uav[:, 2 * b + s, :], ps[:, T % 2, s * L:(s + 1) * L], ACT.Identity,
                          scale=cols[:, bass.ds(8 * LOOP * i + (c0 + 8 * u + 4 * s + 1), 1)],
                          bias=cols[:, bass.ds(8 * LOOP * i + (c0 + 8 * u + 4 * s + 3), 1)])
                a.then_inc(S["conv_mid"], 1)
                act.wait_ge(S["conv_u"], n + 1)
                A(ga[:, b, :], uav[:, 2 * b, :], ACT.Gelu_apprx_tanh).then_inc(S["gelu_done"], 1)

            stage("up", 22, conv_page)
            stage("dn", 11)
            x_norm(1)
            x_norm(2)
            for k in range(8):
                act.wait_ge(S["hraw"], 24 + k + 1)
                A(h[0][:, k, :], sq[:, k, :], ACT.Copy).then_inc(S["h_hi"], 1)
            stage("lora", 1, lambda u, i: evac(TURN["lora"], zraw[:, 12:14, :]))
            stage("rkv", 6, lambda u, i: evac(TURN["rkv"] + u, zraw[:, 2 * u:2 * u + 2, :]))
            act.wait_ge(S["mqk_pad"], 1)
            stage("mqk", 4, lambda u, i: evac(TURN["mqk"] + u, mqk_raw[:, 2 * u:2 * u + 2, 3:259]))
            stage("mv", 2, lambda u, i: evac(TURN["mv"] + u, mv_tok[:, :, u * L:(u + 1) * L]))
            stage("mo", 2, lambda u, i: evac(TURN["mo"] + u, so[:, 2 * u:2 * u + 2, :], ACT.Sigmoid))
            T = TURN["if"]
            act.wait_ge(S["acc_ready"], T + 1)
            A(m_rows[0:4, 0, :], ps[0:4, T % 2, 0:L], ACT.Identity, bias=col("if_b", 0)[0:4])
            A(m_rows[0:4, 1, :], ps[0:4, T % 2, L:2 * L], ACT.Identity, bias=col("if_b", 1)[0:4]).then_inc(acc_free[T % 2], 1)
            sigmoids("gt", gates2, "gate_b")
            cq = COL["cqk"][0]
            for n in range(8):
                A(mqk[:, n, :], mqk_raw[:, n, 3:259], ACT.Identity, scale=cols[:, cq + 5 * n + 3:cq + 5 * n + 4],
                  bias=cols[:, cq + 5 * n + 4:cq + 5 * n + 5]).then_inc(S["mqk_conv"], 1)
            act.wait_ge(S["lf_abs"], 1)
            A(m_rows[0:4, 2, :], m_rows[0:4, 2, :], ACT.Exp, scale=-1.0).then_inc(S["lf_exp"], 1)
            act.wait_ge(S["lf_exp"], 1)
            A(m_rows[0:4, 2, :], m_rows[0:4, 2, :], ACT.Ln, bias=1.0).then_inc(S["lf_ln"], 1)
            act.wait_ge(S["rows_done"], 1)
            A(m_rows[0:4, 6, :], m_rows[0:4, 6, :], ACT.Exp).then_inc(S["rows_done"], 1)
            for n in range(8):
                act.wait_ge(S["mqk_taps"], n + 1)
                A(mqk[:, n, :], mqk[:, n, :], ACT.Silu).then_inc(S["mqk_silu"], 1)
            act.wait_ge(S["uc_mm"], 1)
            A(ucol, ps[:, 2, 0:8], ACT.Copy).then_inc(S["uc_sb"], 1)
            for n in range(4):
                act.wait_ge(S["bc_mm"], n + 1)
                A(m_bc[:, n, :], ps[:, 4 + n, :], ACT.Copy).then_inc(S["em_row"], 1)
            for n in range(4):
                act.wait_ge(S["m_arg"], n + 1)
                A(m_e[:, n % 2, :], m_e[:, n % 2, :], ACT.Exp, scale=-1.0).then_inc(S["m_exp"], 1)
            head_norm(m_dn, m_sq, 2, 4, (2, 3), 128, eps_ml)
            act.wait_ge(S["zs_ready"], 2)
            A(lora_in[0:64, 0, :], zs[0:64, 12, :], ACT.Tanh).then_inc(S["lora_tanh"], 1)
            A(lora_in[:, 1, :], zs[:, 13, :], ACT.Sigmoid).then_inc(S["lora_tanh"], 1)
            for q in range(6):
                act.wait_ge(S["lora_mm"], q + 1)
                for e in range(2):
                    m = (2 * q + e) % 4
                    src = ps[:, 2 + q, e * L:(e + 1) * L]
                    if q < 2:
                        a = A(lw[:, m, :], src, ACT.Sigmoid, bias=col("w0", m))
                    elif q < 4:
                        a = A(aT[:, m, :], src, ACT.Sigmoid, bias=col("a0", m))
                    else:
                        a = A(gT[:, m, :], src, ACT.Copy)
                    a.then_inc(S["lora_act"], 1)
            for q in range(2):
                act.wait_ge(S["kk_mm"], q + 1)
                A(ltmp[:, 2 * q:2 * q + 2, :], ps[:, 2 + q, :].rearrange("p (a n) -> p a n", a=2),
                  ACT.Sqrt).then_inc(S["kk_root"], 1)
            act.wait_ge(S["scan_done"], 1)
            A(wcum, cum, ACT.Exp).then_inc(S["w_exp"], 1)
            A(winv, cum, ACT.Exp, scale=-1.0).then_inc(S["w_exp"], 1)
            A(wprev, wprev, ACT.Exp).then_inc(S["w_exp"], 1)
            for n in range(8):
                act.wait_ge(S["tok_mm"], n + 1)
                A((atok, btok, ktok, vtok)[n // 2][:, n % 2, :], ps[:, 2 + n % 6, :], ACT.Copy).then_inc(S["tok_sb"], 1)
            for q in range(20):
                act.wait_ge(S["p1_mm"], q + 1)
                if q >= 2:
                    act.wait_ge(S["x_mm"], q - 1)
                A(P1[q % 2], ps[:, 2 + q % 2, :].rearrange("p (a n) -> p a n", a=4), ACT.Copy).then_inc(S["p1_sb"], 1)
            for i in range(2):
                act.wait_ge(S["xa_mm"], i + 1)
                A(xat[:, :, i, :], ps[:, 2 + i, :].rearrange("p (a n) -> p a n", a=4), ACT.Copy).then_inc(S["xa_sb"], 1)
            for i in range(2):
                act.wait_ge(S["xa_mm"], i + 3)
                A(lv[:, i, :], ps[:, 4 + i, :], ACT.Copy).then_inc(S["lv_sb"], 1)
            for i in range(2):
                act.wait_ge(S["u0_mm"], i + 1)
                A(U0[:, i, :], ps[:, 6 + i, :], ACT.Copy).then_inc(S["u0_sb"], 1)
            head_norm(yT, rw_tmp, 2, 6, (4, 5), 64, eps_gn)
            hi_part(2, yT, y_r[0], "part_in", 8)
            hi_part(2, so, ym_r[0], "part_in", 10)
            act.dma_start(subk.rearrange("p g n -> p (g n)"), t["subk"]).then_inc(S["subk_in"], 16)
            stage("pr", 2)
            stage("pm", 2)
            hi_part(4, mg2, mg2_r[0], "part_in", 12)
            stage("w2", 4)
            x_norm(3)
            for k in range(8):
                act.wait_ge(S["hraw"], 32 + k + 1)
                A(h[0][:, k, :], sq[:, k, :], ACT.Copy).then_inc(S["h_hi"], 1)

            def key_evac(n):
                act.wait_ge(S["key_mm"], n + 1)
                A(s_sb[:, :, 2 * n:2 * n + 2, :].rearrange("p t g n -> p t (g n)"),
                  ps[:, 6 + n % 2, :].rearrange("p (t n) -> p t n", t=2), ACT.Copy).then_inc(S["key_sb"], 1)

            def wq_page(u, i):
                evac(TURN["wq"] + u, qP[:, 2 * u:2 * u + 2, :])
                if u >= 1:
                    key_evac(u - 1)

            stage("wq", 8, wq_page)
            key_evac(7)
            for tt in range(2):
                act.wait_ge(S["g_arg"], tt + 1)
                A(selv[:, tt, 2, :], selv[:, tt, 2, :], ACT.Exp).then_inc(S["g_exp"], 1)
            act.wait_ge(S["x_in_psum"], 1)
            for tt in range(2):
                act.wait_ge(S["selt_mm"], tt + 1)
                A(selT[:, :, tt * P:(tt + 1) * P], ps[:, 6 + tt, 0:384].rearrange("p (a n) -> p a n", a=3),
                  ACT.Copy).then_inc(S["selt_sb"], 1)
            with act.Fori(0, L // 8) as i:
                for b in range(2):
                    n = 2 * i + b
                    act.wait_ge(S["g_mm"], 2 * n + 2)
                    A(G[:, :, bass.ds(4 * n, 4)].rearrange("p e n -> p n e"),
                      ps[:, 6 + b, :].rearrange("p (a n) -> p a n", a=4), ACT.Copy).then_inc(S["g_sb"], 1)

            def gelu(e, i=0):
                T = TURN["peer"] + e
                act.wait_ge(S["acc_ready"], T + 1 + LOOP * i)
                if not (isinstance(i, int) and e < 2):
                    act.wait_ge(S["a_ready"], LOOP * i + (e - 1))
                A(gelu_t[:, e % 2, :], ps[:, T % 2, 0:L], ACT.Gelu).then_inc(acc_free[T % 2], 1)

            E0 = PAGE["peer"]
            split(E0 + 1)
            gelu(0)
            gelu(1)
            with act.Fori(0, 126 // LOOP) as i:
                for u in range(LOOP):
                    split(E0 + 2 + u, i)
                    gelu(2 + u, i)
            act.wait_ge(S["a_ready"], P)
            act.dma_start(fgrow, t["fg"]).then_inc(S["fg_in"], 16)
            act.wait_ge(S["experts_done"], 1)
            for tt in range(2):
                A(at(1024 * tt, 1024).rearrange("p (a n) -> p a n", a=2), ps[:, 2 + 2 * tt:4 + 2 * tt, :], ACT.Square,
                  accum_out=fstat[:, tt:tt + 1]).then_inc(S["fin_sq"], 1)
            for tt in range(2):
                act.wait_ge(S["fin_sq"], tt + 1)
                A(fstat[:, 2 + tt:3 + tt], fstat[:, tt:tt + 1], ACT.Sqrt, scale=1.0 / D, bias=eps6).then_inc(S["fin_root"], 1)

        @block.vector
        def _(dve):
            V = nc.vector
            TT, STT, TS = V.tensor_tensor, V.scalar_tensor_tensor, V.tensor_scalar
            steps = [0]

            def dv(ins):
                steps[0] += 1
                ins.then_inc(S["dch"], 1)
                dve.wait_ge(S["dch"], steps[0])

            def split(p, i=0):
                for s in range(2):
                    c = 2 * (p - SPLIT0) + s
                    dve.wait_ge(S["hi_ready"], c + 1 + 2 * LOOP * i)
                    TT(piece[:, 1, c % 3], ring[:, p % RING, s], piece[:, 0, c % 3].bitcast(F32),
                       ALU.subtract).then_inc(S["lo_ready"], 1)

            def stage(name, n, epilogue=None):
                rounds = n // LOOP if n >= 2 * LOOP else 0
                if rounds:
                    with dve.Fori(0, rounds) as i:
                        for u in range(LOOP):
                            split(PAGE[name] + u + 1, i)
                            if epilogue:
                                epilogue(u, i)
                for u in range(LOOP * rounds, n):
                    if PAGE[name] + u + 1 < NPAGES:
                        split(PAGE[name] + u + 1)
                    if epilogue:
                        epilogue(u, 0)

            parts = [0]

            def lo_part(pairs, src, dst, sem=None):
                for q in range(pairs):
                    parts[0] += 1
                    dve.wait_ge(S["part_hi"], parts[0])
                    sl = slice(2 * q, 2 * q + 2)
                    ins = TT(dst[1][:, sl, :], src[:, sl, :], dst[0][:, sl, :].bitcast(F32), ALU.subtract)
                    if q == pairs - 1 and sem:
                        ins.then_inc(S[sem], 1)

            def turn_read(T):
                dve.wait_ge(acc_free[T % 2], T // 2 + 1)

            def head_norm(src, sqb, pairs, base, banks, n):
                for q in range(pairs):
                    v = src[:, 2 * q:2 * q + 2, :]
                    dve.wait_ge(S["hn_mm"], base + q + 1)
                    STT(v, ps[:, banks[q], :].rearrange("p (a n) -> p a n", a=2), -1.0 / n, v, ALU.mult,
                        ALU.add).then_inc(S["hn_cs"], 1)
                for q in range(pairs):
                    v, w = src[:, 2 * q:2 * q + 2, :], sqb[:, 2 * q:2 * q + 2, :]
                    dve.wait_ge(S["hn_root"], base + q + 1)
                    dv(V.reciprocal(w, w))
                    dv(TT(v, v, w, ALU.mult))

            his = [16]

            def x_norm(n, dst, gain, shift=None):
                dve.wait_ge(S["xs_root"], n + 1)
                dv(V.reciprocal(rs, rs))
                sem = "xfin" if dst is xres else "hraw"
                for k in range(8):
                    STT(dst[:, k, :], xres[:, k, :], gain[:, k:k + 1], rs, ALU.mult, ALU.mult).then_inc(S[sem], 1)
                if dst is xres:
                    return
                for k in range(8):
                    his[0] += 1
                    dve.wait_ge(S["h_hi"], his[0])
                    STT(h[1][:, k, :], dst[:, k, :], 0.0 if shift is None else mod[:, shift + k, 0:1],
                        h[0][:, k, :].bitcast(F32), ALU.add, ALU.subtract).then_inc(S["h_new"], 1)

            dve.wait_ge(S["lg_ready"], 1)
            dv(TS(small[:, 128:152], small[:, 128:152], -1.0, None, ALU.mult))
            dve.wait_ge(S["root1"], 1)
            dv(V.reciprocal(rs1, rs1))
            split(SPLIT0)
            dve.wait_ge(S["mod_used"], SPLIT0)
            dv(TT(mod, ps[:, 2, 0:96].rearrange("p (m c) -> p m c", c=2),
                  col("b_mod", 0, 48).unsqueeze(2).to_broadcast([P, 48, 2]), ALU.add))
            dv(TS(gain, mod[:, 8:16, :], 1.0, None, ALU.add))
            dv(TT(gain, gain, col("norm1_w", 0, 8).unsqueeze(2).to_broadcast([P, 8, 2]), ALU.mult))
            dv(TS(gain2, mod[:, 32:40, 0], 1.0, None, ALU.add))
            dv(TT(gain2, gain2, col("norm2_w", 0, 8), ALU.mult))
            for n in range(16):
                c, k = n // 8, n % 8
                STT((h_tmp, xctx)[c][:, k, :], (xres, xctx)[c][:, k, :], gain[:, k, c:c + 1], rs1[:, c * L:(c + 1) * L],
                    ALU.mult, ALU.mult).then_inc(S["hraw"], 1)
            for n in range(16):
                c, k = n // 8, n % 8
                hi, lo = (h, hctx_r)[c]
                dve.wait_ge(S["h_hi"], n + 1)
                STT(lo[:, k, :], (h_tmp, xctx)[c][:, k, :], mod[:, k, c:c + 1], hi[:, k, :].bitcast(F32), ALU.add,
                    ALU.subtract).then_inc(S["h_ready"], 1)
            dve.wait_ge(S["const1_in"], 16)
            TT(wctx, c1("pos_ctx", "p (t n) -> p t n", t=2), lgrow.unsqueeze(1).to_broadcast([P, 2, 16]),
               ALU.mult).then_inc(S["wctx_arg"], 1)
            stage("q", 2)
            stage("k", 2)
            stage("v", 4)
            stage("g", 4)
            stage("f", 2)
            for q in range(4):
                cos = c1("cosq" if q < 2 else "cosk").unsqueeze(1).to_broadcast([P, 2, L])
                sin = c1("sinq" if q < 2 else "sink").unsqueeze(1).to_broadcast([P, 2, L])
                dve.wait_ge(S["perm_mm"], q + 1)
                dv(TT(qk[:, 2 * q:2 * q + 2, :], ps[:, 4 + q, :].rearrange("p (a n) -> p a n", a=2), sin, ALU.mult))
                dv(TT(qraw[:, 2 * q:2 * q + 2, :], qraw[:, 2 * q:2 * q + 2, :], cos, ALU.mult))
                TT(qk[:, 2 * q:2 * q + 2, :], qk[:, 2 * q:2 * q + 2, :], qraw[:, 2 * q:2 * q + 2, :],
                   ALU.add).then_inc(S["qk_ready"], 1)
            dve.wait_ge(S["wctx"], 1)
            for d, kw in enumerate((kw_f, kw_b)):
                for tt in range(2):
                    w = wctx[:, tt, 8 * d:8 * d + 8].unsqueeze(2).to_broadcast([P, 8, 64])
                    ins = TT(kw[:, tt, :].rearrange("p (h c) -> p h c", h=8),
                             kc_tok[:, tt, :].rearrange("p (h c) -> p h c", h=8), w, ALU.mult)
                    if d == 1 and tt == 1:
                        ins.then_inc(S["kw_ready"], 1)
            dve.wait_ge(S["w_q"], 8)
            dve.wait_ge(S["qk_ready"], 4)
            for d in range(2):
                TT(qdec[:, 4 * d:4 * d + 4, :], qdec[:, 4 * d:4 * d + 4, :], qk[:, 0:4, :], ALU.mult).then_inc(S["qdec"], 1)

            def decay_arg(n):
                d = decay[:, n % 2, :]
                dv(TS(d, c1("dist_f"), lgrow[:, n:n + 1], None, ALU.mult))
                STT(d, c1("dist_b"), lgrow[:, 8 + n:9 + n], d, ALU.mult, ALU.add).then_inc(S["decay_arg"], 1)

            stage("bg", 8)
            decay_arg(0)
            decay_arg(1)
            for n in range(8):
                dve.wait_ge(S["scores"], n + 1)
                dve.wait_ge(S["decay_m"], n + 1)
                if n >= 2:
                    dve.wait_ge(S["out_mm"], n - 1)
                TT(probs[:, n % 2, :], ps[:, 4 + n % 2, :], decay[:, n % 2, :], ALU.mult).then_inc(S["probs"], 1)
                if n < 6:
                    dve.wait_ge(S["probs"], n + 1)
                    decay_arg(n + 2)
            for q in range(2):
                dve.wait_ge(S["fourier2"], q + 1)
                V.tensor_copy(zT[:, 2 * q:2 * q + 2, :], ps[:, 6 + q, :].rearrange("p (a n) -> p a n", a=2)).then_inc(S["z_sb"], 1)
            head_norm(oT, sq_o, 4, 0, (2, 3, 4, 5), 128)
            lo_part(2, zT, z_r)
            for q in range(4):
                sl = slice(2 * q, 2 * q + 2)
                TT(oT[:, sl, :], oT[:, sl, :], sg[:, sl, :], ALU.mult).then_inc(S["part_in"], 1)
            lo_part(4, oT, o_r, "ret_ready")

            def merge(names, pages, gate, dst, dst_r):
                for b, name in enumerate(names):
                    def page(u_, i):
                        turns = 4 // pages[b]
                        for u in range(turns * u_, turns * (u_ + 1)):
                            T = TURN[name] + u
                            dve.wait_ge(S["acc_ready"], T + 1)
                            v = ps[:, T % 2, :].rearrange("p (a n) -> p a n", a=2)
                            g2 = gate[:, 8 * b + 2 * u:8 * b + 2 * u + 2, :]
                            d2 = dst[:, 2 * u:2 * u + 2, :]
                            if b == 0:
                                TT(d2, v, g2, ALU.mult).then_inc(acc_free[T % 2], 1)
                            else:
                                TT(g2, v, g2, ALU.mult).then_inc(acc_free[T % 2], 1)
                                dve.wait_ge(acc_free[T % 2], T // 2 + 1)
                                TT(d2, d2, g2, ALU.add).then_inc(S["part_in"], 1)
                    stage(name, pages[b], page)
                lo_part(4, dst, dst_r, "mg_ready")

            def residual(name, gate=None):
                def add(u, i=0):
                    T = TURN[name] + u
                    dve.wait_ge(S["acc_ready"], T + 1)
                    if gate is None:
                        x2 = xres[:, 2 * u:2 * u + 2, :]
                        ins = TT(x2, x2, ps[:, T % 2, :].rearrange("p (a n) -> p a n", a=2), ALU.add)
                    else:
                        for s in range(2):
                            k = 2 * u + s
                            ins = STT(xres[:, k, :], ps[:, T % 2, s * L:(s + 1) * L], mod[:, gate + k, 0:1], xres[:, k, :],
                                      ALU.mult, ALU.add)
                    ins.then_inc(acc_free[T % 2], 1)
                if name == "dn":
                    stage(name, 11, lambda u, i: add((2, 5, 8, 10).index(u)) if u in (2, 5, 8, 10) else None)
                else:
                    stage(name, 4, add)
                T = TURN[name] + 3
                dve.wait_ge(acc_free[T % 2], T // 2 + 1)
                dve.wait_ge(acc_free[(T - 1) % 2], (T - 1) // 2 + 1)
                V.engine_nop().then_inc(S["x_new"], 1)

            merge(("ro", "fo"), (4, 2), gates, mg, mg_r)
            residual("wo", 16)
            x_norm(0, sq, gain2, 24)

            def conv_page(u, i):
                T, b = TURN["up"] + u, u % 2
                n = LOOP * i + u
                c0 = COL["conv"][0] + 8 * u
                dve.wait_ge(S["conv_mid"], n + 1)
                for s in range(2):
                    x, y = ps[:, T % 2, s * L:(s + 1) * L], uav[:, 2 * b + s, :]
                    STT(y[:, 1:], x[:, :L - 1], cols[:, bass.ds(8 * LOOP * i + (c0 + 4 * s), 1)], y[:, 1:], ALU.mult,
                        ALU.add).then_inc(S["up_chain"], 1)
                    dve.wait_ge(S["up_chain"], 4 * n + (s + 1))
                    ins = STT(y[:, :L - 1], x[:, 1:], cols[:, bass.ds(8 * LOOP * i + (c0 + 4 * s + 2), 1)], y[:, :L - 1],
                              ALU.mult, ALU.add)
                    ins.then_inc(S["conv_u"] if s == 0 else acc_free[T % 2], 1)
                dve.wait_ge(acc_free[T % 2], T // 2 + 1 + LOOP // 2 * i)
                dve.wait_ge(S["gelu_done"], n + 1)
                hi, lo = (ffn_r[q][:, bass.ds(n, 1), :].rearrange("p a n -> p (a n)") for q in range(2))
                TT(uav[:, 2 * b + 1, :], ga[:, b, :], uav[:, 2 * b + 1, :], ALU.mult).then_inc(S["up_chain"], 1)
                dve.wait_ge(S["up_chain"], 4 * n + 3)
                V.tensor_copy(hi, uav[:, 2 * b + 1, :]).then_inc(S["up_chain"], 1)
                dve.wait_ge(S["up_chain"], 4 * n + 4)
                TT(lo, uav[:, 2 * b + 1, :], hi.bitcast(F32), ALU.subtract).then_inc(S["ffn_ready"], 1)

            V.engine_nop().then_inc(S["ffn_ready"], 1)
            V.engine_nop().then_inc(S["ffn_ready"], 1)
            stage("up", 22, conv_page)
            residual("dn", 40)
            x_norm(1, xres, col("final_norm_w", 0, 8))
            dve.wait_ge(S["xfin"], 8)
            V.engine_nop().then_inc(S["x_new"], 1)
            x_norm(2, sq, col("norm1_g_2", 0, 8))
            stage("lora", 1)
            stage("rkv", 6)
            for T in (TURN["rkv"] + 5, TURN["rkv"] + 4):
                turn_read(T)
            V.tensor_scalar(zd[:, :, 0], zraw[:, :, 0], -1.0, None, ALU.mult)
            dv(TT(zd[:, :, 1:], zraw[:, :, :L - 1], zraw[:, :, 1:], ALU.subtract))
            for n in (12, 13, *range(12)):
                ins = STT(zs[:, n, :], zd[:, n, :], col("mu", n), zraw[:, n, :], ALU.mult, ALU.add)
                if n >= 12 or n == 11:
                    ins.then_inc(S["zs_ready"], 1)
            for name, n in (("mqk", 4), ("mv", 2), ("mo", 2), ("gt", 8)):
                stage(name, n)
            turn_read(TURN["if"])
            r = m_rows[0:4]
            STT(r[:, 2, :], r[:, 1, :], -1.0, r[:, 1, :], ALU.mult, ALU.max).then_inc(S["lf_abs"], 1)
            dv(TS(r[:, 1, :], r[:, 1, :], 0.0, None, ALU.min))
            dv(V.memset(r[:, 7, :], 1.0))
            dve.wait_ge(S["lf_ln"], 1)
            dv(TT(r[:, 3, :], r[:, 1, :], r[:, 2, :], ALU.subtract))
            dv(V.tensor_tensor_scan(r[:, 1, :], r[:, 7, :], r[:, 3, :], 0.0, ALU.mult, ALU.add))
            dv(TT(r[:, 4, :], r[:, 0, :], r[:, 1, :], ALU.subtract))
            dv(V.tensor_tensor_scan(r[:, 5, :], r[:, 4, :], r[:, 4, :], 0.0, ALU.max, ALU.max))
            dv(TT(r[:, 6, :], r[:, 1, :], r[:, 5, :], ALU.add))
            TS(r[:, 6, :], r[:, 6, :], -1.0, 88.0, ALU.mult, ALU.min).then_inc(S["rows_done"], 1)
            cq = COL["cqk"][0]
            for n in range(8):
                dve.wait_ge(S["mqk_conv"], n + 1)
                for tap in range(3):
                    ins = STT(mqk[:, n, :], mqk_raw[:, n, tap:tap + L], cols[:, cq + 5 * n + tap:cq + 5 * n + tap + 1],
                              mqk[:, n, :], ALU.mult, ALU.add)
                    if tap < 2:
                        dv(ins)
                ins.then_inc(S["mqk_taps"], 1)
            dve.wait_ge(S["uc_sb"], 1)

            def m_arg(n):
                dve.wait_ge(S["em_row"], n + 1)
                for st in range(2):
                    ins = TS(m_e[:, n % 2, st * L:(st + 1) * L], m_bc[:, n, 0:L], ucol[:, 4 * st + n:4 * st + n + 1], 0.0,
                             ALU.subtract, ALU.max)
                ins.then_inc(S["m_arg"], 1)

            def m_head(n):
                dve.wait_ge(S["nd_mm"], n + 1)
                d = m_dn[:, n, :]
                den = ps[:, 4 + n % 2, L:2 * L]
                dv(STT(d, den, -1.0, m_bc[:, n, L:2 * L], ALU.mult, ALU.max))
                dv(STT(d, den, 1.0, d, ALU.mult, ALU.max))
                dv(V.reciprocal(d, d))
                TT(d, d, ps[:, 4 + n % 2, 0:L], ALU.mult).then_inc(S["m_h"], 1)

            m_arg(0)
            for n in range(4):
                if n < 3:
                    m_arg(n + 1)
                dve.wait_ge(S["m_exp"], n + 1)
                dv(TT(m_e[:, n % 2, :], m_e[:, n % 2, :], c2("causal"), ALU.mult))
                dve.wait_ge(S["ms_mm"], n + 1)
                if n >= 2:
                    dve.wait_ge(S["nd_mm"], n - 1)
                STT(m_p[:, n % 2, :], ps[:, 2 + n % 2, :], 128.0 ** -0.5, m_e[:, n % 2, :], ALU.mult,
                    ALU.mult).then_inc(S["m_probs"], 1)
                dve.wait_ge(S["m_probs"], n + 1)
                if n >= 1:
                    m_head(n - 1)
            m_head(3)
            dve.wait_ge(S["m_h"], 4)
            head_norm(m_dn, m_sq, 2, 4, (6, 7), 128)
            turn_read(TURN["mo"] + 1)
            for n in range(4):
                ins = STT(so[:, n, :], m_dn[:, n, :], col("ml_norm", n), so[:, n, :], ALU.mult, ALU.mult)
            ins.then_inc(S["ym_ready"], 1)

            dve.wait_ge(S["zs_ready"], 3)
            for m in range(4):
                TS(kk[:, m, :], zs[:, 4 + m, :], col("k_k", m), None, ALU.mult).then_inc(S["kk_in"], 1)
            dve.wait_ge(S["kk_in"], 4)
            TT(ltmp, kk, kk, ALU.mult).then_inc(S["kk_sq"], 1)
            dve.wait_ge(S["lora_act"], 4)
            dv(TS(lw, lw, -EXP_HALF, None, ALU.mult))
            for m in range(4):
                ins = V.tensor_tensor_scan(cum[:, m, :], c2("scan"), lw[:, m, :], 0.0, ALU.mult, ALU.add)
            dv(ins)
            TT(wprev, cum, lw, ALU.subtract).then_inc(S["scan_done"], 1)
            dve.wait_ge(S["kk_root"], 2)
            dv(TS(ltmp, ltmp, 1e-12, None, ALU.max))
            dv(V.reciprocal(ltmp, ltmp))
            dv(TT(kk, kk, ltmp, ALU.mult))
            dve.wait_ge(S["lora_act"], 8)
            for m in range(4):
                ins = TS(ltmp[:, m, :], aT[:, m, :], -1.0, col("k_a", m), ALU.add, ALU.mult)
            dv(ins)
            dv(STT(zs[:, 4:8, :], ltmp, 1.0, zs[:, 4:8, :], ALU.add, ALU.mult))
            TT(bT, kk, aT, ALU.mult)
            dv(TT(bon, zs[:, 0:4, :], zs[:, 4:8, :], ALU.mult))
            for m in range(4):
                ins = TS(bon[:, m, :], bon[:, m, :], col("r_k", m), None, ALU.mult)
            ins.then_inc(S["bon_in"], 1)
            for q in range(2):
                dve.wait_ge(S["bon_mm"], q + 1)
                TT(bon[:, 2 * q:2 * q + 2, :], ps[:, 4 + q, :].rearrange("p (a n) -> p a n", a=2),
                   zs[:, 8 + 2 * q:10 + 2 * q, :], ALU.mult)
            dve.wait_ge(S["w_exp"], 3)
            flat = "p j (i n) -> p (j i) n"
            STT(ar2[:, :, 0, :], wprev.rearrange(flat, i=2), -1.0, kk.rearrange(flat, i=2), ALU.mult, ALU.mult)
            TT(ar2[:, :, 1, :], wcum.rearrange(flat, i=2), zs[:, 0:4, :].rearrange(flat, i=2), ALU.mult)
            TT(beta, bT, winv, ALU.mult)
            V.tensor_copy(wend, wcum[:, :, 63::64])
            TT(kappa, zs[:, 4:8, :], winv, ALU.mult).then_inc(S["alpha_ready"], 1)
            for n in range(16):
                g4 = n // 4
                dve.wait_ge(S["gram_mm"], n + 1)
                TT(gram[:, n].rearrange("p a s -> p (a s)"), ps[:, 2 + n % 4, :], c2("mask4"), ALU.mult).then_inc(S["gram_sb"], 1)
                if n % 4 == 3:
                    X4, T4 = Xn[:, n - 3:n + 1, :], XT[:, n - 3:n + 1, :]
                    idb = ident.unsqueeze(1).to_broadcast([P, 4, P])
                    dve.wait_ge(S["l_mm"], g4 + 1)
                    l4 = ps[:, 6:8, 0:256].rearrange("p e (a n) -> p a e n", a=2)
                    dv(TT(X4.rearrange("p (a e) n -> p a e n", a=2), l4,
                          c2("m1").unsqueeze(1).unsqueeze(1).to_broadcast([P, 2, 2, P]), ALU.mult))
                    dve.wait_ge(S["gram_sb"], n + 1)
                    dv(TT(T4, gram[:, n - 3:n + 1, 0, :], c2("m1t").unsqueeze(1).to_broadcast([P, 4, P]), ALU.mult))
                    TT(X4, X4, idb, ALU.add)
                    TT(T4, T4, idb, ALU.add).then_inc(S["x_init"], 1)
            V.memset(states[:, 0], 0.0).then_inc(S["s_sb"], 1)
            for q in range(20):
                g4 = 4 * (q % 4)
                dve.wait_ge(S["x_mm"], q + 1)
                if q < 16:
                    TT(Xn[:, g4:g4 + 4, :], Xn[:, g4:g4 + 4, :], ps[:, 4 + q % 2, :].rearrange("p (a n) -> p a n", a=4), ALU.add)
                TT(XT[:, g4:g4 + 4, :], XT[:, g4:g4 + 4, :], ps[:, 6 + q % 2, :].rearrange("p (a n) -> p a n", a=4),
                   ALU.add).then_inc(S["x_sb"], 1)
            dve.wait_ge(S["u0_sb"], 2)
            for n in range(4):
                i, c = n // 2, n % 2
                rr = slice(64 * c, 64 * c + 64)
                dve.wait_ge(S["sa_mm"], n + 1)
                by_row = "p (j e v) -> p e j v"
                TT(sa[rr, i, :].rearrange(by_row, e=2, v=64),
                   ps[rr, 2:4, 256 * c:256 * c + 256].rearrange("p e (j v) -> p e j v", v=64),
                   U0[rr, i, :].rearrange(by_row, e=2, v=64), ALU.add).then_inc(S["sa_sb"], 1)
                if n < 3:
                    dve.wait_ge(S["ds_mm"], n + 1)
                    dv(TT(states[:, n + 1], states[:, n], ps[:, 4 + c, 0:256].rearrange("p (j v) -> p j v", j=4), ALU.add))
                    TT(states[:, n + 1], states[:, n + 1], wend[:, :, n:n + 1].to_broadcast([P, 4, 64]),
                       ALU.mult).then_inc(S["s_sb"], 1)
                    dve.wait_ge(S["s_sb"], n + 2)
            for i in range(2):
                dve.wait_ge(S["y_mm"], i + 1)
                V.tensor_copy(yT[:, :, i * P:(i + 1) * P],
                              ps[:, 6 + i, :].rearrange("p (j n) -> p j n", j=4)).then_inc(S["y_sb"], 1)
            dve.wait_ge(S["y_sb"], 2)
            head_norm(yT, rw_tmp, 2, 6, (2, 3), 64)
            for m in range(4):
                ins = TS(yT[:, m, :], yT[:, m, :], col("gn_w", m), col("gn_b", m), ALU.mult, ALU.add)
            dv(ins)
            dv(TT(yT, yT, bon, ALU.add))
            for q in range(2):
                sl = slice(2 * q, 2 * q + 2)
                TT(yT[:, sl, :], yT[:, sl, :], gT[:, sl, :], ALU.mult).then_inc(S["part_in"], 1)
            V.engine_nop().then_inc(S["part_in"], 1)
            V.engine_nop().then_inc(S["part_in"], 1)
            lo_part(2, yT, y_r, "y_ready")
            lo_part(2, so, ym_r, "y_ready")
            merge(("pr", "pm"), (2, 2), gates2, mg2, mg2_r)
            residual("w2")
            x_norm(3, sq, col("norm2_g", 0, 8))

            def best16s(srcs, vals, idxs):
                for v, x in zip(vals, srcs):
                    ins = V.max(v[:, 0:8], x)
                dv(ins)
                for v, x, j in zip(vals, srcs, idxs):
                    V.max_index(j[:, 0:8].bitcast(U32), v[:, 0:8], x)
                for v, x in zip(vals, srcs):
                    ins = V.match_replace(x, v[:, 0:8], x, -3.0e38)
                dv(ins)
                for v, x in zip(vals, srcs):
                    ins = V.max(v[:, 8:16], x)
                dv(ins)
                for v, x, j in zip(vals, srcs, idxs):
                    ins = V.max_index(j[:, 8:16].bitcast(U32), v[:, 8:16], x)
                dv(ins)

            def select(hh, i=0):
                dve.wait_ge(S["key_sb"], hh + 1)
                both = [(tt, 2 * hh + c) for tt in range(2) for c in range(2)]
                best16s(*([a[:, tt, g_, :] for tt, g_ in both] for a in (s_sb, topv, topi)))
                for tt in range(2):
                    ins = TT(cand[:, tt, hh, :].rearrange("p (a b) -> p a b", a=16),
                             topv[:, tt, 2 * hh, :].unsqueeze(2).to_broadcast([P, 16, 16]),
                             topv[:, tt, 2 * hh + 1, :].unsqueeze(1).to_broadcast([P, 16, 16]), ALU.add)
                dv(ins)
                best16s(*([a[:, tt, hh, :] for tt in range(2)] for a in (cand, best, posi)))

            stage("wq", 8, lambda u, i: select(u - 1) if u else None)
            select(7)
            for tt in range(2):
                dv(V.tensor_copy(topf[:, tt], topi[:, tt].bitcast(U32)))
                tf = topf[:, tt].rearrange("p (h c) n -> p h c n", c=2)
                pi = posi[:, tt].rearrange("p g n -> p (g n)").bitcast(U32)
                TS(hlo[:, 0:128].bitcast(U32), pi, 4, None, ALU.logical_shift_right)
                dv(TS(hlo[:, 128:256].bitcast(U32), pi, 15, None, ALU.bitwise_and))
                dv(V.tensor_copy(hlo[:, 256:512], hlo[:, 0:256].bitcast(U32)))
                for c in range(2):
                    e4 = eqb.rearrange("p (h k j) -> p h k j", h=8, k=16)
                    pf = hlo[:, 256 + 128 * c:384 + 128 * c].rearrange("p (h k) -> p h k", h=8)
                    dv(TT(e4, iota[:, 0:16].unsqueeze(1).unsqueeze(1).to_broadcast([P, 8, 16, 16]),
                          pf.unsqueeze(3).to_broadcast([P, 8, 16, 16]), ALU.is_equal))
                    dv(TT(e4, e4, tf[:, :, c, :].unsqueeze(2).to_broadcast([P, 8, 16, 16]), ALU.mult))
                    dv(V.tensor_reduce(selv[:, tt, c, :], eqb.rearrange("p (m j) -> p m j", j=16), AX, ALU.add))
                gv = selv[:, tt, 2, :].rearrange("p (h k) -> p h k", h=8)
                TT(gv, best[:, tt], best[:, tt, :, 0:1].to_broadcast([P, 8, 16]), ALU.subtract).then_inc(S["g_arg"], 1)
                dve.wait_ge(S["g_exp"], tt + 1)
                dv(V.tensor_reduce(gsm[:, 0:8], gv, AX, ALU.add))
                dv(V.reciprocal(gsm[:, 0:8], gsm[:, 0:8]))
                TT(gv, gv, gsm[:, 0:8].unsqueeze(2).to_broadcast([P, 8, 16]), ALU.mult).then_inc(S["selt_ready"], 1)

            def onehots(i):
                for b in range(4):
                    n = 4 * i + b
                    if not (isinstance(i, int) and n < 2):
                        dve.wait_ge(S["g_mm"], 4 * i + (b - 1))
                    for e in range(2):
                        TS(onehot[:, b % 2, 0, e, :], iota, selT[:, 0, bass.ds(2 * n + e, 1)], None, ALU.is_equal)
                        ins = TS(onehot[:, b % 2, 1, e, :], iota, selT[:, 1, bass.ds(2 * n + e, 1)],
                                 selT[:, 2, bass.ds(2 * n + e, 1)], ALU.is_equal, ALU.mult)
                    ins.then_inc(S["oh_ready"], 1)

            dve.wait_ge(S["selt_sb"], 2)
            onehots(0)
            with dve.Fori(1, L // 8) as i:
                onehots(i)
            dve.wait_ge(S["g_sb"], L // 4)

            def gate(e, i=0):
                T = TURN["peer"] + e
                b = e % 2
                dve.wait_ge(acc_free[T % 2], T // 2 + 1 + LOOP // 2 * i)
                a_t = gelu_t[:, b, :]
                TT(a_t, gelu_t[:, b, :], G[:, bass.ds(LOOP * i + e, 1), :].rearrange("p a n -> p (a n)"),
                   ALU.mult).then_inc(S["a_chain"], 1)
                dve.wait_ge(S["a_chain"], 2 * e + 1 + 2 * LOOP * i)
                V.tensor_copy(a_r[:, 0, b, :], a_t).then_inc(S["a_chain"], 1)
                dve.wait_ge(S["a_chain"], 2 * e + 2 + 2 * LOOP * i)
                TT(a_r[:, 1, b, :], a_t, a_r[:, 0, b, :].bitcast(F32), ALU.subtract).then_inc(S["a_ready"], 1)

            E0 = PAGE["peer"]
            split(E0 + 1)
            gate(0)
            gate(1)
            with dve.Fori(0, 126 // LOOP) as i:
                for u in range(LOOP):
                    split(E0 + 2 + u, i)
                    gate(2 + u, i)
            dve.wait_ge(S["fg_in"], 16)
            for tt in range(2):
                f = fin[:, tt * 1024:(tt + 1) * 1024]
                dve.wait_ge(S["fin_root"], tt + 1)
                dv(V.reciprocal(fstat[:, 2 + tt:3 + tt], fstat[:, 2 + tt:3 + tt]))
                STT(f.rearrange("p (a n) -> p a n", a=2), ps[:, 2 + 2 * tt:4 + 2 * tt, :], fstat[:, 2 + tt:3 + tt],
                    fgrow.rearrange("p (a n) -> p a n", a=2), ALU.mult, ALU.mult).then_inc(S["fin_out"], 1)


def lay_out(x):
    f = {k: np.asarray(v) for k, v in x.items()}

    def tiles(w, order=None):
        K, M = w.shape
        w = w.reshape(K // P, P, M // P, P).transpose(2, 0, 1, 3)
        return w if order is None else w[order]

    def pages(w, order=None):
        w = tiles(w, order).reshape(-1, 16, P, P)
        return w.transpose(0, 2, 1, 3).reshape(-1, P, 2048)

    def wide_pages(w):
        return w.reshape(KD, P, -1, L).transpose(2, 1, 0, 3).reshape(-1, P, 2048)

    wi, w2 = f["w_in"][0], f["w_in_2"][0]
    up_order = [m for e in range(22) for m in (e, 22 + e)]
    u = f["peer_u_2"][0].reshape(P, P, KD, P).transpose(1, 3, 2, 0).reshape(P, P, 1024)
    v = f["peer_v_2"][0].reshape(P, P, D).transpose(1, 0, 2)
    parts = [pages(f["w_mod"][0]), pages(wi[:, 0:512]), wide_pages(wi[:, 512:1024]), wide_pages(wi[:, 1024:2048]),
             pages(wi[:, 2048:3072]), pages(wi[:, 3072:3584]), pages(f["w_branch_gate"][0]), pages(f["w_ret_out"][0]),
             pages(f["w_four_out"][0]), pages(f["w_out"][0]), pages(f["w_up"][0], up_order), pages(f["w_down"][0]),
             pages(w2[:, 1536:1792]), pages(w2[:, 0:1536]), pages(w2[:, 1792:2816]), wide_pages(w2[:, 2816:3328]),
             pages(w2[:, 3328:3840]), pages(w2[:, 3848:5896]), pages(f["p_rw_2"][0]), pages(f["p_ml_2"][0]),
             pages(f["w_out_2"][0]), pages(f["peer_w_q_2"][0])]
    stream = np.empty((NPAGES, P, 2048), np.float32)
    n = 0
    for part in parts:
        stream[n:n + len(part)] = part
        n += len(part)
    left, right = stream[n:, :, :1024], stream[n:, :, 1024:]
    left[0], right[0] = u[0], u[1]
    left[1:], right[1:127], right[127] = v[:127], u[2:], v[127]

    def column(a):
        return a.reshape(-1, P).T

    def full(a, n):
        return np.broadcast_to(a.reshape(1, -1), (P, n))

    conv = np.stack([f["conv_w"][0][0], f["conv_w"][0][1], f["conv_w"][0][2], f["conv_b"][0]])
    conv = conv.reshape(4, 2, 22, P).transpose(3, 2, 1, 0).reshape(P, 176)
    cqk = np.stack([np.concatenate([f[f"ml_conv_{n}_w_2"][0], f[f"ml_conv_{n}_b_2"][0][None]]) for n in "qk"])
    cqk = cqk.reshape(2, 5, 4, P).transpose(3, 0, 2, 1).reshape(P, 40)
    df, db = f["ret_decay_f"][0], f["ret_decay_b"][0]
    if_b = np.zeros((P, 2), np.float32)
    if_b[0:4, 0], if_b[0:4, 1] = f["ml_b_i_2"][0], f["ml_b_f_2"][0]
    vals = {
        "b_mod": column(f["b_mod"]), "norm1_w": column(f["norm1_w"]), "b_bg": column(f["b_branch_gate"]),
        "norm2_w": column(f["norm2_w"]), "conv": conv, "final_norm_w": column(f["final_norm_w"]),
        "norm1_g_2": column(f["norm1_g_2"]), "mu": column(f["rw_mu_2"]), "w0": column(f["rw_w0_2"]),
        "a0": column(f["rw_a0_2"]), "k_k": column(f["rw_k_k_2"]), "k_a": column(f["rw_k_a_2"]),
        "r_k": column(f["rw_r_k_2"]), "gn_w": column(f["rw_gn_w_2"]), "gn_b": column(f["rw_gn_b_2"]), "cqk": cqk,
        "ml_norm": column(f["ml_norm_w_2"]), "gate_b": column(f["gate_b_2"]), "norm2_g": column(f["norm2_g_2"]),
        "dec_pair": np.concatenate([column(np.repeat(d, 64)) for d in (df, db)], axis=1),
        "dec_row": full(np.concatenate([df, db]), 16), "if_b": if_b,
        "eps6": np.full((P, 1), 1e-6), "eps_gn": np.full((P, 1), 64e-5), "eps_ml": np.full((P, 1), 1e-5)}
    cols = np.concatenate([vals[n].reshape(P, -1) for n, _ in COLS], axis=1).astype(np.float32)

    q, s = np.arange(P), np.arange(L)
    inv = (10000.0 ** (-np.arange(16, dtype=np.float32) / 16)).astype(np.float32)
    ang = np.concatenate([(s // 64)[:, None] * inv, (s % 64)[:, None] * inv], axis=1).astype(np.float32)
    cos, sin = np.cos(ang).T, np.sin(ang).T
    cos = np.tile(cos, (4, 1))
    sin = np.tile(np.concatenate([-sin, sin]), (2, 1))
    key = np.stack([q, q + P], axis=1)
    dist = s[None, None, :] - key[:, :, None]
    same = (q[:, None] // 64) == (q[None, :] // 64)
    strict = same & (q[:, None] < q[None, :])
    incl = same & (q[:, None] <= q[None, :])

    def block_mask(b):
        return (q[:, None] // (2 * b) == q[None, :] // (2 * b)) & (q[:, None] % (2 * b) < b) & (q[None, :] % (2 * b) >= b)

    dn = 2 * np.pi * np.outer(q, q) / P
    ln = 2 * np.pi * np.outer(s, s) / L
    scale = 1.0 / np.sqrt(P * L)
    dft_l = np.stack([np.cos(ln), -np.sin(ln)]).reshape(2, 2, P, L).transpose(2, 0, 1, 3)
    sel = np.zeros((P, 4, P))
    for n in range(4):
        sel[n, n] = 1
    pos_ctx = np.stack([np.stack([255 - k] * 8 + [k] * 8, axis=1) for k in key.T], axis=1)
    k1 = {"cosq": cos / 8, "sinq": sin / 8, "cosk": cos, "sink": sin, "dist_f": np.maximum(dist, 0),
          "dist_b": np.maximum(-dist, 0), "mask12": 1 + (dist == 0),
          "dft_d": np.concatenate([np.cos(dn), np.sin(dn)], axis=1) * scale, "dft_l": dft_l,
          "perm": (q[:, None] == (q[None, :] ^ 32)), "pos_ctx": pos_ctx,
          "pos_q": np.broadcast_to(np.concatenate([s + 1, 256 - s])[None], (P, 512))}
    k2 = {"mask4": np.concatenate([strict, incl, strict, incl], axis=1), "m1": block_mask(1).T, "m1t": block_mask(1),
          "levels": np.concatenate([block_mask(b) for b in (2, 4, 8, 16, 32)], axis=1),
          "scan": np.broadcast_to((s % 64 != 0)[None], (P, L)), "causal": dist >= 0, "sel": sel,
          "wa_up": np.concatenate([f["rw_w_up_2"][0], f["rw_a_up_2"][0]]), "g_up": f["rw_g_up_2"][0],
          "w_if": w2[:, 3840:3848].reshape(8, P, 8).transpose(1, 0, 2)}
    kp = {"ident": np.eye(P), "ones": np.ones((P, P)), "bones": same, "iota": np.broadcast_to(q[None], (P, P))}

    def pack(vals, table):
        return np.concatenate([np.asarray(vals[n], np.float32).reshape(P, -1) for n, _ in table], axis=1)

    both = np.stack([f["x"][0], f["ctx"][0]])
    return {
        "stream": stream,
        "xT": both.reshape(2, L, KD, P).transpose(3, 0, 2, 1),
        "cT": np.stack([f["c"][0], f["c_ctx"]]).reshape(2, KD, P).transpose(2, 1, 0),
        "cols": cols, "pconst": pack(kp, PCONST), "const1": pack(k1, CONST1), "const2": pack(k2, CONST2),
        "subk": f["peer_sub_keys_2"][0].reshape(16, P, P).transpose(2, 0, 1).reshape(P, 2048),
        "fg": full(f["final_g_2"], D)}


def kernel(**inputs):
    import concourse.bacc as _bacc
    from concourse import mybir as _mybir
    from concourse.bass_utils import run_bass_kernel_spmd as _run

    nc = _bacc.Bacc("TRN2", target_bir_lowering=False, num_devices=1)
    arrays, t = {}, {}
    for name, a in lay_out(inputs).items():
        a = np.ascontiguousarray(a)
        arrays[f"in_{name}"] = a
        t[name] = nc.dram_tensor(f"in_{name}", a.shape, _mybir.dt.from_np(a.dtype), kind="ExternalInput").ap()
    out = nc.dram_tensor("out_0", (L, D), F32, kind="ExternalOutput").ap()
    build(nc, t, out)
    r = _run(nc, [arrays], core_ids=[0])
    return np.asarray(r.results[0]["out_0"]).reshape(1, L, D)
```

```python
from contextlib import ExitStack

import numpy as np
import concourse.bass as bass
from concourse import mybir

P = 128
D = 1024
KD = D // P
L = 256
RING = 3
LOOP = 6
F32 = mybir.dt.float32
F32R = mybir.dt.float32r
U32 = mybir.dt.uint32
ALU = mybir.AluOpType
ACT = mybir.ActivationFunctionType
AX = mybir.AxisListType.X
EXP_HALF = float(np.exp(-0.5))

PAGES = [("mod", 8), ("q", 2), ("k", 2), ("v", 4), ("g", 4), ("f", 2), ("bg", 8), ("ro", 4), ("fo", 2),
         ("wo", 4), ("up", 22), ("dn", 11), ("lora", 1), ("rkv", 6), ("mqk", 4), ("mv", 2), ("mo", 2),
         ("gt", 8), ("pr", 2), ("pm", 2), ("w2", 4), ("wq", 8), ("peer", 128)]
PAGE = {}
NPAGES = 0
for _name, _n in PAGES:
    PAGE[_name] = NPAGES
    NPAGES += _n

MOD2 = 16
SPLIT0 = PAGE["q"]

TURNS = [("q", 2), ("k", 4), ("v", 8), ("g", 4), ("f", 2), ("bg", 8), ("ro", 4), ("fo", 4), ("wo", 4), ("up", 22),
         ("dn", 4), ("lora", 1), ("rkv", 6), ("mqk", 4), ("mv", 2), ("mo", 2), ("if", 1), ("gt", 8), ("pr", 4),
         ("pm", 4), ("w2", 4), ("wq", 8), ("peer", 128)]
TURN = {}
_t = 0
for _name, _n in TURNS:
    TURN[_name] = _t
    _t += _n

COLS = [("b_mod", 48), ("norm1_w", 8), ("b_bg", 16), ("norm2_w", 8), ("conv", 176), ("final_norm_w", 8),
        ("norm1_g_2", 8), ("mu", 14), ("w0", 4), ("a0", 4), ("k_k", 4), ("k_a", 4), ("r_k", 4), ("gn_w", 4),
        ("gn_b", 4), ("cqk", 40), ("ml_norm", 4), ("gate_b", 16), ("norm2_g", 8), ("dec_pair", 8), ("dec_row", 16),
        ("if_b", 2), ("eps6", 1), ("eps_gn", 1), ("eps_ml", 1)]
COL = {}
NCOLS = 0
for _name, _n in COLS:
    COL[_name] = (NCOLS, _n)
    NCOLS += _n

CONST1 = [("cosq", 256), ("sinq", 256), ("cosk", 256), ("sink", 256), ("dist_f", 512), ("dist_b", 512),
          ("mask12", 512), ("dft_d", 256), ("dft_l", 1024), ("perm", 128), ("pos_ctx", 32), ("pos_q", 512)]
CONST2 = [("mask4", 512), ("m1", 128), ("m1t", 128), ("levels", 640), ("scan", 256), ("causal", 512), ("sel", 512),
          ("wa_up", 512), ("g_up", 512), ("w_if", 64)]


def widths(table):
    at, out = 0, {}
    for name, n in table:
        out[name] = (at, n)
        at += n
    return out, at


C1, N1 = widths(CONST1)
C2, N2 = widths(CONST2)
PCONST = [("ident", 128), ("ones", 128), ("bones", 128), ("iota", 128)]
CP, NP_ = widths(PCONST)

SEMS = """acc_free0 acc_free1 x_in mod_used lo_ready fin_out out_dma c_silu stat1 acc_ready mod2_mm mod2_step mod2_sum
 const1_in decay_exp decay_m ffn_ready gelu_done gated gated_hi x_new mqk_pad const2_in gram_sb p1_mm mt_ready
 places place_no placed hi_ready g_mm row_minus selt_sb piece_used hn_mm hn_sq hn_sqmm xs_sq xs_mm mrow_sb
 pconst_in sq1 mod_cols h_ready perm_mm kw_ready state_mm qk_ready probs scores o_sb out_mm state_sb qdec
 fourier1 four_sb fourier2 z_sb ret_ready mg_ready h_new rows_done uc_mm bc_mm mqk_silu uc_sb m_probs ms_mm
 em_row m_h nd_mm ym_ready lora_tanh lora_mm kk_sq lora_act kk_mm bon_in bon_mm alpha_ready tok_sb tok_mm
 gram_mm x_init l_mm x_sb p1_sb x_mm xa_mm lv_sb u0_mm xa_sb s_sb sa_mm sa_sb ds_mm u0_sb y_mm y_sb y_ready
 xs_root x_in_psum subk_in key_sb key_mm selt_ready selt_mm oh_ready row_hot g_sb a_ready experts_done ach hn_cs
 hn_ln hn_root c_in cols_in lg_ready root1 hraw h_hi wctx_arg wctx w_q part_hi decay_arg conv_mid conv_u
 mqk_conv lf_abs lf_ln mqk_taps m_arg m_exp zs_ready kk_root scan_done w_exp g_arg g_exp row_square fg_in fin_sq
 fin_root dch part_in up_chain xfin a_chain mod2_in0 mod2_in1""".split()


def build(nc, t, out):
    with ExitStack() as ctx:
        S = {n: ctx.enter_context(nc.semaphore(n)) for n in dict.fromkeys(SEMS)}
        loaded = [ctx.enter_context(nc.semaphore(f"page_loaded{i}")) for i in range(RING)]
        acc_free = [S["acc_free0"], S["acc_free1"]]

        B0 = 16512

        def place(name, off, shape, dt=F32):
            return nc.alloc_sbuf_tensor_at(name, [P, *shape], dt, offset=B0 + 4 * off)

        arena = place("arena", 0, [32768])
        xres = place("xres", 32768, [KD, L])
        late = place("late", 32768, [2048])
        late_r = place("late_r", 32768, [2048], F32R)
        h_r = place("h_r", 34816, [2, KD, L], F32R)
        hx = place("hx", 34816, [4096])
        ring = place("ring", 38912, [RING, 2, 8, P])
        piece = place("piece", 45056, [2, 3, 8, P], F32R)
        small = place("small", 51200, [512])
        cols = place("cols", 51712, [NCOLS])
        pc = place("pconst_sb", 52128, [NP_])
        row_more = place("row_more", 52640, [512])
        ps = ctx.enter_context(nc.psum_tensor("ps", [P, 8, 512], F32))

        def at(off, n, base=arena, **kw):
            v = base[:, off:off + n]
            return v.rearrange(kw.pop("r"), **kw) if kw else v

        def col(name, i=0, n=1):
            return cols[:, COL[name][0] + i:COL[name][0] + i + n]

        ident = pc[:, 0:128]
        ones = pc[:, 128:256]
        bones = pc[:, 256:384]
        iota = pc[:, 384:512]

        def c1(name, r=None, **kw):
            v = at(4096 + C1[name][0], C1[name][1])
            return v.rearrange(r, **kw) if r else v

        def c2(name, r=None, **kw):
            v = at(28672 + C2[name][0], C2[name][1])
            return v.rearrange(r, **kw) if r else v

        def w3(off, a, b=L):
            return arena[:, off:off + a * b].rearrange("p (a b) -> p a b", a=a)

        def pair(name, hi, lo, a):
            return place(name + "_hi", hi, [a, L], F32R), place(name + "_lo", lo, [a, L], F32R)

        h = h_r[:, 0], h_r[:, 1]
        h_tmp = w3(12800, 8)
        hctx_r = pair("hctx", 2048, 25088, 8)
        o_r = pair("o", 29184, 18944, 8)
        z_r = pair("z", 17920, 20992, 4)
        mg_r = pair("mg", 22016, 25088, 8)
        ffn_r = pair("ffn", 0, 10752, 22)
        y_r = pair("y", 10752, 12800, 4)
        ym_r = pair("ym", 8192, 9216, 4)
        mg2_r = pair("mg2", 4096, 6144, 8)

        xctx = w3(0, 8)
        sq1 = at(8704, 4096).rearrange("p (k n) -> p k n", k=8)
        gates = w3(8704, 16)
        sg = w3(12800, 8)
        v_tok = w3(14848, 2, 1024)
        qraw = w3(16896, 8)
        qk = w3(18944, 8)
        kc_tok = w3(20992, 2, 512)
        vc_tok = w3(22016, 2, 1024)
        fT = w3(24064, 4)
        oT = w3(25088, 8)
        decay = w3(27136, 2, 512)
        probs = w3(28160, 2, 512)
        qdec = w3(29184, 8)
        st_f = at(31232, 512)
        st_b = at(31744, 512)
        rs1 = at(32256, 512)
        kw_f = w3(0, 2, 512)
        kw_b = w3(1024, 2, 512)
        four_a = w3(2048, 8)
        zT = w3(16896, 4)
        mg = w3(14848, 8)
        sq_o = w3(29184, 8)
        sq = w3(8704, 8)
        uav = w3(27136, 4)
        ga = w3(28160, 2)
        ffn_t = at(16384, 256)
        mrow = at(14848, 2048)
        mod_w = [at(off, 2048) for off in (8704, 10752, 2048, 25088)]
        mod_sum = at(27136, 2048)
        zraw = w3(0, 14)
        zs = w3(3584, 14)
        zd = w3(7168, 14)
        mqk_raw = w3(10752, 8, 259)
        mqk = w3(12832, 8)
        mv_tok = w3(14880, 2, 512)
        so = w3(15904, 4)
        gates2 = w3(16928, 16)
        gT = w3(0, 4)
        bon = w3(1024, 4)
        lw = w3(2048, 4)
        kk = w3(7168, 4)
        cum = w3(8192, 4)
        wcum = w3(9216, 4)
        winv = w3(10752, 4)
        wprev = w3(11776, 4)
        bT = w3(12800, 4)
        aT = w3(13824, 4)
        atok = w3(14848, 2, 512)
        ar = at(21024, 2048).rearrange("p (j i a n) -> p j i a n", j=4, i=2, a=2)
        beta = w3(23072, 4)
        kappa = w3(24096, 4)
        btok = w3(25120, 2, 512)
        ktok = w3(26144, 2, 512)
        vtok = w3(27168, 2, 512)
        gram = at(2048, 8192).rearrange("p (n a s) -> p n a s", n=16, a=4)
        mt = at(10752, 2048).rearrange("p (n s) -> p n s", n=16)
        sa = w3(12800, 2, 512)
        yT = w3(13824, 4)
        states = at(23072, 1280).rearrange("p (n j v) -> p n j v", n=5, j=4)
        rw_tmp = w3(11776, 4)
        mg2 = w3(2048, 8)
        Xn = at(0, 2048, hx).rearrange("p (n s) -> p n s", n=16)
        XT = at(2048, 2048, hx).rearrange("p (n s) -> p n s", n=16)
        P1 = [at(off, 512).rearrange("p (n s) -> p n s", n=4) for off in (10240, 24352)]
        U0 = at(10752, 1024).rearrange("p (i n) -> p i n", i=2)
        ltmp = w3(23072, 4)
        xat = at(0, 1024, hx).rearrange("p (j i n) -> p j i n", j=4, i=2)
        lv = at(1024, 1024, hx).rearrange("p (i n) -> p i n", i=2)
        m_rows = at(21024, 2048).rearrange("p (r n) -> p r n", r=8)
        m_bc = w3(23072, 4, 512)
        m_e = w3(25120, 2, 512)
        m_p = w3(26144, 2, 512)
        m_dn = w3(27168, 4)
        qP = w3(4096, 16)
        s_sb = at(8192, 4096).rearrange("p (t g n) -> p t g n", t=2, g=16)
        topv = at(12288, 512).rearrange("p (t g n) -> p t g n", t=2, g=16)
        topi = at(12800, 512).rearrange("p (t g n) -> p t g n", t=2, g=16)
        topf = at(13312, 512).rearrange("p (t g n) -> p t g n", t=2, g=16)
        cand = at(13824, 4096).rearrange("p (t g n) -> p t g n", t=2, g=8)
        best = at(17920, 256).rearrange("p (t g n) -> p t g n", t=2, g=8)
        posi = at(18176, 256).rearrange("p (t g n) -> p t g n", t=2, g=8)
        place_i = at(18432, 64).rearrange("p (c t n) -> p c t n", c=2, t=2).bitcast(U32)
        place_eq = [at(off, 1024).rearrange("p (a k j) -> p a k j", a=4, k=16) for off in (19456, 20480)]
        place_f = at(18496, 64).rearrange("p (c t n) -> p c t n", c=2, t=2)
        eqb = at(19456, 2048)
        selv = at(21504, 768).rearrange("p (t c n) -> p t c n", t=2, c=3)
        gsm = at(22272, 64)
        subk = at(28672, 2048).rearrange("p (g n) -> p g n", g=16)
        G = arena[:, 0:32768].rearrange("p (e n) -> p e n", e=128)
        selT = at(0, 768, late).rearrange("p (c n) -> p c n", c=3)
        row_hot = [v.rearrange("p (n e) -> p n e", n=4) for v in (at(768, 512, late), at(1280, 512, late), row_more, small)]
        gate_banks = (6, 7, 0, 1)
        col_hot = [v.rearrange("p (n e) -> p n e", n=2) for v in (at(1792, 256, late), cols[:, 0:256],
                                                                  pc[:, 0:256])]
        col_hot = [[v[:, 0], v[:, 1]] for v in col_hot] + [[cols[:, 256:384], pc[:, 256:384]]]
        gelu_t = at(0, 512, late).rearrange("p (b n) -> p b n", b=2)
        a_r = late_r[:, 768:1792].rearrange("p (c b n) -> p c b n", c=2, b=2)
        fin = at(0, 2048)

        mod = small[:, 0:96].rearrange("p (m c) -> p m c", c=2)
        csil = small[:, 96:112].rearrange("p (k c) -> p k c", c=2)
        gain = small[:, 112:128].rearrange("p (k c) -> p k c", c=2)
        lgpair = small[:, 128:136]
        lgrow = small[:, 136:152]
        wctx = small[:, 152:184].rearrange("p (t n) -> p t n", t=2)
        gain2 = small[:, 184:192]
        wend = small[:, 192:208].rearrange("p (j c) -> p j c", j=4)
        ucol = small[:, 208:216]
        ar2 = at(21024, 2048).rearrange("p (m a n) -> p m a n", m=8, a=2)
        lora_in = w3(24096, 2)
        m_sq = w3(23072, 4)
        fgrow = at(3072, 1024)
        fstat = small[:, 216:224]
        rs = small[:, 256:512]
        eps6, eps_gn, eps_ml = col("eps6"), col("eps_gn"), col("eps_ml")

        block = ctx.enter_context(nc.Block())

        @block.sync
        def _(sp):
            def page(p, i=0):
                sp.dma_start(ring[:, p % RING], t["stream"][p + RING * i]).then_inc(loaded[p % RING], 16)

            page(0)
            page(1)
            sp.dma_start(xres[:], t["xT"][:, 0]).then_inc(S["x_in"], 16)
            sp.dma_start(xctx, t["xT"][:, 1]).then_inc(S["x_in"], 16)
            page(2)
            for p in range(RING, SPLIT0 + RING):
                sp.wait_ge(S["mod_used"], p - RING + 1)
                page(p)
            rounds = (NPAGES - SPLIT0) // RING - 1
            with sp.Fori(0, rounds) as i:
                for u in range(RING):
                    sp.wait_ge(S["lo_ready"], 2 * RING * i + (2 * u + 2))
                    page(SPLIT0 + RING + u, i)
            for p in range(SPLIT0 + RING + RING * rounds, NPAGES):
                sp.wait_ge(S["lo_ready"], 2 * (p - SPLIT0 - RING) + 2)
                page(p)

            for tt in range(2):
                sp.wait_ge(S["fin_out"], tt + 1)
                sp.dma_start(out[tt * P:(tt + 1) * P, :], fin[:, tt * 1024:(tt + 1) * 1024]).then_inc(S["out_dma"], 16)
            sp.wait_ge(S["out_dma"], 32)

        @block.gpsimd
        def _(pool):
            g = nc.gpsimd
            def mod_page(b, n):
                pool.dma_start(mod_w[b], t["mod2"][n]).then_inc(S[("mod2_in0", "mod2_in1")[b % 2]], 16)

            pool.wait_ge(S["c_silu"], 1)
            for half in range(2):
                if half == 0:
                    pool.wait_ge(S["stat1"], 1)
                else:
                    pool.wait_ge(S["acc_ready"], TURN["v"] + 8)
                for b in range(2):
                    mod_page(2 * half + b, 8 * half + b)
                if half == 1:
                    pool.wait_ge(S["mod2_mm"], 1)
                for n in range(8):
                    b = 2 * half + n % 2
                    pool.wait_ge(S[("mod2_in0", "mod2_in1")[n % 2]], 16 * (4 * half + n // 2 + 1))
                    w = mod_w[b].rearrange("p (k n) -> p k n", k=8)
                    steps = 4 * (8 * half + n)
                    g.tensor_tensor(w, w, csil[:, :, 0:1].to_broadcast([P, 8, L]), ALU.mult).then_inc(S["mod2_step"], 1)
                    for s, k in enumerate((4, 2, 1)):
                        pool.wait_ge(S["mod2_step"], steps + s + 1)
                        dst = mod_sum[:, n * L:(n + 1) * L].unsqueeze(1) if k == 1 else w[:, 0:k, :]
                        ins = g.tensor_tensor(dst, w[:, 0:k, :], w[:, k:2 * k, :], ALU.add)
                        ins.then_inc(S["mod2_step" if k > 1 else "mod2_sum"], 1)
                    pool.wait_ge(S["mod2_sum"], 8 * half + n + 1)
                    g.engine_nop().then_inc(S["mod2_step"], 1)
                    if n < 6:
                        mod_page(b, 8 * half + n + 2)
            pool.wait_ge(S["const1_in"], 16)
            for hh in range(8):
                pool.wait_ge(S["decay_exp"], hh + 1)
                g.tensor_tensor(decay[:, hh % 2], decay[:, hh % 2], c1("mask12"), ALU.mult).then_inc(S["decay_m"], 1)
            g.engine_nop().then_inc(S["ffn_ready"], 2)

            def gated_page(u, i=0):
                T, b = TURN["up"] + u, u % 2
                n = LOOP * i + u
                v = uav[:, 2 * b + 1, :]
                pool.wait_ge(S["gelu_done"], n + 1)
                pool.wait_ge(acc_free[T % 2], T // 2 + 1 + LOOP // 2 * i)
                g.tensor_tensor(v, ga[:, b, :], v, ALU.mult).then_inc(S["gated"], 1)
                pool.wait_ge(S["gated_hi"], n + 1)
                hi, lo = (ffn_r[q][:, bass.ds(n, 1), :].rearrange("p a n -> p (a n)") for q in range(2))
                g.tensor_tensor(lo, v, hi.bitcast(F32), ALU.subtract).then_inc(S["ffn_ready"], 1)

            with pool.Fori(0, 3) as i:
                for u in range(LOOP):
                    gated_page(u, i)
            for u in range(18, 22):
                gated_page(u)
            pool.wait_ge(S["x_new"], 2)
            g.memset(mqk_raw[:, :, 0:3], 0.0).then_inc(S["mqk_pad"], 1)
            pool.wait_ge(S["const2_in"], 16)
            pool.wait_ge(S["gram_sb"], 16)
            for lev in range(5):
                m = c2("levels")[:, lev * P:(lev + 1) * P].unsqueeze(1).to_broadcast([P, 4, P])
                for gr in range(4):
                    if lev:
                        pool.wait_ge(S["p1_mm"], 4 * (lev - 1) + gr + 1)
                    g.tensor_tensor(mt[:, 4 * gr:4 * gr + 4, :], gram[:, 4 * gr:4 * gr + 4, 0, :], m,
                                    ALU.mult).then_inc(S["mt_ready"], 1)
            def number(hh):
                pool.wait_ge(S["places"], hh + 1)
                e4 = [place_eq[hh % 2][:, 2 * c:2 * c + 2] for c in range(2)]
                for c in range(2):
                    g.tensor_tensor(e4[c], e4[c], topf[:, :, 2 * hh + c, :].unsqueeze(2).to_broadcast([P, 2, 16, 16]),
                                    ALU.mult).then_inc(S["place_no"], 1)
                e, steps = place_eq[hh % 2], 5 * hh + 2
                for m in (8, 4, 2):
                    pool.wait_ge(S["place_no"], steps)
                    g.tensor_tensor(e[:, :, :, 0:m], e[:, :, :, 0:m], e[:, :, :, m:2 * m], ALU.add).then_inc(S["place_no"], 1)
                    steps += 1
                pool.wait_ge(S["place_no"], steps)
                for c in range(2):
                    ins = g.tensor_tensor(selv[:, :, c, 16 * hh:16 * hh + 16], e4[c][:, :, :, 0], e4[c][:, :, :, 1], ALU.add)
                ins.then_inc(S["placed"], 1)
                pool.wait_ge(S["placed"], hh + 1)

            for u in range(8):
                for c in range(2 * (PAGE["wq"] + u + 1 - SPLIT0), 2 * (PAGE["wq"] + u + 2 - SPLIT0)):
                    pool.wait_ge(S["hi_ready"], c + 1)
                    g.tensor_tensor(piece[:, 1, c % 3], ring[:, (PAGE["wq"] + u + 1) % RING, c % 2],
                                    piece[:, 0, c % 3].bitcast(F32), ALU.subtract).then_inc(S["lo_ready"], 1)
                if u >= 2:
                    number(u - 2)
            number(6)
            number(7)

            def row_minus(i):
                for b in range(4):
                    if not isinstance(i, int):
                        pool.wait_ge(S["g_mm"], 8 * i + (2 * b - 6))
                    g.tensor_tensor(row_hot[b][:, 0:3], iota.unsqueeze(1).to_broadcast([P, 3, P]),
                                    selT[:, 0, bass.ds(16 * i + 4 * b, 3)].unsqueeze(2).to_broadcast([P, 3, P]),
                                    ALU.subtract).then_inc(S["row_minus"], 1)

            pool.wait_ge(S["selt_sb"], 2)
            row_minus(0)
            with pool.Fori(1, L // 16) as i:
                row_minus(i)

        @block.tensor
        def _(pe):
            def piece_of(p):
                return 2 * (p - SPLIT0)

            def three(o, a, b, start, stop, skip=False):
                m = mm(o, a[1], b[0], start=start, stop=False, skip_group_check=skip)
                mm(o, a[0], b[0], start=False, stop=False, skip_group_check=skip)
                mm(o, a[0], b[1], start=False, stop=stop, skip_group_check=skip)
                return m, mm_last[0]

            mm_last = [None]

            def mm(*args, **kw):
                mm_last[0] = nc.tensor.matmul(*args, **kw)
                return mm_last[0]

            def part(c, k):
                return piece[:, 0, c % 3, k, :], piece[:, 1, c % 3, k, :]

            def piece_in(c, i=0):
                pe.wait_ge(S["lo_ready"], c + 1 + 2 * LOOP * i)

            def turn(T, i=0):
                v = T // 2 + LOOP // 2 * i
                if not (isinstance(v, int) and v <= 0):
                    pe.wait_ge(acc_free[T % 2], v)

            def wide(p, T, rhs, ctx):
                turn(T)
                if ctx:
                    turn(T + 1)
                for s in range(2):
                    c = piece_of(p) + s
                    piece_in(c)
                    w = [piece[:, q, c % 3].rearrange("p k m -> p (k m)").rearrange("p (k m) -> p k m", k=4) for q in range(2)]
                    for b, lhs in enumerate((h, hctx_r)[:1 + ctx]):
                        for e in range(2):
                            half = slice(e * P, (e + 1) * P)
                            for kk in range(4):
                                k = 4 * s + kk
                                if b == 0 and rhs:
                                    a, m_ = [w[q][:, kk, half] for q in range(2)], [rhs[q][:, k, :] for q in range(2)]
                                else:
                                    a, m_ = [lhs[q][:, k, half] for q in range(2)], [w[q][:, kk, :] for q in range(2)]
                                first, last = three(ps[:, (T + b) % 2, e * L:(e + 1) * L], a, m_, k == 0 and e == 0, k == 7,
                                                    True)
                                if b == 0 and e == 0 and kk == 0:
                                    first.then_inc(S["piece_used"], 1)
                        if s == 1:
                            last.then_inc(S["acc_ready"], 1)

            def fm_piece(c, o, rhs, i=0):
                piece_in(c, i)
                for k in range(8):
                    first, last = three(o, part(c, k), (rhs[0][:, k, :], rhs[1][:, k, :]), k == 0, k == 7)
                    if k == 0:
                        first.then_inc(S["piece_used"], 1)
                return last

            def fm_page(p, T, rhs, i=0):
                turn(T, i)
                for s in range(2):
                    last = fm_piece(piece_of(p) + s, ps[:, T % 2, s * L:(s + 1) * L], rhs, i)
                last.then_inc(S["acc_ready"], 1)

            def fm_pages(name, n, rhs):
                rounds = n // LOOP if n >= 2 * LOOP else 0
                if rounds:
                    with pe.Fori(0, rounds) as i:
                        for u in range(LOOP):
                            fm_page(PAGE[name] + u, TURN[name] + u, rhs, i)
                for u in range(LOOP * rounds, n):
                    fm_page(PAGE[name] + u, TURN[name] + u, rhs)

            def packed(name, T, K, rhs, tiles=8):
                for n in range(tiles * K):
                    c, tile, k = piece_of(PAGE[name]) + n // 8, n // K, n % K
                    if n % 8 == 0:
                        piece_in(c)
                    if tile % 2 == 0 and k == 0:
                        turn(T + tile // 2)
                    first, last = three(ps[:, (T + tile // 2) % 2, (tile % 2) * L:(tile % 2 + 1) * L], part(c, n % 8),
                                        (rhs[0][:, k, :], rhs[1][:, k, :]), k == 0, k == K - 1)
                    if n % 8 == 0:
                        first.then_inc(S["piece_used"], 1)
                    if tile % 2 == 1 and k == K - 1:
                        last.then_inc(S["acc_ready"], 1)

            def head_norm(src, sqb, pairs, weights, base, banks):
                for q in range(pairs):
                    mm(ps[:, banks[q], :], weights, src[:, 2 * q:2 * q + 2, :], start=True,
                       stop=True).then_inc(S["hn_mm"], 1)
                for q in range(pairs):
                    pe.wait_ge(S["hn_sq"], base + q + 1)
                    mm(ps[:, banks[pairs + q], :], weights, sqb[:, 2 * q:2 * q + 2, :], start=True,
                       stop=True).then_inc(S["hn_sqmm"], 1)

            def x_norm(n):
                pe.wait_ge(S["xs_sq"], n + 1)
                for k in range(8):
                    m = mm(ps[:, 2, 0:L], ones, sq[:, k, :], start=k == 0, stop=k == 7)
                m.then_inc(S["xs_mm"], 1)

            def mod_columns(g):
                pe.wait_ge(S["mrow_sb"], g + 1)
                for j in range(4 * g, 4 * g + 4):
                    m = nc.tensor.transpose(ps[:, 2, 2 * j:2 * j + 2], mrow[0:2, j * P:(j + 1) * P], ident[0:2, 0:2])
                return m

            pe.wait_ge(S["c_silu"], 1)
            for g in range(4):
                for q in range(2):
                    p = 2 * g + q
                    pe.wait_ge(loaded[p % RING], 16 * (p // RING + 1))
                    for k in range(4):
                        m = mm(ps[0:2, 4 + g, :], csil[:, 4 * q + k, :], ring[:, p % RING, k // 2, 4 * (k % 2):4 * (k % 2) + 4, :],
                               start=p % 2 == 0 and k == 0, stop=q == 1 and k == 3)
                    m.then_inc(S["mod_used"], 1)
                if g == 1:
                    pe.wait_ge(S["pconst_in"], 16)
                    pe.wait_ge(S["sq1"], 2)
                    for k in range(8):
                        m = mm(ps[:, 3, :], ones, sq1[:, k, :], start=k == 0, stop=k == 7)
                    m.then_inc(S["stat1"], 1)
                if g > 1:
                    mod_columns(g - 2)
            mod_columns(2)
            mod_columns(3).then_inc(S["mod_cols"], 1)

            def late_columns(half):
                pe.wait_ge(S["mod2_sum"], 8 * (half + 1))
                b, c = ((2, 32), (7, 0))[half]
                for j in range(16):
                    m = mm(ps[:, b, c + j:c + j + 1], mod_sum[:, j * P:(j + 1) * P], ones[:, 0:1], start=True, stop=True)
                m.then_inc(S["mod2_mm"], 1)

            pe.wait_ge(S["h_ready"], 8)
            fm_pages("q", 2, h)
            pe.wait_ge(S["h_ready"], 16)
            for u in range(2):
                wide(PAGE["k"] + u, TURN["k"] + 2 * u, h, True)
            for u in range(4):
                wide(PAGE["v"] + u, TURN["v"] + 2 * u, None, True)
            fm_pages("g", 4, h)
            late_columns(0)
            fm_pages("f", 2, h)
            pe.wait_ge(S["const1_in"], 16)
            for q in range(4):
                mm(ps[:, 4 + q, :], c1("perm"), qraw[:, 2 * q:2 * q + 2, :], start=True,
                   stop=True).then_inc(S["perm_mm"], 1)
            pe.wait_ge(S["kw_ready"], 1)
            for d, kw in enumerate((kw_f, kw_b)):
                for hh in range(8):
                    r, j = (hh % 2) * 64, hh // 2
                    for tt in range(2):
                        m = mm(ps[r:r + 64, 2 + d, j * P:(j + 1) * P], kw[:, tt, hh * 64:(hh + 1) * 64],
                               vc_tok[:, tt, hh * P:(hh + 1) * P], start=tt == 0, stop=tt == 1)
                m.then_inc(S["state_mm"], 1)
            for u in range(8):
                if u == 7:
                    pe.wait_ge(S["qk_ready"], 4)
                    late_columns(1)
                fm_page(PAGE["bg"] + u, TURN["bg"] + u, h)

            def scores(n):
                r, j = (n % 2) * 64, n // 2
                if n >= 2:
                    pe.wait_ge(S["probs"], n - 1)
                for st in range(2):
                    m = mm(ps[:, 4 + n % 2, st * L:(st + 1) * L], qk[r:r + 64, 4 + j, st * P:(st + 1) * P],
                           qk[r:r + 64, j, :], start=True, stop=True)
                m.then_inc(S["scores"], 1)

            def outputs(n):
                r, j = (n % 2) * 64, n // 2
                pe.wait_ge(S["probs"], n + 1)
                if n >= 2:
                    pe.wait_ge(S["o_sb"], n - 1)
                o = ps[:, 6 + n % 2, 0:L]
                for st in range(2):
                    mm(o, v_tok[:, st, n * P:(n + 1) * P], probs[:, n % 2, st * L:(st + 1) * L], start=st == 0,
                       stop=False)
                mm(o, st_f[r:r + 64, j * P:(j + 1) * P], qdec[r:r + 64, j, :], start=False, stop=False)
                mm(o, st_b[r:r + 64, j * P:(j + 1) * P], qdec[r:r + 64, 4 + j, :], start=False,
                   stop=True).then_inc(S["out_mm"], 1)

            pe.wait_ge(S["qk_ready"], 4)
            scores(0)
            pe.wait_ge(S["state_sb"], 2)
            pe.wait_ge(S["qdec"], 2)
            for n in range(8):
                if n < 7:
                    scores(n + 1)
                outputs(n)

            for n in range(8):
                b = (2, 3, 4, 5)[n // 2]
                if n % 2 == 0 and b == 5:
                    pe.wait_ge(S["probs"], 8)
                m = mm(ps[:, b, (n % 2) * L:(n % 2 + 1) * L], fT[:, n // 2, (n % 2) * P:(n % 2 + 1) * P], c1("dft_d"),
                       start=True, stop=True)
                if n % 2 == 1:
                    m.then_inc(S["fourier1"], 1)
            pe.wait_ge(S["o_sb"], 8)
            pe.wait_ge(S["four_sb"], 4)
            dft_l = c1("dft_l", "p (c t n) -> p c t n", c=2, t=2)
            for gi in range(4):
                n = 0
                for lt in range(2):
                    for c in range(2):
                        m = mm(ps[:, 6 + gi // 2, (gi % 2) * L:(gi % 2 + 1) * L],
                               four_a[:, 2 * gi + lt, c * P:(c + 1) * P], dft_l[:, c, lt, :], start=n == 0, stop=n == 3)
                        n += 1
                if gi % 2 == 1:
                    m.then_inc(S["fourier2"], 1)
            for q in range(4):
                mm(ps[:, 2 + q, :], ones, oT[:, 2 * q:2 * q + 2, :], start=True, stop=True).then_inc(S["hn_mm"], 1)
            pe.wait_ge(S["z_sb"], 2)
            for q in range(4):
                pe.wait_ge(S["hn_sq"], q + 1)
                mm(ps[:, (6, 7, 2, 3)[q], :], ones, sq_o[:, 2 * q:2 * q + 2, :], start=True,
                   stop=True).then_inc(S["hn_sqmm"], 1)
            pe.wait_ge(S["ret_ready"], 1)
            fm_pages("ro", 4, o_r)
            packed("fo", TURN["fo"], 4, z_r)
            pe.wait_ge(S["mg_ready"], 1)
            fm_pages("wo", 4, mg_r)
            x_norm(0)
            pe.wait_ge(S["h_new"], 8)
            fm_pages("up", 22, h)
            pe.wait_ge(S["ffn_ready"], 24)
            packed("dn", TURN["dn"], 22, ffn_r)
            x_norm(1)
            x_norm(2)
            pe.wait_ge(S["h_new"], 16)
            fm_pages("lora", 1, h)
            fm_pages("rkv", 6, h)
            fm_pages("mqk", 4, h)
            for u in range(2):
                wide(PAGE["mv"] + u, TURN["mv"] + u, None, False)
            fm_pages("mo", 2, h)
            pe.wait_ge(S["const2_in"], 16)
            T = TURN["if"]
            turn(T)
            w_if = c2("w_if", "p (k c) -> p k c", k=8)
            for c in range(2):
                for k in range(16):
                    m = mm(ps[0:4, T % 2, c * L:(c + 1) * L], w_if[:, k % 8, 4 * c:4 * c + 4], h[k // 8][:, k % 8, :].bitcast(F32),
                           start=k == 0, stop=k == 15)
            m.then_inc(S["acc_ready"], 1)

            def gate_page(u):
                fm_page(PAGE["gt"] + u, TURN["gt"] + u, h)

            gate_page(0)
            gate_page(1)

            pe.wait_ge(S["rows_done"], 2)
            for tt in range(2):
                m = nc.tensor.transpose(ps[:, 2, 4 * tt:4 * tt + 4], m_rows[0:4, 4, tt * P:(tt + 1) * P], ident[0:4, 0:4])
            m.then_inc(S["uc_mm"], 1)
            for n in range(4):
                mm(ps[:, 4 + n, :], c2("sel")[0:4, n * P:(n + 1) * P], m_rows[0:4, 5:7, :], start=True,
                   stop=True).then_inc(S["bc_mm"], 1)
            gate_page(2)
            pe.wait_ge(S["mqk_silu"], 8)
            pe.wait_ge(S["uc_sb"], 1)

            def m_scores(n):
                if n >= 2:
                    pe.wait_ge(S["m_probs"], n - 1)
                for st in range(2):
                    m = mm(ps[:, 2 + n % 2, st * L:(st + 1) * L], mqk[:, 4 + n, st * P:(st + 1) * P], mqk[:, n, :],
                           start=True, stop=True)
                m.then_inc(S["ms_mm"], 1)

            m_scores(0)
            pe.wait_ge(S["em_row"], 4)
            for n in range(4):
                if n < 3:
                    m_scores(n + 1)
                pe.wait_ge(S["m_probs"], n + 1)
                if n >= 2:
                    pe.wait_ge(S["m_h"], n - 1)
                for st in range(2):
                    mm(ps[:, 4 + n % 2, 0:L], mv_tok[:, st, n * P:(n + 1) * P], m_p[:, n % 2, st * L:(st + 1) * L],
                       start=st == 0, stop=st == 1)
                for st in range(2):
                    m = mm(ps[:, 4 + n % 2, L:2 * L], ones, m_p[:, n % 2, st * L:(st + 1) * L], start=st == 0,
                           stop=st == 1)
                m.then_inc(S["nd_mm"], 1)
            gate_page(3)
            pe.wait_ge(S["m_h"], 4)
            head_norm(m_dn, m_sq, 2, ones, 4, (6, 7, 2, 3))

            gate_page(4)
            pe.wait_ge(S["ym_ready"], 1)
            pe.wait_ge(S["lora_tanh"], 2)
            wa_up, g_up = c2("wa_up"), c2("g_up")
            for q in range(6):
                for e in range(2):
                    m_ = (2 * q + e) % 4
                    o = ps[:, 2 + q, e * L:(e + 1) * L]
                    if q < 2:
                        m = mm(o, wa_up[0:64, m_ * P:(m_ + 1) * P], lora_in[0:64, 0, :], start=True, stop=True)
                    elif q < 4:
                        m = mm(o, wa_up[64:128, m_ * P:(m_ + 1) * P], zs[64:128, 12, :], start=True, stop=True)
                    else:
                        m = mm(o, g_up[:, m_ * P:(m_ + 1) * P], lora_in[:, 1, :], start=True, stop=True)
                m.then_inc(S["lora_mm"], 1)
            gate_page(5)
            pe.wait_ge(S["kk_sq"], 1)
            pe.wait_ge(S["lora_act"], 4)
            for q in range(2):
                mm(ps[:, 2 + q, :], bones, ltmp[:, 2 * q:2 * q + 2, :], start=True, stop=True).then_inc(S["kk_mm"], 1)
            gate_page(6)
            pe.wait_ge(S["bon_in"], 1)
            pe.wait_ge(S["lora_act"], 12)
            for q in range(2):
                mm(ps[:, 4 + q, :], bones, bon[:, 2 * q:2 * q + 2, :], start=True, stop=True).then_inc(S["bon_mm"], 1)
            gate_page(7)
            pe.wait_ge(S["alpha_ready"], 1)
            for n in range(8):
                src, i = n // 2, n % 2
                if n >= 6:
                    pe.wait_ge(S["tok_sb"], n - 5)
                for j in range(4):
                    sl = slice(i * P, (i + 1) * P)
                    s_ = (ar[:, j, i, 0, :], beta[:, j, sl], kappa[:, j, sl], zs[:, 8 + j, sl])[src]
                    m = nc.tensor.transpose(ps[:, 2 + n % 6, j * P:(j + 1) * P], s_, ident)
                m.then_inc(S["tok_mm"], 1)
            pe.wait_ge(S["tok_sb"], 8)
            for n in range(16):
                i, hh = n // 8, n % 8
                r, j = (hh % 2) * 64, hh // 2
                sl = slice(i * P, (i + 1) * P)
                if n >= 4:
                    pe.wait_ge(S["gram_sb"], n - 3)
                o = ps[:, 2 + n % 4, :]
                mm(o[:, 0:256], beta[r:r + 64, j, sl], ar[r:r + 64, j, i, :, :], start=True, stop=True)
                mm(o[:, 256:512], kappa[r:r + 64, j, sl], ar[r:r + 64, j, i, :, :], start=True,
                   stop=True).then_inc(S["gram_mm"], 1)
                if n % 4 == 0 and n >= 4:
                    pe.wait_ge(S["x_init"], n // 4)
                c = n // 2 % 2
                m = mm(ps[:, 6 + n % 2, c * P:(c + 1) * P], ar[r:r + 64, j, i, 0, :], beta[r:r + 64, j, sl], start=True,
                       stop=True)
                if n % 4 == 3:
                    m.then_inc(S["l_mm"], 1)
            pe.wait_ge(S["x_init"], 4)

            def first_product(q):
                g4 = 4 * (q % 4)
                pe.wait_ge(S["mt_ready"], q + 1)
                if q >= 4:
                    pe.wait_ge(S["x_sb"], q - 3)
                if q >= 2:
                    pe.wait_ge(S["p1_sb"], q - 1)
                for e in range(4):
                    m = mm(ps[:, 2 + q % 2, e * P:(e + 1) * P], mt[:, g4 + e, :], Xn[:, g4 + e, :], start=True, stop=True)
                m.then_inc(S["p1_mm"], 1)

            first_product(0)
            for q in range(20):
                if q < 19:
                    first_product(q + 1)
                g4 = 4 * (q % 4)
                pe.wait_ge(S["p1_sb"], q + 1)
                if q >= 2:
                    pe.wait_ge(S["x_sb"], q - 1)
                for e in range(4):
                    if q < 16:
                        mm(ps[:, 4 + q % 2, e * P:(e + 1) * P], XT[:, g4 + e, :], P1[q % 2][:, e, :], start=True, stop=True)
                    m = mm(ps[:, 6 + q % 2, e * P:(e + 1) * P], P1[q % 2][:, e, :], XT[:, g4 + e, :], start=True, stop=True)
                m.then_inc(S["x_mm"], 1)
            pe.wait_ge(S["x_sb"], 20)
            for i in range(2):
                for hh in range(8):
                    r, j, n = (hh % 2) * 64, hh // 2, 8 * i + hh
                    m = mm(ps[r:r + 64, 2 + i, j * P:(j + 1) * P], atok[:, i, hh * 64:(hh + 1) * 64], XT[:, n, :],
                           start=True, stop=True)
                m.then_inc(S["xa_mm"], 1)
            for i in range(2):
                for hh in range(8):
                    m = mm(ps[:, 4 + i, hh * 64:(hh + 1) * 64], gram[:, 8 * i + hh, 2, :], vtok[:, i, hh * 64:(hh + 1) * 64],
                           start=True, stop=True)
                m.then_inc(S["xa_mm"], 1)
            for i in range(2):
                pe.wait_ge(S["lv_sb"], i + 1)
                for hh in range(8):
                    m = mm(ps[:, 6 + i, hh * 64:(hh + 1) * 64], XT[:, 8 * i + hh, :], lv[:, i, hh * 64:(hh + 1) * 64],
                           start=True, stop=True)
                m.then_inc(S["u0_mm"], 1)
            pe.wait_ge(S["xa_sb"], 2)
            pe.wait_ge(S["lv_sb"], 2)
            for n in range(4):
                i, r0 = n // 2, (n % 2) * 64
                pe.wait_ge(S["s_sb"], n + 1)
                for hh in range(8):
                    r, j = (hh % 2) * 64, hh // 2
                    c = 256 * (n % 2) + 64 * j
                    m = mm(ps[r0:r0 + 64, 2 + hh % 2, c:c + 64], xat[r:r + 64, j, i, r0:r0 + 64],
                           states[r:r + 64, n, j, :], start=True, stop=True)
                m.then_inc(S["sa_mm"], 1)
                pe.wait_ge(S["sa_sb"], n + 1)
                if n == 3:
                    break
                for hh in range(8):
                    r, j, c = (hh % 2) * 64, hh // 2, slice(hh * 64, (hh + 1) * 64)
                    o = ps[r:r + 64, 4 + n % 2, j * 64:(j + 1) * 64]
                    mm(o, btok[r0:r0 + 64, i, c], sa[r0:r0 + 64, i, c], start=True, stop=False)
                    m = mm(o, ktok[r0:r0 + 64, i, c], vtok[r0:r0 + 64, i, c], start=False, stop=True)
                m.then_inc(S["ds_mm"], 1)
            pe.wait_ge(S["u0_sb"], 2)
            for i in range(2):
                for hh in range(8):
                    r, j, c, n = (hh % 2) * 64, hh // 2, slice(hh * 64, (hh + 1) * 64), 8 * i + hh
                    o = ps[r:r + 64, 6 + i, j * P:(j + 1) * P]
                    mm(o, sa[:, i, c], gram[:, n, 1, :], start=True, stop=False)
                    mm(o, vtok[:, i, c], gram[:, n, 3, :], start=False, stop=False)
                    for e in range(2):
                        m = mm(o[:, e * 64:(e + 1) * 64], states[r:r + 64, 2 * i + e, j, :],
                               ar[r:r + 64, j, i, 1, e * 64:(e + 1) * 64], start=False, stop=e == 1)
                m.then_inc(S["y_mm"], 1)
            pe.wait_ge(S["y_sb"], 2)
            head_norm(yT, rw_tmp, 2, bones, 6, (2, 3, 4, 5))
            pe.wait_ge(S["y_ready"], 1)
            packed("pr", TURN["pr"], 4, y_r)
            pe.wait_ge(S["y_ready"], 2)
            packed("pm", TURN["pm"], 4, ym_r)
            pe.wait_ge(S["mg_ready"], 2)
            fm_pages("w2", 4, mg2_r)
            x_norm(3)
            pe.wait_ge(S["xs_root"], 4)
            for n in range(4):
                for k in range(4):
                    m = mm(ps[:, 2 + n, k * P:(k + 1) * P], xres[:, 4 * (n % 2) + k, (n // 2) * P:(n // 2 + 1) * P], ident,
                           start=k == 0, stop=False, skip_group_check=True)
            m.then_inc(S["x_in_psum"], 1)
            pe.wait_ge(S["h_new"], 24)

            pe.wait_ge(S["subk_in"], 16)

            def key_scores(n):
                T = TURN["wq"] + n
                pe.wait_ge(acc_free[T % 2], T // 2 + 1)
                if n >= 2:
                    pe.wait_ge(S["key_sb"], n - 1)
                for e in range(4):
                    m = mm(ps[:, 6 + n % 2, e * P:(e + 1) * P], qP[:, 2 * n + e % 2, (e // 2) * P:(e // 2 + 1) * P],
                           subk[:, 2 * n + e % 2, :], start=True, stop=True)
                m.then_inc(S["key_mm"], 1)

            for n in range(8):
                fm_page(PAGE["wq"] + n, TURN["wq"] + n, h)
                if n >= 1:
                    key_scores(n - 1)
            key_scores(7)
            pe.wait_ge(S["key_sb"], 8)
            for tt in range(2):
                pe.wait_ge(S["selt_ready"], tt + 1)
                pe.wait_ge(S["placed"], 8)
                for c in range(3):
                    m = nc.tensor.transpose(ps[:, 6 + tt, c * P:(c + 1) * P], selv[:, tt, c, :], ident)
                m.then_inc(S["selt_mm"], 1)

            def scatter(i):
                for b in range(8):
                    n = 4 * i + b // 2
                    pe.wait_ge(S["oh_ready"], 2 * n + (b % 2 + 1))
                    if b % 2 == 0:
                        pe.wait_ge(S["row_hot"], n + 1)
                        if not isinstance(i, int):
                            pe.wait_ge(S["g_sb"], 4 * i + (b // 2 - 3))
                    for e in range(2):
                        c = 2 * (b % 2) + e
                        m = mm(ps[:, gate_banks[b // 2], c * P:(c + 1) * P], row_hot[b // 2][:, c, :], col_hot[b % 4][e],
                               start=True, stop=True)
                    m.then_inc(S["g_mm"], 1)

            pe.wait_ge(S["selt_sb"], 2)
            scatter(0)
            with pe.Fori(1, L // 16) as i:
                scatter(i)

            C0, T0 = piece_of(PAGE["peer"]), TURN["peer"]

            def up(e, c, i=0):
                turn(T0 + e, i)
                fm_piece(c, ps[:, (T0 + e) % 2, 0:L], h, i).then_inc(S["acc_ready"], 1)

            def down(e, c, i=0):
                piece_in(c, i)
                pe.wait_ge(S["a_ready"], e + 1 + LOOP * i)
                for tt in range(2):
                    tok = slice(tt * P, (tt + 1) * P)
                    for half in range(2):
                        o = ps[:, 2 + 2 * tt + half, :]
                        a = a_r[:, 0, e % 2, tok], a_r[:, 1, e % 2, tok]
                        v = [piece[:, q, c % 3, 4 * half:4 * half + 4, :] for q in range(2)]
                        end = isinstance(i, int) and e == P - 1
                        f = mm(o, a[1], v[0], start=False, stop=False, skip_group_check=True)
                        if tt == 0 and half == 0:
                            f.then_inc(S["piece_used"], 1)
                        mm(o, a[0], v[0], start=False, stop=False, skip_group_check=True)
                        m = mm(o, a[0], v[1], start=False, stop=end, skip_group_check=True)
                if end:
                    m.then_inc(S["experts_done"], 1)

            pe.wait_ge(S["g_sb"], L // 4)
            up(0, C0)
            up(1, C0 + 1)
            with pe.Fori(0, 126 // LOOP) as i:
                for u in range(LOOP):
                    down(u, C0 + 2 + 2 * u, i)
                    up(2 + u, C0 + 3 + 2 * u, i)
            down(126, C0 + 254)
            down(127, C0 + 255)

        @block.scalar
        def _(act):
            A = nc.scalar.activation
            steps = [0]

            def ac(ins):
                steps[0] += 1
                ins.then_inc(S["ach"], 1)
                act.wait_ge(S["ach"], steps[0])

            def split(p, i=0):
                for s in range(2):
                    c = 2 * (p - SPLIT0) + s
                    if s == 0:
                        act.wait_ge(loaded[p % RING], 16 * (p // RING + 1 + LOOP // RING * i))
                    if c >= 2 or not isinstance(i, int):
                        act.wait_ge(S["piece_used"], c - 1 + 2 * LOOP * i)
                    A(piece[:, 0, c % 3], ring[:, p % RING, s], ACT.Copy).then_inc(S["hi_ready"], 1)

            def stage(name, n, epilogue=None):
                rounds = n // LOOP if n >= 2 * LOOP else 0
                if rounds:
                    for u in range(LOOP):
                        split(PAGE[name] + u + 1)
                        epilogue(u, 0)
                    with act.Fori(1, rounds) as i:
                        for u in range(LOOP):
                            split(PAGE[name] + u + 1, i)
                            epilogue(u, i)
                for u in range(LOOP * rounds, n):
                    if PAGE[name] + u + 1 < NPAGES:
                        split(PAGE[name] + u + 1)
                    if epilogue:
                        epilogue(u, 0)

            def evac(T, dst, func=ACT.Copy, src=slice(0, 512), i=0, per=0, **kw):
                act.wait_ge(S["acc_ready"], T + 1 + 2 * per * i)
                A(dst, ps[:, T % 2, src], func, **kw).then_inc(acc_free[T % 2], 1)

            def head_norm(src, sqb, pairs, base, banks, n, eps):
                for q in range(pairs):
                    act.wait_ge(S["hn_cs"], base + q + 1)
                    A(sqb[:, 2 * q:2 * q + 2, :], src[:, 2 * q:2 * q + 2, :], ACT.Square).then_inc(S["hn_sq"], 1)
                for q in range(pairs):
                    act.wait_ge(S["hn_sqmm"], base + q + 1)
                    A(sqb[:, 2 * q:2 * q + 2, :], ps[:, banks[q], :].rearrange("p (a n) -> p a n", a=2), ACT.Ln,
                      scale=1.0 / n, bias=eps).then_inc(S["hn_ln"], 1)
                for q in range(pairs):
                    act.wait_ge(S["hn_ln"], base + q + 1)
                    A(sqb[:, 2 * q:2 * q + 2, :], sqb[:, 2 * q:2 * q + 2, :], ACT.Exp, scale=-0.5).then_inc(S["hn_root"], 1)

            def x_norm(n):
                act.wait_ge(S["x_new"], n + 1)
                A(sq, xres[:], ACT.Square).then_inc(S["xs_sq"], 1)
                act.wait_ge(S["xs_mm"], n + 1)
                ac(A(rs, ps[:, 2, 0:L], ACT.Ln, scale=1.0 / D, bias=eps6))
                A(rs, rs, ACT.Exp, scale=-0.5).then_inc(S["xs_root"], 1)

            act.dma_start(csil, t["cT"]).then_inc(S["c_in"], 16)
            act.dma_start(cols[:], t["cols"]).then_inc(S["cols_in"], 16)
            act.dma_start(pc[:], t["pconst"]).then_inc(S["pconst_in"], 16)
            act.wait_ge(S["c_in"], 16)
            A(csil, csil, ACT.Silu).then_inc(S["c_silu"], 1)
            act.wait_ge(S["x_in"], 32)
            A(sq1[:, :, 0:L], xres[:], ACT.Square).then_inc(S["sq1"], 1)
            A(sq1[:, :, L:], xctx, ACT.Square).then_inc(S["sq1"], 1)
            act.wait_ge(S["cols_in"], 16)
            A(lgpair, col("dec_pair", 0, 8), ACT.Exp)
            A(lgrow, col("dec_row", 0, 16), ACT.Exp).then_inc(S["lg_ready"], 1)
            act.wait_ge(S["stat1"], 1)
            ac(A(rs1, ps[:, 3, :], ACT.Ln, scale=1.0 / D, bias=eps6))
            A(rs1, rs1, ACT.Exp, scale=-0.5).then_inc(S["root1"], 1)
            act.dma_start(at(4096, N1), t["const1"]).then_inc(S["const1_in"], 16)
            split(SPLIT0)
            for n in range(16):
                c, k = n // 8, n % 8
                act.wait_ge(S["hraw"], n + 1)
                A((h, hctx_r)[c][0][:, k, :], (h_tmp, xctx)[c][:, k, :], ACT.Identity,
                  bias=mod[:, k, c:c + 1]).then_inc(S["h_hi"], 1)
            stage("q", 2, lambda u, i: evac(TURN["q"] + u, qraw[:, 2 * u:2 * u + 2, :]))

            def k_page(u, i):
                evac(TURN["k"] + 2 * u, qraw[:, 4 + 2 * u:6 + 2 * u, :])
                evac(TURN["k"] + 2 * u + 1, kc_tok[:, :, u * L:(u + 1) * L])

            stage("k", 2, k_page)
            act.wait_ge(S["wctx_arg"], 1)
            A(small[:, 152:184], small[:, 152:184], ACT.Exp).then_inc(S["wctx"], 1)
            act.wait_ge(S["const1_in"], 16)
            for n in range(8):
                A(qdec[:, n, :], c1("pos_q")[:, (n // 4) * L:(n // 4 + 1) * L], ACT.Exp,
                  scale=lgpair[:, n:n + 1]).then_inc(S["w_q"], 1)

            def v_page(u, i):
                evac(TURN["v"] + 2 * u, v_tok[:, :, u * L:(u + 1) * L])
                evac(TURN["v"] + 2 * u + 1, vc_tok[:, :, u * L:(u + 1) * L])

            stage("v", 4, v_page)
            stage("g", 4, lambda u, i: evac(TURN["g"] + u, sg[:, 2 * u:2 * u + 2, :], ACT.Silu))
            stage("f", 2, lambda u, i: evac(TURN["f"] + u, fT[:, 2 * u:2 * u + 2, :]))
            for d, st in enumerate((st_f, st_b)):
                act.wait_ge(S["state_mm"], d + 1)
                A(st, ps[:, 2 + d, :], ACT.Copy).then_inc(S["state_sb"], 1)

            def sigmoids(name, dst, bias):
                def page(u, i=0):
                    T = TURN[name] + u
                    act.wait_ge(S["acc_ready"], T + 1)
                    for s in range(2):
                        m = 2 * u + s
                        a = A(dst[:, m, :], ps[:, T % 2, s * L:(s + 1) * L], ACT.Sigmoid, bias=col(bias, m))
                    a.then_inc(acc_free[T % 2], 1)
                return page

            def hi_part(pairs, src, dst, sem, base=0):
                for q in range(pairs):
                    act.wait_ge(S[sem], base + q + 1)
                    A(dst[:, 2 * q:2 * q + 2, :], src[:, 2 * q:2 * q + 2, :], ACT.Copy).then_inc(S["part_hi"], 1)

            stage("bg", 8, sigmoids("bg", gates, "b_bg"))

            def decay_exp(n):
                act.wait_ge(S["decay_arg"], n + 1)
                A(decay[:, n % 2, :], decay[:, n % 2, :], ACT.Exp).then_inc(S["decay_exp"], 1)

            decay_exp(0)
            decay_exp(1)
            for n in range(8):
                act.wait_ge(S["out_mm"], n + 1)
                A(oT[:, n, :], ps[:, 6 + n % 2, 0:L], ACT.Copy).then_inc(S["o_sb"], 1)
                if n < 6:
                    decay_exp(n + 2)
            for n in range(4):
                act.wait_ge(S["fourier1"], n + 1)
                A(four_a[:, 2 * n:2 * n + 2, :], ps[:, 2 + n, :].rearrange("p (a n) -> p a n", a=2),
                  ACT.Copy).then_inc(S["four_sb"], 1)
            head_norm(oT, sq_o, 4, 0, (6, 7, 2, 3), 128, eps6)
            hi_part(2, zT, z_r[0], "z_sb")
            hi_part(4, oT, o_r[0], "part_in")
            stage("ro", 4)
            stage("fo", 2)
            hi_part(4, mg, mg_r[0], "part_in", 4)
            stage("wo", 4)
            act.wait_ge(S["x_new"], 1)
            act.dma_start(at(28672, N2), t["const2"]).then_inc(S["const2_in"], 16)
            x_norm(0)
            for k in range(8):
                act.wait_ge(S["hraw"], 16 + k + 1)
                A(h[0][:, k, :], sq[:, k, :], ACT.Identity, bias=mod[:, 24 + k, 0:1]).then_inc(S["h_hi"], 1)

            def gated_part(u, i):
                act.wait_ge(S["gated"], LOOP * i + (u + 1))
                A(ffn_r[0][:, bass.ds(LOOP * i + u, 1), :].rearrange("p a n -> p (a n)"), uav[:, 2 * (u % 2) + 1, :],
                  ACT.Copy).then_inc(S["gated_hi"], 1)

            def conv_page(u, i):
                T, b = TURN["up"] + u, u % 2
                n = LOOP * i + u
                act.wait_ge(S["acc_ready"], T + 1 + LOOP * i)
                act.wait_ge(S["ffn_ready"], n + 1)
                c0 = COL["conv"][0]
                for s in range(2):
                    a = A(uav[:, 2 * b + s, :], ps[:, T % 2, s * L:(s + 1) * L], ACT.Identity,
                          scale=cols[:, bass.ds(8 * LOOP * i + (c0 + 8 * u + 4 * s + 1), 1)],
                          bias=cols[:, bass.ds(8 * LOOP * i + (c0 + 8 * u + 4 * s + 3), 1)])
                a.then_inc(S["conv_mid"], 1)
                if not (isinstance(i, int) and u == 0):
                    gated_part(u - 1, i)
                act.wait_ge(S["conv_u"], n + 1)
                A(ga[:, b, :], uav[:, 2 * b, :], ACT.Gelu_apprx_tanh).then_inc(S["gelu_done"], 1)

            stage("up", 22, conv_page)
            gated_part(21, 0)
            stage("dn", 11)
            x_norm(1)
            x_norm(2)
            for k in range(8):
                act.wait_ge(S["hraw"], 24 + k + 1)
                A(h[0][:, k, :], sq[:, k, :], ACT.Copy).then_inc(S["h_hi"], 1)
            stage("lora", 1, lambda u, i: evac(TURN["lora"], zraw[:, 12:14, :]))
            stage("rkv", 6, lambda u, i: evac(TURN["rkv"] + u, zraw[:, 2 * u:2 * u + 2, :]))
            act.wait_ge(S["mqk_pad"], 1)
            stage("mqk", 4, lambda u, i: evac(TURN["mqk"] + u, mqk_raw[:, 2 * u:2 * u + 2, 3:259]))
            stage("mv", 2, lambda u, i: evac(TURN["mv"] + u, mv_tok[:, :, u * L:(u + 1) * L]))
            stage("mo", 2, lambda u, i: evac(TURN["mo"] + u, so[:, 2 * u:2 * u + 2, :], ACT.Sigmoid))
            T = TURN["if"]
            act.wait_ge(S["acc_ready"], T + 1)
            A(m_rows[0:4, 0, :], ps[0:4, T % 2, 0:L], ACT.Identity, bias=col("if_b", 0)[0:4])
            A(m_rows[0:4, 1, :], ps[0:4, T % 2, L:2 * L], ACT.Identity, bias=col("if_b", 1)[0:4]).then_inc(acc_free[T % 2], 1)
            gt_sigmoids = sigmoids("gt", gates2, "gate_b")

            def gate_page(u):
                split(PAGE["gt"] + u + 1)
                gt_sigmoids(u)

            gate_page(0)
            cq = COL["cqk"][0]
            for n in range(8):
                A(mqk[:, n, :], mqk_raw[:, n, 3:259], ACT.Identity, scale=cols[:, cq + 5 * n + 3:cq + 5 * n + 4],
                  bias=cols[:, cq + 5 * n + 4:cq + 5 * n + 5]).then_inc(S["mqk_conv"], 1)
            act.wait_ge(S["lf_abs"], 1)
            ac(A(m_rows[0:4, 2, :], m_rows[0:4, 2, :], ACT.Exp, scale=-1.0))
            A(m_rows[0:4, 2, :], m_rows[0:4, 2, :], ACT.Ln, bias=1.0).then_inc(S["lf_ln"], 1)
            gate_page(1)
            act.wait_ge(S["rows_done"], 1)
            A(m_rows[0:4, 6, :], m_rows[0:4, 6, :], ACT.Exp).then_inc(S["rows_done"], 1)
            for n in range(8):
                act.wait_ge(S["mqk_taps"], n + 1)
                A(mqk[:, n, :], mqk[:, n, :], ACT.Silu).then_inc(S["mqk_silu"], 1)
            act.wait_ge(S["uc_mm"], 1)
            A(ucol, ps[:, 2, 0:8], ACT.Copy).then_inc(S["uc_sb"], 1)
            for n in range(4):
                act.wait_ge(S["bc_mm"], n + 1)
                A(m_bc[:, n, :], ps[:, 4 + n, :], ACT.Copy).then_inc(S["em_row"], 1)
            gate_page(2)
            for n in range(4):
                act.wait_ge(S["m_arg"], n + 1)
                A(m_e[:, n % 2, :], m_e[:, n % 2, :], ACT.Exp, scale=-1.0).then_inc(S["m_exp"], 1)
            gate_page(3)
            head_norm(m_dn, m_sq, 2, 4, (2, 3), 128, eps_ml)
            act.wait_ge(S["zs_ready"], 2)
            A(lora_in[0:64, 0, :], zs[0:64, 12, :], ACT.Tanh).then_inc(S["lora_tanh"], 1)
            A(lora_in[:, 1, :], zs[:, 13, :], ACT.Sigmoid).then_inc(S["lora_tanh"], 1)
            gate_page(4)
            for q in range(6):
                act.wait_ge(S["lora_mm"], q + 1)
                for e in range(2):
                    m = (2 * q + e) % 4
                    src = ps[:, 2 + q, e * L:(e + 1) * L]
                    if q < 2:
                        a = A(lw[:, m, :], src, ACT.Sigmoid, bias=col("w0", m))
                    elif q < 4:
                        a = A(aT[:, m, :], src, ACT.Sigmoid, bias=col("a0", m))
                    else:
                        a = A(gT[:, m, :], src, ACT.Copy)
                    a.then_inc(S["lora_act"], 1)
            gate_page(5)
            for q in range(2):
                act.wait_ge(S["kk_mm"], q + 1)
                A(ltmp[:, 2 * q:2 * q + 2, :], ps[:, 2 + q, :].rearrange("p (a n) -> p a n", a=2),
                  ACT.Sqrt).then_inc(S["kk_root"], 1)
            act.wait_ge(S["scan_done"], 1)
            A(wcum, cum, ACT.Exp).then_inc(S["w_exp"], 1)
            A(winv, cum, ACT.Exp, scale=-1.0).then_inc(S["w_exp"], 1)
            A(wprev, wprev, ACT.Exp).then_inc(S["w_exp"], 1)
            gate_page(6)
            gate_page(7)
            for n in range(8):
                act.wait_ge(S["tok_mm"], n + 1)
                A((atok, btok, ktok, vtok)[n // 2][:, n % 2, :], ps[:, 2 + n % 6, :], ACT.Copy).then_inc(S["tok_sb"], 1)
            for q in range(20):
                act.wait_ge(S["p1_mm"], q + 1)
                if q >= 2:
                    act.wait_ge(S["x_mm"], q - 1)
                A(P1[q % 2], ps[:, 2 + q % 2, :].rearrange("p (a n) -> p a n", a=4), ACT.Copy).then_inc(S["p1_sb"], 1)
            for i in range(2):
                act.wait_ge(S["xa_mm"], i + 1)
                A(xat[:, :, i, :], ps[:, 2 + i, :].rearrange("p (a n) -> p a n", a=4), ACT.Copy).then_inc(S["xa_sb"], 1)
            for i in range(2):
                act.wait_ge(S["xa_mm"], i + 3)
                A(lv[:, i, :], ps[:, 4 + i, :], ACT.Copy).then_inc(S["lv_sb"], 1)
            for i in range(2):
                act.wait_ge(S["u0_mm"], i + 1)
                A(U0[:, i, :], ps[:, 6 + i, :], ACT.Copy).then_inc(S["u0_sb"], 1)
            head_norm(yT, rw_tmp, 2, 6, (4, 5), 64, eps_gn)
            hi_part(2, yT, y_r[0], "part_in", 8)
            hi_part(2, so, ym_r[0], "part_in", 10)
            act.dma_start(subk.rearrange("p g n -> p (g n)"), t["subk"]).then_inc(S["subk_in"], 16)
            stage("pr", 2)
            stage("pm", 2)
            hi_part(4, mg2, mg2_r[0], "part_in", 12)
            stage("w2", 4)
            x_norm(3)
            for k in range(8):
                act.wait_ge(S["hraw"], 32 + k + 1)
                A(h[0][:, k, :], sq[:, k, :], ACT.Copy).then_inc(S["h_hi"], 1)

            def key_evac(n):
                act.wait_ge(S["key_mm"], n + 1)
                A(s_sb[:, :, 2 * n:2 * n + 2, :].rearrange("p t g n -> p t (g n)"),
                  ps[:, 6 + n % 2, :].rearrange("p (t n) -> p t n", t=2), ACT.Copy).then_inc(S["key_sb"], 1)

            def wq_page(u, i):
                evac(TURN["wq"] + u, qP[:, 2 * u:2 * u + 2, :])
                if u >= 1:
                    key_evac(u - 1)

            stage("wq", 8, wq_page)
            key_evac(7)
            for tt in range(2):
                act.wait_ge(S["g_arg"], tt + 1)
                A(selv[:, tt, 2, :], selv[:, tt, 2, :], ACT.Exp).then_inc(S["g_exp"], 1)
            act.wait_ge(S["x_in_psum"], 1)
            for tt in range(2):
                act.wait_ge(S["selt_mm"], tt + 1)
                A(selT[:, :, tt * P:(tt + 1) * P], ps[:, 6 + tt, 0:384].rearrange("p (a n) -> p a n", a=3),
                  ACT.Copy).then_inc(S["selt_sb"], 1)

            def gates_out(i, b):
                act.wait_ge(S["g_mm"], 8 * i + (2 * b + 2))
                A(G[:, :, bass.ds(16 * i + 4 * b, 4)].rearrange("p e n -> p n e"),
                  ps[:, gate_banks[b % 4], :].rearrange("p (a n) -> p a n", a=4), ACT.Copy).then_inc(S["g_sb"], 1)

            def rows(i):
                for b in range(4):
                    r = row_hot[b][:, 0:3]
                    act.wait_ge(S["row_minus"], 4 * i + (b + 1))
                    A(r, r, ACT.Square).then_inc(S["row_square"], 1)
                    if not isinstance(i, int) or b >= 2:
                        gates_out(i, b - 2)
                    act.wait_ge(S["row_square"], 4 * i + (b + 1))
                    A(r, r, ACT.Relu, scale=-1.0, bias=1.0).then_inc(S["row_hot"], 1)

            rows(0)
            with act.Fori(1, L // 16) as i:
                rows(i)
            gates_out(L // 16 - 1, 2)
            gates_out(L // 16 - 1, 3)

            def gelu(e, i=0):
                T = TURN["peer"] + e
                act.wait_ge(S["acc_ready"], T + 1 + LOOP * i)
                if not (isinstance(i, int) and e < 2):
                    act.wait_ge(S["a_ready"], LOOP * i + (e - 1))
                A(gelu_t[:, e % 2, :], ps[:, T % 2, 0:L], ACT.Gelu).then_inc(acc_free[T % 2], 1)

            E0 = PAGE["peer"]
            split(E0 + 1)
            gelu(0)
            gelu(1)
            with act.Fori(0, 126 // LOOP) as i:
                for u in range(LOOP):
                    split(E0 + 2 + u, i)
                    gelu(2 + u, i)
            act.wait_ge(S["a_ready"], P)
            act.dma_start(fgrow, t["fg"]).then_inc(S["fg_in"], 16)
            act.wait_ge(S["experts_done"], 1)
            for tt in range(2):
                A(at(1024 * tt, 1024).rearrange("p (a n) -> p a n", a=2), ps[:, 2 + 2 * tt:4 + 2 * tt, :], ACT.Square,
                  accum_out=fstat[:, tt:tt + 1]).then_inc(S["fin_sq"], 1)
            for tt in range(2):
                act.wait_ge(S["fin_sq"], tt + 1)
                A(fstat[:, 2 + tt:3 + tt], fstat[:, tt:tt + 1], ACT.Sqrt, scale=1.0 / D, bias=eps6).then_inc(S["fin_root"], 1)

        @block.vector
        def _(dve):
            V = nc.vector
            TT, STT, TS = V.tensor_tensor, V.scalar_tensor_tensor, V.tensor_scalar
            steps = [0]

            def dv(ins):
                steps[0] += 1
                ins.then_inc(S["dch"], 1)
                dve.wait_ge(S["dch"], steps[0])

            def split(p, i=0):
                for s in range(2):
                    c = 2 * (p - SPLIT0) + s
                    dve.wait_ge(S["hi_ready"], c + 1 + 2 * LOOP * i)
                    TT(piece[:, 1, c % 3], ring[:, p % RING, s], piece[:, 0, c % 3].bitcast(F32),
                       ALU.subtract).then_inc(S["lo_ready"], 1)

            def stage(name, n, epilogue=None):
                rounds = n // LOOP if n >= 2 * LOOP else 0
                if rounds:
                    with dve.Fori(0, rounds) as i:
                        for u in range(LOOP):
                            split(PAGE[name] + u + 1, i)
                            if epilogue:
                                epilogue(u, i)
                for u in range(LOOP * rounds, n):
                    if PAGE[name] + u + 1 < NPAGES:
                        split(PAGE[name] + u + 1)
                    if epilogue:
                        epilogue(u, 0)

            parts = [0]

            def lo_part(pairs, src, dst, sem=None):
                for q in range(pairs):
                    parts[0] += 1
                    dve.wait_ge(S["part_hi"], parts[0])
                    sl = slice(2 * q, 2 * q + 2)
                    ins = TT(dst[1][:, sl, :], src[:, sl, :], dst[0][:, sl, :].bitcast(F32), ALU.subtract)
                    if q == pairs - 1 and sem:
                        ins.then_inc(S[sem], 1)

            def turn_read(T):
                dve.wait_ge(acc_free[T % 2], T // 2 + 1)

            def head_norm(src, sqb, pairs, base, banks, n):
                for q in range(pairs):
                    v = src[:, 2 * q:2 * q + 2, :]
                    dve.wait_ge(S["hn_mm"], base + q + 1)
                    STT(v, ps[:, banks[q], :].rearrange("p (a n) -> p a n", a=2), -1.0 / n, v, ALU.mult,
                        ALU.add).then_inc(S["hn_cs"], 1)
                for q in range(pairs):
                    v, w = src[:, 2 * q:2 * q + 2, :], sqb[:, 2 * q:2 * q + 2, :]
                    dve.wait_ge(S["hn_root"], base + q + 1)
                    dv(TT(v, v, w, ALU.mult))

            his = [16]

            def x_norm(n, dst, gain, shift=None):
                dve.wait_ge(S["xs_root"], n + 1)
                sem = "xfin" if dst is xres else "hraw"
                for k in range(8):
                    STT(dst[:, k, :], xres[:, k, :], gain[:, k:k + 1], rs, ALU.mult, ALU.mult).then_inc(S[sem], 1)
                if dst is xres:
                    return
                for k in range(8):
                    his[0] += 1
                    dve.wait_ge(S["h_hi"], his[0])
                    STT(h[1][:, k, :], dst[:, k, :], 0.0 if shift is None else mod[:, shift + k, 0:1],
                        h[0][:, k, :].bitcast(F32), ALU.add, ALU.subtract).then_inc(S["h_new"], 1)

            dve.wait_ge(S["lg_ready"], 1)
            dv(TS(small[:, 128:152], small[:, 128:152], -1.0, None, ALU.mult))
            for g in range(4):
                dve.wait_ge(S["mod_used"], 2 * g + 2)
                V.tensor_copy(mrow[0:2, 512 * g:512 * g + 512], ps[0:2, 4 + g, :]).then_inc(S["mrow_sb"], 1)
            split(SPLIT0)
            dve.wait_ge(S["mod_cols"], 1)
            dv(TT(mod[:, 0:16, :], ps[:, 2, 0:32].rearrange("p (m c) -> p m c", c=2),
                  col("b_mod", 0, 16).unsqueeze(2).to_broadcast([P, 16, 2]), ALU.add))
            dv(TS(gain, mod[:, 8:16, :], 1.0, None, ALU.add))
            dv(TT(gain, gain, col("norm1_w", 0, 8).unsqueeze(2).to_broadcast([P, 8, 2]), ALU.mult))
            dve.wait_ge(S["root1"], 1)
            for n in range(16):
                c, k = n // 8, n % 8
                STT((h_tmp, xctx)[c][:, k, :], (xres, xctx)[c][:, k, :], gain[:, k, c:c + 1], rs1[:, c * L:(c + 1) * L],
                    ALU.mult, ALU.mult).then_inc(S["hraw"], 1)
            for n in range(16):
                c, k = n // 8, n % 8
                hi, lo = (h, hctx_r)[c]
                dve.wait_ge(S["h_hi"], n + 1)
                STT(lo[:, k, :], (h_tmp, xctx)[c][:, k, :], mod[:, k, c:c + 1], hi[:, k, :].bitcast(F32), ALU.add,
                    ALU.subtract).then_inc(S["h_ready"], 1)
            dve.wait_ge(S["const1_in"], 16)
            TT(wctx, c1("pos_ctx", "p (t n) -> p t n", t=2), lgrow.unsqueeze(1).to_broadcast([P, 2, 16]),
               ALU.mult).then_inc(S["wctx_arg"], 1)
            stage("q", 2)
            stage("k", 2)
            stage("v", 4)
            stage("g", 4)

            def late_mod(half):
                dve.wait_ge(S["mod2_mm"], half + 1)
                b, c, m = ((2, 32, 16), (7, 0, 32))[half]
                return TT(mod[:, m:m + 16, 0], ps[:, b, c:c + 16], col("b_mod", m, 16), ALU.add)

            late_mod(0)
            stage("f", 2)
            for q in range(4):
                cos = c1("cosq" if q < 2 else "cosk").unsqueeze(1).to_broadcast([P, 2, L])
                sin = c1("sinq" if q < 2 else "sink").unsqueeze(1).to_broadcast([P, 2, L])
                dve.wait_ge(S["perm_mm"], q + 1)
                dv(TT(qk[:, 2 * q:2 * q + 2, :], ps[:, 4 + q, :].rearrange("p (a n) -> p a n", a=2), sin, ALU.mult))
                dv(TT(qraw[:, 2 * q:2 * q + 2, :], qraw[:, 2 * q:2 * q + 2, :], cos, ALU.mult))
                TT(qk[:, 2 * q:2 * q + 2, :], qk[:, 2 * q:2 * q + 2, :], qraw[:, 2 * q:2 * q + 2, :],
                   ALU.add).then_inc(S["qk_ready"], 1)
            dve.wait_ge(S["wctx"], 1)
            for d, kw in enumerate((kw_f, kw_b)):
                for tt in range(2):
                    w = wctx[:, tt, 8 * d:8 * d + 8].unsqueeze(2).to_broadcast([P, 8, 64])
                    ins = TT(kw[:, tt, :].rearrange("p (h c) -> p h c", h=8),
                             kc_tok[:, tt, :].rearrange("p (h c) -> p h c", h=8), w, ALU.mult)
                    if d == 1 and tt == 1:
                        ins.then_inc(S["kw_ready"], 1)
            dve.wait_ge(S["w_q"], 8)
            dve.wait_ge(S["qk_ready"], 4)
            for d in range(2):
                TT(qdec[:, 4 * d:4 * d + 4, :], qdec[:, 4 * d:4 * d + 4, :], qk[:, 0:4, :], ALU.mult).then_inc(S["qdec"], 1)

            def decay_arg(n):
                d = decay[:, n % 2, :]
                dv(TS(d, c1("dist_f"), lgrow[:, n:n + 1], None, ALU.mult))
                STT(d, c1("dist_b"), lgrow[:, 8 + n:9 + n], d, ALU.mult, ALU.add).then_inc(S["decay_arg"], 1)

            stage("bg", 8)
            dv(late_mod(1))
            dv(TS(gain2, mod[:, 32:40, 0], 1.0, None, ALU.add))
            TT(gain2, gain2, col("norm2_w", 0, 8), ALU.mult)
            decay_arg(0)
            decay_arg(1)
            for n in range(8):
                dve.wait_ge(S["scores"], n + 1)
                dve.wait_ge(S["decay_m"], n + 1)
                if n >= 2:
                    dve.wait_ge(S["out_mm"], n - 1)
                TT(probs[:, n % 2, :], ps[:, 4 + n % 2, :], decay[:, n % 2, :], ALU.mult).then_inc(S["probs"], 1)
                if n < 6:
                    dve.wait_ge(S["probs"], n + 1)
                    decay_arg(n + 2)
            for q in range(2):
                dve.wait_ge(S["fourier2"], q + 1)
                V.tensor_copy(zT[:, 2 * q:2 * q + 2, :], ps[:, 6 + q, :].rearrange("p (a n) -> p a n", a=2)).then_inc(S["z_sb"], 1)
            head_norm(oT, sq_o, 4, 0, (2, 3, 4, 5), 128)
            lo_part(2, zT, z_r)
            for q in range(4):
                sl = slice(2 * q, 2 * q + 2)
                TT(oT[:, sl, :], oT[:, sl, :], sg[:, sl, :], ALU.mult).then_inc(S["part_in"], 1)
            lo_part(4, oT, o_r, "ret_ready")

            def merge(names, pages, gate, dst, dst_r):
                for b, name in enumerate(names):
                    def page(u_, i):
                        turns = 4 // pages[b]
                        for u in range(turns * u_, turns * (u_ + 1)):
                            T = TURN[name] + u
                            dve.wait_ge(S["acc_ready"], T + 1)
                            v = ps[:, T % 2, :].rearrange("p (a n) -> p a n", a=2)
                            g2 = gate[:, 8 * b + 2 * u:8 * b + 2 * u + 2, :]
                            d2 = dst[:, 2 * u:2 * u + 2, :]
                            if b == 0:
                                TT(d2, v, g2, ALU.mult).then_inc(acc_free[T % 2], 1)
                            else:
                                TT(g2, v, g2, ALU.mult).then_inc(acc_free[T % 2], 1)
                                dve.wait_ge(acc_free[T % 2], T // 2 + 1)
                                TT(d2, d2, g2, ALU.add).then_inc(S["part_in"], 1)
                    stage(name, pages[b], page)
                lo_part(4, dst, dst_r, "mg_ready")

            def residual(name, gate=None):
                def add(u, i=0):
                    T = TURN[name] + u
                    dve.wait_ge(S["acc_ready"], T + 1)
                    if gate is None:
                        x2 = xres[:, 2 * u:2 * u + 2, :]
                        ins = TT(x2, x2, ps[:, T % 2, :].rearrange("p (a n) -> p a n", a=2), ALU.add)
                    else:
                        for s in range(2):
                            k = 2 * u + s
                            ins = STT(xres[:, k, :], ps[:, T % 2, s * L:(s + 1) * L], mod[:, gate + k, 0:1], xres[:, k, :],
                                      ALU.mult, ALU.add)
                    ins.then_inc(acc_free[T % 2], 1)
                if name == "dn":
                    stage(name, 11, lambda u, i: add((2, 5, 8, 10).index(u)) if u in (2, 5, 8, 10) else None)
                else:
                    stage(name, 4, add)
                T = TURN[name] + 3
                dve.wait_ge(acc_free[T % 2], T // 2 + 1)
                dve.wait_ge(acc_free[(T - 1) % 2], (T - 1) // 2 + 1)
                V.engine_nop().then_inc(S["x_new"], 1)

            merge(("ro", "fo"), (4, 2), gates, mg, mg_r)
            residual("wo", 16)
            x_norm(0, sq, gain2, 24)

            def conv_page(u, i):
                T, b = TURN["up"] + u, u % 2
                n = LOOP * i + u
                c0 = COL["conv"][0] + 8 * u
                dve.wait_ge(S["conv_mid"], n + 1)
                for s in range(2):
                    x, y = ps[:, T % 2, s * L:(s + 1) * L], uav[:, 2 * b + s, :]
                    STT(y[:, 1:], x[:, :L - 1], cols[:, bass.ds(8 * LOOP * i + (c0 + 4 * s), 1)], y[:, 1:], ALU.mult,
                        ALU.add).then_inc(S["up_chain"], 1)
                    dve.wait_ge(S["up_chain"], 2 * n + (s + 1))
                    ins = STT(y[:, :L - 1], x[:, 1:], cols[:, bass.ds(8 * LOOP * i + (c0 + 4 * s + 2), 1)], y[:, :L - 1],
                              ALU.mult, ALU.add)
                    ins.then_inc(S["conv_u"] if s == 0 else acc_free[T % 2], 1)
            stage("up", 22, conv_page)
            residual("dn", 40)
            x_norm(1, xres, col("final_norm_w", 0, 8))
            dve.wait_ge(S["xfin"], 8)
            V.engine_nop().then_inc(S["x_new"], 1)
            x_norm(2, sq, col("norm1_g_2", 0, 8))
            stage("lora", 1)
            stage("rkv", 6)
            for T in (TURN["rkv"] + 5, TURN["rkv"] + 4):
                turn_read(T)
            V.tensor_scalar(zd[:, :, 0], zraw[:, :, 0], -1.0, None, ALU.mult)
            dv(TT(zd[:, :, 1:], zraw[:, :, :L - 1], zraw[:, :, 1:], ALU.subtract))
            for n in (12, 13, *range(12)):
                ins = STT(zs[:, n, :], zd[:, n, :], col("mu", n), zraw[:, n, :], ALU.mult, ALU.add)
                if n >= 12 or n == 11:
                    ins.then_inc(S["zs_ready"], 1)
            for name, n in (("mqk", 4), ("mv", 2), ("mo", 2)):
                stage(name, n)

            def gate_page(u):
                split(PAGE["gt"] + u + 1)

            gate_page(0)
            turn_read(TURN["if"])
            r = m_rows[0:4]
            STT(r[:, 2, :], r[:, 1, :], -1.0, r[:, 1, :], ALU.mult, ALU.max).then_inc(S["lf_abs"], 1)
            dv(TS(r[:, 1, :], r[:, 1, :], 0.0, None, ALU.min))
            dv(V.memset(r[:, 7, :], 1.0))
            dve.wait_ge(S["lf_ln"], 1)
            dv(TT(r[:, 3, :], r[:, 1, :], r[:, 2, :], ALU.subtract))
            dv(V.tensor_tensor_scan(r[:, 1, :], r[:, 7, :], r[:, 3, :], 0.0, ALU.mult, ALU.add))
            dv(TT(r[:, 4, :], r[:, 0, :], r[:, 1, :], ALU.subtract))
            dv(V.tensor_tensor_scan(r[:, 5, :], r[:, 4, :], r[:, 4, :], 0.0, ALU.max, ALU.max))
            dv(TT(r[:, 6, :], r[:, 1, :], r[:, 5, :], ALU.add))
            TS(r[:, 6, :], r[:, 6, :], -1.0, 88.0, ALU.mult, ALU.min).then_inc(S["rows_done"], 1)
            gate_page(1)
            cq = COL["cqk"][0]
            for n in range(8):
                dve.wait_ge(S["mqk_conv"], n + 1)
                for tap in range(3):
                    ins = STT(mqk[:, n, :], mqk_raw[:, n, tap:tap + L], cols[:, cq + 5 * n + tap:cq + 5 * n + tap + 1],
                              mqk[:, n, :], ALU.mult, ALU.add)
                    if tap < 2:
                        dv(ins)
                ins.then_inc(S["mqk_taps"], 1)
            dve.wait_ge(S["uc_sb"], 1)

            def m_arg(n):
                dve.wait_ge(S["em_row"], n + 1)
                for st in range(2):
                    ins = TS(m_e[:, n % 2, st * L:(st + 1) * L], m_bc[:, n, 0:L], ucol[:, 4 * st + n:4 * st + n + 1], 0.0,
                             ALU.subtract, ALU.max)
                ins.then_inc(S["m_arg"], 1)

            def m_head(n):
                dve.wait_ge(S["nd_mm"], n + 1)
                d = m_dn[:, n, :]
                den = ps[:, 4 + n % 2, L:2 * L]
                dv(STT(d, den, -1.0, m_bc[:, n, L:2 * L], ALU.mult, ALU.max))
                dv(STT(d, den, 1.0, d, ALU.mult, ALU.max))
                dv(V.reciprocal(d, d))
                TT(d, d, ps[:, 4 + n % 2, 0:L], ALU.mult).then_inc(S["m_h"], 1)

            m_arg(0)
            gate_page(2)
            for n in range(4):
                if n < 3:
                    m_arg(n + 1)
                dve.wait_ge(S["m_exp"], n + 1)
                dv(TT(m_e[:, n % 2, :], m_e[:, n % 2, :], c2("causal"), ALU.mult))
                dve.wait_ge(S["ms_mm"], n + 1)
                if n >= 2:
                    dve.wait_ge(S["nd_mm"], n - 1)
                STT(m_p[:, n % 2, :], ps[:, 2 + n % 2, :], 128.0 ** -0.5, m_e[:, n % 2, :], ALU.mult,
                    ALU.mult).then_inc(S["m_probs"], 1)
                dve.wait_ge(S["m_probs"], n + 1)
                if n >= 1:
                    m_head(n - 1)
            m_head(3)
            gate_page(3)
            dve.wait_ge(S["m_h"], 4)
            head_norm(m_dn, m_sq, 2, 4, (6, 7), 128)
            turn_read(TURN["mo"] + 1)
            for n in range(4):
                ins = STT(so[:, n, :], m_dn[:, n, :], col("ml_norm", n), so[:, n, :], ALU.mult, ALU.mult)
            ins.then_inc(S["ym_ready"], 1)

            dve.wait_ge(S["zs_ready"], 3)
            for m in range(4):
                ins = TS(kk[:, m, :], zs[:, 4 + m, :], col("k_k", m), None, ALU.mult)
            dv(ins)
            TT(ltmp, kk, kk, ALU.mult).then_inc(S["kk_sq"], 1)
            gate_page(4)
            dve.wait_ge(S["lora_act"], 4)
            dv(TS(lw, lw, -EXP_HALF, None, ALU.mult))
            for m in range(4):
                ins = V.tensor_tensor_scan(cum[:, m, :], c2("scan"), lw[:, m, :], 0.0, ALU.mult, ALU.add)
            dv(ins)
            TT(wprev, cum, lw, ALU.subtract).then_inc(S["scan_done"], 1)
            gate_page(5)
            dve.wait_ge(S["kk_root"], 2)
            dv(TS(ltmp, ltmp, 1e-12, None, ALU.max))
            dv(V.reciprocal(ltmp, ltmp))
            dv(TT(kk, kk, ltmp, ALU.mult))
            dve.wait_ge(S["lora_act"], 8)
            for m in range(4):
                ins = TS(ltmp[:, m, :], aT[:, m, :], -1.0, col("k_a", m), ALU.add, ALU.mult)
            dv(ins)
            dv(STT(zs[:, 4:8, :], ltmp, 1.0, zs[:, 4:8, :], ALU.add, ALU.mult))
            TT(bT, kk, aT, ALU.mult)
            dv(TT(bon, zs[:, 0:4, :], zs[:, 4:8, :], ALU.mult))
            for m in range(4):
                ins = TS(bon[:, m, :], bon[:, m, :], col("r_k", m), None, ALU.mult)
            ins.then_inc(S["bon_in"], 1)
            gate_page(6)
            for q in range(2):
                dve.wait_ge(S["bon_mm"], q + 1)
                TT(bon[:, 2 * q:2 * q + 2, :], ps[:, 4 + q, :].rearrange("p (a n) -> p a n", a=2),
                   zs[:, 8 + 2 * q:10 + 2 * q, :], ALU.mult)
            dve.wait_ge(S["w_exp"], 3)
            flat = "p j (i n) -> p (j i) n"
            STT(ar2[:, :, 0, :], wprev.rearrange(flat, i=2), -1.0, kk.rearrange(flat, i=2), ALU.mult, ALU.mult)
            TT(ar2[:, :, 1, :], wcum.rearrange(flat, i=2), zs[:, 0:4, :].rearrange(flat, i=2), ALU.mult)
            TT(beta, bT, winv, ALU.mult)
            V.tensor_copy(wend, wcum[:, :, 63::64])
            TT(kappa, zs[:, 4:8, :], winv, ALU.mult).then_inc(S["alpha_ready"], 1)
            gate_page(7)
            for n in range(16):
                g4 = n // 4
                dve.wait_ge(S["gram_mm"], n + 1)
                TT(gram[:, n].rearrange("p a s -> p (a s)"), ps[:, 2 + n % 4, :], c2("mask4"), ALU.mult).then_inc(S["gram_sb"], 1)
                if n % 4 == 3:
                    X4, T4 = Xn[:, n - 3:n + 1, :], XT[:, n - 3:n + 1, :]
                    idb = ident.unsqueeze(1).to_broadcast([P, 4, P])
                    dve.wait_ge(S["l_mm"], g4 + 1)
                    l4 = ps[:, 6:8, 0:256].rearrange("p e (a n) -> p a e n", a=2)
                    dv(TT(X4.rearrange("p (a e) n -> p a e n", a=2), l4,
                          c2("m1").unsqueeze(1).unsqueeze(1).to_broadcast([P, 2, 2, P]), ALU.mult))
                    dve.wait_ge(S["gram_sb"], n + 1)
                    dv(TT(T4, gram[:, n - 3:n + 1, 0, :], c2("m1t").unsqueeze(1).to_broadcast([P, 4, P]), ALU.mult))
                    TT(X4, X4, idb, ALU.add)
                    TT(T4, T4, idb, ALU.add).then_inc(S["x_init"], 1)
            V.memset(states[:, 0], 0.0).then_inc(S["s_sb"], 1)
            for q in range(20):
                g4 = 4 * (q % 4)
                dve.wait_ge(S["x_mm"], q + 1)
                if q < 16:
                    TT(Xn[:, g4:g4 + 4, :], Xn[:, g4:g4 + 4, :], ps[:, 4 + q % 2, :].rearrange("p (a n) -> p a n", a=4), ALU.add)
                TT(XT[:, g4:g4 + 4, :], XT[:, g4:g4 + 4, :], ps[:, 6 + q % 2, :].rearrange("p (a n) -> p a n", a=4),
                   ALU.add).then_inc(S["x_sb"], 1)
            dve.wait_ge(S["u0_sb"], 2)
            for n in range(4):
                i, c = n // 2, n % 2
                rr = slice(64 * c, 64 * c + 64)
                dve.wait_ge(S["sa_mm"], n + 1)
                by_row = "p (j e v) -> p e j v"
                TT(sa[rr, i, :].rearrange(by_row, e=2, v=64),
                   ps[rr, 2:4, 256 * c:256 * c + 256].rearrange("p e (j v) -> p e j v", v=64),
                   U0[rr, i, :].rearrange(by_row, e=2, v=64), ALU.add).then_inc(S["sa_sb"], 1)
                if n < 3:
                    dve.wait_ge(S["ds_mm"], n + 1)
                    dv(TT(states[:, n + 1], states[:, n], ps[:, 4 + c, 0:256].rearrange("p (j v) -> p j v", j=4), ALU.add))
                    TT(states[:, n + 1], states[:, n + 1], wend[:, :, n:n + 1].to_broadcast([P, 4, 64]),
                       ALU.mult).then_inc(S["s_sb"], 1)
                    dve.wait_ge(S["s_sb"], n + 2)
            for i in range(2):
                dve.wait_ge(S["y_mm"], i + 1)
                V.tensor_copy(yT[:, :, i * P:(i + 1) * P],
                              ps[:, 6 + i, :].rearrange("p (j n) -> p j n", j=4)).then_inc(S["y_sb"], 1)
            dve.wait_ge(S["y_sb"], 2)
            head_norm(yT, rw_tmp, 2, 6, (2, 3), 64)
            for m in range(4):
                ins = TS(yT[:, m, :], yT[:, m, :], col("gn_w", m), col("gn_b", m), ALU.mult, ALU.add)
            dv(ins)
            dv(TT(yT, yT, bon, ALU.add))
            for q in range(2):
                sl = slice(2 * q, 2 * q + 2)
                TT(yT[:, sl, :], yT[:, sl, :], gT[:, sl, :], ALU.mult).then_inc(S["part_in"], 1)
            V.engine_nop().then_inc(S["part_in"], 1)
            V.engine_nop().then_inc(S["part_in"], 1)
            lo_part(2, yT, y_r, "y_ready")
            lo_part(2, so, ym_r, "y_ready")
            merge(("pr", "pm"), (2, 2), gates2, mg2, mg2_r)
            residual("w2")
            x_norm(3, sq, col("norm2_g", 0, 8))

            def best16s(srcs, vals, idxs):
                for v, x in zip(vals, srcs):
                    ins = V.max(v[:, 0:8], x)
                dv(ins)
                for v, x, j in zip(vals, srcs, idxs):
                    V.max_index(j[:, 0:8].bitcast(U32), v[:, 0:8], x)
                for v, x in zip(vals, srcs):
                    ins = V.match_replace(x, v[:, 0:8], x, -3.0e38)
                dv(ins)
                for v, x in zip(vals, srcs):
                    ins = V.max(v[:, 8:16], x)
                dv(ins)
                for v, x, j in zip(vals, srcs, idxs):
                    ins = V.max_index(j[:, 8:16].bitcast(U32), v[:, 8:16], x)
                dv(ins)

            def select(hh, i=0):
                dve.wait_ge(S["key_sb"], hh + 1)
                both = [(tt, 2 * hh + c) for tt in range(2) for c in range(2)]
                best16s(*([a[:, tt, g_, :] for tt, g_ in both] for a in (s_sb, topv, topi)))
                for tt in range(2):
                    ins = TT(cand[:, tt, hh, :].rearrange("p (a b) -> p a b", a=16),
                             topv[:, tt, 2 * hh, :].unsqueeze(2).to_broadcast([P, 16, 16]),
                             topv[:, tt, 2 * hh + 1, :].unsqueeze(1).to_broadcast([P, 16, 16]), ALU.add)
                dv(ins)
                best16s(*([a[:, tt, hh, :] for tt in range(2)] for a in (cand, best, posi)))
                pi = posi[:, :, hh, :].bitcast(U32)
                TS(place_i[:, 0], pi, 4, None, ALU.logical_shift_right)
                dv(TS(place_i[:, 1], pi, 15, None, ALU.bitwise_and))
                V.tensor_copy(topf[:, :, 2 * hh:2 * hh + 2, :], topi[:, :, 2 * hh:2 * hh + 2, :].bitcast(U32))
                dv(V.tensor_copy(place_f, place_i))
                if hh >= 2:
                    dve.wait_ge(S["placed"], hh - 1)
                TT(place_eq[hh % 2], iota[:, 0:16].unsqueeze(1).unsqueeze(1).to_broadcast([P, 4, 16, 16]),
                   place_f.rearrange("p c t n -> p (c t) n").unsqueeze(3).to_broadcast([P, 4, 16, 16]),
                   ALU.is_equal).then_inc(S["places"], 1)
                dve.wait_ge(S["places"], hh + 1)

            for hh in range(8):
                select(hh)
            for tt in range(2):
                gv = selv[:, tt, 2, :].rearrange("p (h k) -> p h k", h=8)
                TT(gv, best[:, tt], best[:, tt, :, 0:1].to_broadcast([P, 8, 16]), ALU.subtract).then_inc(S["g_arg"], 1)
                dve.wait_ge(S["g_exp"], tt + 1)
                dv(V.tensor_reduce(gsm[:, 0:8], gv, AX, ALU.add))
                dv(V.reciprocal(gsm[:, 0:8], gsm[:, 0:8]))
                TT(gv, gv, gsm[:, 0:8].unsqueeze(2).to_broadcast([P, 8, 16]), ALU.mult).then_inc(S["selt_ready"], 1)

            def onehots(i):
                for b in range(8):
                    if not (isinstance(i, int) and b < 4):
                        dve.wait_ge(S["g_mm"], 8 * i + (b - 3))
                    if b % 2 == 1:
                        TS(row_hot[b // 2][:, 3, :], iota, selT[:, 0, bass.ds(16 * i + (2 * b + 1), 1)], None, ALU.is_equal)
                    for e in range(2):
                        ins = TS(col_hot[b % 4][e], iota, selT[:, 1, bass.ds(16 * i + (2 * b + e), 1)],
                                 selT[:, 2, bass.ds(16 * i + (2 * b + e), 1)], ALU.is_equal, ALU.mult)
                    ins.then_inc(S["oh_ready"], 1)

            dve.wait_ge(S["selt_sb"], 2)
            onehots(0)
            with dve.Fori(1, L // 16) as i:
                onehots(i)
            dve.wait_ge(S["g_sb"], L // 4)

            def gate(e, i=0):
                T = TURN["peer"] + e
                b = e % 2
                dve.wait_ge(acc_free[T % 2], T // 2 + 1 + LOOP // 2 * i)
                a_t = gelu_t[:, b, :]
                TT(a_t, gelu_t[:, b, :], G[:, bass.ds(LOOP * i + e, 1), :].rearrange("p a n -> p (a n)"),
                   ALU.mult).then_inc(S["a_chain"], 1)
                dve.wait_ge(S["a_chain"], 2 * e + 1 + 2 * LOOP * i)
                V.tensor_copy(a_r[:, 0, b, :], a_t).then_inc(S["a_chain"], 1)
                dve.wait_ge(S["a_chain"], 2 * e + 2 + 2 * LOOP * i)
                TT(a_r[:, 1, b, :], a_t, a_r[:, 0, b, :].bitcast(F32), ALU.subtract).then_inc(S["a_ready"], 1)

            E0 = PAGE["peer"]
            split(E0 + 1)
            gate(0)
            gate(1)
            with dve.Fori(0, 126 // LOOP) as i:
                for u in range(LOOP):
                    split(E0 + 2 + u, i)
                    gate(2 + u, i)
            dve.wait_ge(S["fg_in"], 16)
            for tt in range(2):
                f = fin[:, tt * 1024:(tt + 1) * 1024]
                dve.wait_ge(S["fin_root"], tt + 1)
                dv(V.reciprocal(fstat[:, 2 + tt:3 + tt], fstat[:, 2 + tt:3 + tt]))
                STT(f.rearrange("p (a n) -> p a n", a=2), ps[:, 2 + 2 * tt:4 + 2 * tt, :], fstat[:, 2 + tt:3 + tt],
                    fgrow.rearrange("p (a n) -> p a n", a=2), ALU.mult, ALU.mult).then_inc(S["fin_out"], 1)


def lay_out(x):
    f = {k: np.asarray(v) for k, v in x.items()}

    def tiles(w, order=None):
        K, M = w.shape
        w = w.reshape(K // P, P, M // P, P).transpose(2, 0, 1, 3)
        return w if order is None else w[order]

    def pages(w, order=None):
        w = tiles(w, order).reshape(-1, 16, P, P)
        return w.transpose(0, 2, 1, 3).reshape(-1, P, 2048)

    def wide_pages(w):
        return w.reshape(KD, P, -1, L).transpose(2, 1, 0, 3).reshape(-1, P, 2048)

    wi, w2 = f["w_in"][0], f["w_in_2"][0]
    up_order = [m for e in range(22) for m in (e, 22 + e)]
    wm = f["w_mod"][0]
    mod_rows = wm[:, :2048].reshape(2, 4, P, 4, 512).transpose(3, 0, 2, 1, 4).reshape(8, P, 2048)
    mod2 = wm[:, 2048:].reshape(KD, P, MOD2, L).transpose(2, 1, 0, 3).reshape(MOD2, P, 2048)
    u = f["peer_u_2"][0].reshape(P, P, KD, P).transpose(1, 3, 2, 0).reshape(P, P, 1024)
    v = f["peer_v_2"][0].reshape(P, P, D).transpose(1, 0, 2)
    parts = [mod_rows, pages(wi[:, 0:512]), wide_pages(wi[:, 512:1024]), wide_pages(wi[:, 1024:2048]),
             pages(wi[:, 2048:3072]), pages(wi[:, 3072:3584]), pages(f["w_branch_gate"][0]), pages(f["w_ret_out"][0]),
             pages(f["w_four_out"][0]), pages(f["w_out"][0]), pages(f["w_up"][0], up_order), pages(f["w_down"][0]),
             pages(w2[:, 1536:1792]), pages(w2[:, 0:1536]), pages(w2[:, 1792:2816]), wide_pages(w2[:, 2816:3328]),
             pages(w2[:, 3328:3840]), pages(w2[:, 3848:5896]), pages(f["p_rw_2"][0]), pages(f["p_ml_2"][0]),
             pages(f["w_out_2"][0]), pages(f["peer_w_q_2"][0])]
    stream = np.empty((NPAGES, P, 2048), np.float32)
    n = 0
    for part in parts:
        stream[n:n + len(part)] = part
        n += len(part)
    left, right = stream[n:, :, :1024], stream[n:, :, 1024:]
    left[0], right[0] = u[0], u[1]
    left[1:], right[1:127], right[127] = v[:127], u[2:], v[127]

    def column(a):
        return a.reshape(-1, P).T

    def full(a, n):
        return np.broadcast_to(a.reshape(1, -1), (P, n))

    conv = np.stack([f["conv_w"][0][0], f["conv_w"][0][1], f["conv_w"][0][2], f["conv_b"][0]])
    conv = conv.reshape(4, 2, 22, P).transpose(3, 2, 1, 0).reshape(P, 176)
    cqk = np.stack([np.concatenate([f[f"ml_conv_{n}_w_2"][0], f[f"ml_conv_{n}_b_2"][0][None]]) for n in "qk"])
    cqk = cqk.reshape(2, 5, 4, P).transpose(3, 0, 2, 1).reshape(P, 40)
    df, db = f["ret_decay_f"][0], f["ret_decay_b"][0]
    if_b = np.zeros((P, 2), np.float32)
    if_b[0:4, 0], if_b[0:4, 1] = f["ml_b_i_2"][0], f["ml_b_f_2"][0]
    vals = {
        "b_mod": column(f["b_mod"]), "norm1_w": column(f["norm1_w"]), "b_bg": column(f["b_branch_gate"]),
        "norm2_w": column(f["norm2_w"]), "conv": conv, "final_norm_w": column(f["final_norm_w"]),
        "norm1_g_2": column(f["norm1_g_2"]), "mu": column(f["rw_mu_2"]), "w0": column(f["rw_w0_2"]),
        "a0": column(f["rw_a0_2"]), "k_k": column(f["rw_k_k_2"]), "k_a": column(f["rw_k_a_2"]),
        "r_k": column(f["rw_r_k_2"]), "gn_w": column(f["rw_gn_w_2"]), "gn_b": column(f["rw_gn_b_2"]), "cqk": cqk,
        "ml_norm": column(f["ml_norm_w_2"]), "gate_b": column(f["gate_b_2"]), "norm2_g": column(f["norm2_g_2"]),
        "dec_pair": np.concatenate([column(np.repeat(d, 64)) for d in (df, db)], axis=1),
        "dec_row": full(np.concatenate([df, db]), 16), "if_b": if_b,
        "eps6": np.full((P, 1), 1e-6), "eps_gn": np.full((P, 1), 64e-5), "eps_ml": np.full((P, 1), 1e-5)}
    cols = np.concatenate([vals[n].reshape(P, -1) for n, _ in COLS], axis=1).astype(np.float32)

    q, s = np.arange(P), np.arange(L)
    inv = (10000.0 ** (-np.arange(16, dtype=np.float32) / 16)).astype(np.float32)
    ang = np.concatenate([(s // 64)[:, None] * inv, (s % 64)[:, None] * inv], axis=1).astype(np.float32)
    cos, sin = np.cos(ang).T, np.sin(ang).T
    cos = np.tile(cos, (4, 1))
    sin = np.tile(np.concatenate([-sin, sin]), (2, 1))
    key = np.stack([q, q + P], axis=1)
    dist = s[None, None, :] - key[:, :, None]
    same = (q[:, None] // 64) == (q[None, :] // 64)
    strict = same & (q[:, None] < q[None, :])
    incl = same & (q[:, None] <= q[None, :])

    def block_mask(b):
        return (q[:, None] // (2 * b) == q[None, :] // (2 * b)) & (q[:, None] % (2 * b) < b) & (q[None, :] % (2 * b) >= b)

    dn = 2 * np.pi * np.outer(q, q) / P
    ln = 2 * np.pi * np.outer(s, s) / L
    scale = 1.0 / np.sqrt(P * L)
    dft_l = np.stack([np.cos(ln), -np.sin(ln)]).reshape(2, 2, P, L).transpose(2, 0, 1, 3)
    sel = np.zeros((P, 4, P))
    for n in range(4):
        sel[n, n] = 1
    pos_ctx = np.stack([np.stack([255 - k] * 8 + [k] * 8, axis=1) for k in key.T], axis=1)
    k1 = {"cosq": cos / 8, "sinq": sin / 8, "cosk": cos, "sink": sin, "dist_f": np.maximum(dist, 0),
          "dist_b": np.maximum(-dist, 0), "mask12": 1 + (dist == 0),
          "dft_d": np.concatenate([np.cos(dn), np.sin(dn)], axis=1) * scale, "dft_l": dft_l,
          "perm": (q[:, None] == (q[None, :] ^ 32)), "pos_ctx": pos_ctx,
          "pos_q": np.broadcast_to(np.concatenate([s + 1, 256 - s])[None], (P, 512))}
    k2 = {"mask4": np.concatenate([strict, incl, strict, incl], axis=1), "m1": block_mask(1).T, "m1t": block_mask(1),
          "levels": np.concatenate([block_mask(b) for b in (2, 4, 8, 16, 32)], axis=1),
          "scan": np.broadcast_to((s % 64 != 0)[None], (P, L)), "causal": dist >= 0, "sel": sel,
          "wa_up": np.concatenate([f["rw_w_up_2"][0], f["rw_a_up_2"][0]]), "g_up": f["rw_g_up_2"][0],
          "w_if": w2[:, 3840:3848].reshape(8, P, 8).transpose(1, 0, 2)}
    kp = {"ident": np.eye(P), "ones": np.ones((P, P)), "bones": same, "iota": np.broadcast_to(q[None], (P, P))}

    def pack(vals, table):
        return np.concatenate([np.asarray(vals[n], np.float32).reshape(P, -1) for n, _ in table], axis=1)

    both = np.stack([f["x"][0], f["ctx"][0]])
    return {
        "stream": stream, "mod2": mod2,
        "xT": both.reshape(2, L, KD, P).transpose(3, 0, 2, 1),
        "cT": np.stack([f["c"][0], f["c_ctx"]]).reshape(2, KD, P).transpose(2, 1, 0),
        "cols": cols, "pconst": pack(kp, PCONST), "const1": pack(k1, CONST1), "const2": pack(k2, CONST2),
        "subk": f["peer_sub_keys_2"][0].reshape(16, P, P).transpose(2, 0, 1).reshape(P, 2048),
        "fg": full(f["final_g_2"], D)}


def kernel(**inputs):
    import concourse.bacc as _bacc
    from concourse import mybir as _mybir
    from concourse.bass_utils import run_bass_kernel_spmd as _run

    nc = _bacc.Bacc("TRN2", target_bir_lowering=False, num_devices=1)
    arrays, t = {}, {}
    for name, a in lay_out(inputs).items():
        a = np.ascontiguousarray(a)
        arrays[f"in_{name}"] = a
        t[name] = nc.dram_tensor(f"in_{name}", a.shape, _mybir.dt.from_np(a.dtype), kind="ExternalInput").ap()
    out = nc.dram_tensor("out_0", (L, D), F32, kind="ExternalOutput").ap()
    build(nc, t, out)
    r = _run(nc, [arrays], core_ids=[0])
    return np.asarray(r.results[0]["out_0"]).reshape(1, L, D)
```
